# Optimizing a Trainium2 kernel written in Bass

```python
import jax, jax.numpy as jnp
from jax import lax
import numpy as np

D_MODEL = 1024
BATCH = 1
SEQ = 128
DEPTH = 1
DEC_BATCH = 1
DEC_SEQ = 1024
PAST_LEN = 256

GRID_W = 64
A_HEADS = 4
A_HEAD_DIM = 64
A_WIDTH = A_HEADS * A_HEAD_DIM
CHUNK = 128
POOL_WINDOWS = (2, 4, 8, 16)
POOL_GROUP = 64
B_WIDTH = len(POOL_WINDOWS) * POOL_GROUP
C_HEADS = 8
QK_NOPE = 64
QK_ROPE = 32
V_DIM = 64
Q_LORA = 384
KV_LORA = 256
C_WIDTH = C_HEADS * V_DIM
MIX_WIDTH = A_WIDTH + B_WIDTH + C_WIDTH
ROPE_AXIS = QK_ROPE // 2
ROPE_THETA = 10000.0
Q_BLOCK = 128
ATTN_SCALE = (QK_NOPE + QK_ROPE) ** -0.5
OFF_U = 0
OFF_V = OFF_U + A_WIDTH
OFF_P = OFF_V + A_WIDTH
OFF_CQ = OFF_P + B_WIDTH
OFF_CKV = OFF_CQ + Q_LORA
OFF_KR = OFF_CKV + KV_LORA
PROJ_COLS = OFF_KR + QK_ROPE
N_EXPERTS = 16
EXPERT_FF = 1024
EC_CAPACITY = 2
NORM_EPS = 1e-6

kernel_name = "hybrid_diffusion_ec_mla_step"

def rmsnorm(x, g):
    xf = x.astype(jnp.float32)
    y = xf * lax.rsqrt(jnp.mean(xf * xf, axis=-1, keepdims=True) + NORM_EPS)
    return y.astype(x.dtype) * g

def axial_rope_tables(n, dtype):
    rows = n // GRID_W
    row = jnp.repeat(jnp.arange(rows), GRID_W).astype(jnp.float32)
    col = jnp.broadcast_to(jnp.arange(GRID_W), (rows, GRID_W)).reshape(-1).astype(jnp.float32)
    inv = 1.0 / (ROPE_THETA ** (jnp.arange(0, ROPE_AXIS, 2, dtype=jnp.float32) / ROPE_AXIS))
    ang_r = row[:, None] * inv[None, :]
    ang_c = col[:, None] * inv[None, :]
    return (jnp.cos(ang_r).astype(dtype), jnp.sin(ang_r).astype(dtype),
            jnp.cos(ang_c).astype(dtype), jnp.sin(ang_c).astype(dtype))

def rotate(x, cos, sin):
    h = ROPE_AXIS // 2
    x1, x2 = x[..., :h], x[..., h:]
    return jnp.concatenate([x1 * cos - x2 * sin, x1 * sin + x2 * cos], axis=-1)

def axial_rope(x, tabs):
    cos_r, sin_r, cos_c, sin_c = tabs
    return jnp.concatenate([rotate(x[..., :ROPE_AXIS], cos_r, sin_r),
                            rotate(x[..., ROPE_AXIS:], cos_c, sin_c)], axis=-1)

def chunk_mlp(u, v, w_s, b_s):
    b, n, _ = u.shape
    nc = n // CHUNK
    vc = v.reshape(b, nc, CHUNK, A_HEADS, A_HEAD_DIM)
    s = jnp.einsum('hpq,bcqhd->bcphd', w_s, vc) + b_s.T[:, :, None]
    return u * s.reshape(b, n, A_WIDTH)

def multiscale_pool(p, w_pool, pool_scale):
    b, n, _ = p.shape
    pf = p.astype(jnp.float32)
    cs = jnp.concatenate([jnp.zeros((b, 1, B_WIDTH), jnp.float32), jnp.cumsum(pf, axis=1)], axis=1)
    t = jnp.arange(n)
    outs = []
    for g, w in enumerate(POOL_WINDOWS):
        sl = slice(g * POOL_GROUP, (g + 1) * POOL_GROUP)
        left = w // 2
        right = w - 1 - left
        lo = jnp.clip(t - left, 0, n)
        hi = jnp.clip(t + right + 1, 0, n)
        seg = cs[..., sl]
        mean = (seg[:, hi] - seg[:, lo]) / (hi - lo).astype(jnp.float32)[None, :, None]
        diff = (mean - pf[..., sl]).astype(p.dtype)
        outs.append(jnp.einsum('bnc,cd->bnd', diff, w_pool[g]))
    return jnp.concatenate(outs, axis=-1) * pool_scale

def attention(q, k, v):
    b, nq, h, dq = q.shape
    nb = nq // Q_BLOCK
    qb = q.reshape(b, nb, Q_BLOCK, h, dq).transpose(1, 0, 2, 3, 4)

    def block(qi):
        s = jnp.einsum('bqhd,bkhd->bhqk', qi, k).astype(jnp.float32) * ATTN_SCALE
        pr = jax.nn.softmax(s, axis=-1).astype(v.dtype)
        return jnp.einsum('bhqk,bkhd->bqhd', pr, v)

    o = lax.map(block, qb)
    return o.transpose(1, 0, 2, 3, 4).reshape(b, nq, h * v.shape[-1])

def mla_keys_values(ckv, krope, w_kvb_l):
    b, m, _ = ckv.shape
    kv = jnp.einsum('bmr,rf->bmf', ckv, w_kvb_l).reshape(b, m, C_HEADS, QK_NOPE + V_DIM)
    k_nope, v = kv[..., :QK_NOPE], kv[..., QK_NOPE:]
    k = jnp.concatenate([k_nope, jnp.broadcast_to(krope[:, :, None, :], (b, m, C_HEADS, QK_ROPE))], axis=-1)
    return k, v

def ec_ffn(h, w_router, w1, w3, w2):
    b, n, d = h.shape
    cap = EC_CAPACITY * n // N_EXPERTS
    logits = jnp.einsum('bnd,de->bne', h, w_router).astype(jnp.float32)
    aff = jax.nn.softmax(logits, axis=-1).transpose(0, 2, 1)
    gate, idx = lax.top_k(aff, cap)
    xs = jax.vmap(lambda hb, ib: hb[ib])(h, idx)
    hid = jax.nn.silu(jnp.einsum('becd,edf->becf', xs, w1)) * jnp.einsum('becd,edf->becf', xs, w3)
    y = jnp.einsum('becf,efd->becd', hid, w2) * gate[..., None].astype(h.dtype)
    return jax.vmap(lambda ib, yb: jnp.zeros((n, d), yb.dtype).at[ib.reshape(-1)].add(yb.reshape(-1, d)))(idx, y)

def mixing(h, P, l, ctx):
    b, n, _ = h.shape
    proj = jnp.einsum('bnd,df->bnf', h, P['w_in'][l])
    u = jax.nn.gelu(proj[..., OFF_U:OFF_V])
    va = jax.nn.gelu(proj[..., OFF_V:OFF_P])
    pin = proj[..., OFF_P:OFF_CQ]
    c_q = proj[..., OFF_CQ:OFF_CKV]
    c_kv = proj[..., OFF_CKV:OFF_KR]
    k_rope = proj[..., OFF_KR:PROJ_COLS]
    out_a = chunk_mlp(u, va, P['w_s'][l], P['b_s'][l])
    out_b = multiscale_pool(pin, P['w_pool'][l], P['pool_scale'][l])
    q = jnp.einsum('bnr,rf->bnf', rmsnorm(c_q, P['q_norm_g'][l]), P['w_qb'][l])
    q = q.reshape(b, n, C_HEADS, QK_NOPE + QK_ROPE)
    ckv = rmsnorm(c_kv, P['kv_norm_g'][l])
    if ctx is None:
        all_ckv, all_krope = ckv, k_rope
    else:
        ctx_ckv, ctx_krope = ctx
        tabs = axial_rope_tables(n, h.dtype)
        q_tabs = tuple(t[:, None, :] for t in tabs)
        q = jnp.concatenate([q[..., :QK_NOPE], axial_rope(q[..., QK_NOPE:], q_tabs)], axis=-1)
        all_ckv = jnp.concatenate([ctx_ckv, ckv], axis=1)
        all_krope = jnp.concatenate([ctx_krope, axial_rope(k_rope, tabs)], axis=1)
    k, v = mla_keys_values(all_ckv, all_krope, P['w_kvb'][l])
    out_c = attention(q, k, v)
    mixed = jnp.concatenate([out_a, out_b, out_c], axis=-1)
    return jnp.einsum('bnm,md->bnd', mixed, P['w_out'][l]), ckv, k_rope

def trunk_layer(x, cond, P, l, ctx=None):
    mod = jnp.einsum('bd,df->bf', jax.nn.silu(cond), P['w_ada'][l]) + P['b_ada'][l]
    sh1, sc1, g1, sh2, sc2, g2 = jnp.split(mod[:, None, :], 6, axis=-1)
    h = rmsnorm(x, P['norm1_g'][l]) * (1 + sc1) + sh1
    mix, ckv, krope = mixing(h, P, l, ctx)
    x = x + g1 * mix
    h = rmsnorm(x, P['norm2_g'][l]) * (1 + sc2) + sh2
    x = x + g2 * ec_ffn(h, P['w_router'][l], P['w_e1'][l], P['w_e3'][l], P['w_e2'][l])
    return x, ckv, krope

def setup_inputs(seed: int = 0) -> dict:
    key = jax.random.key(seed)
    ks = jax.random.split(key, 26)
    f32 = jnp.float32

    def nrm(k, shape, scale):
        return jax.random.normal(k, shape, f32) * scale

    return {
        "x_prompt": nrm(ks[0], (BATCH, SEQ, D_MODEL), 1.0),
        "x_sample": nrm(ks[1], (DEC_BATCH, DEC_SEQ, D_MODEL), 1.0),
        "cache_ckv": nrm(ks[2], (DEC_BATCH, DEPTH, PAST_LEN, KV_LORA), 1.0),
        "cache_krope": nrm(ks[3], (DEC_BATCH, DEPTH, PAST_LEN, QK_ROPE), 1.0),
        "c": nrm(ks[4], (DEC_BATCH, D_MODEL), 1.0),
        "c_ctx": nrm(ks[5], (D_MODEL,), 1.0),
        "w_ada": nrm(ks[6], (DEPTH, D_MODEL, 6 * D_MODEL), 0.5 * D_MODEL ** -0.5),
        "b_ada": nrm(ks[7], (DEPTH, 6 * D_MODEL), 0.01),
        "norm1_g": 1.0 + nrm(ks[8], (DEPTH, D_MODEL), 0.05),
        "norm2_g": 1.0 + nrm(ks[9], (DEPTH, D_MODEL), 0.05),
        "w_in": nrm(ks[10], (DEPTH, D_MODEL, PROJ_COLS), D_MODEL ** -0.5),
        "w_s": nrm(ks[11], (DEPTH, A_HEADS, CHUNK, CHUNK), CHUNK ** -0.5),
        "b_s": 1.0 + nrm(ks[12], (DEPTH, A_HEADS, CHUNK), 0.1),
        "w_pool": nrm(ks[13], (DEPTH, len(POOL_WINDOWS), POOL_GROUP, POOL_GROUP), POOL_GROUP ** -0.5),
        "pool_scale": 1.0 + nrm(ks[14], (DEPTH, B_WIDTH), 0.1),
        "q_norm_g": 1.0 + nrm(ks[15], (DEPTH, Q_LORA), 0.05),
        "w_qb": nrm(ks[16], (DEPTH, Q_LORA, C_HEADS * (QK_NOPE + QK_ROPE)), Q_LORA ** -0.5),
        "kv_norm_g": 1.0 + nrm(ks[17], (DEPTH, KV_LORA), 0.05),
        "w_kvb": nrm(ks[18], (DEPTH, KV_LORA, C_HEADS * (QK_NOPE + V_DIM)), KV_LORA ** -0.5),
        "w_out": nrm(ks[19], (DEPTH, MIX_WIDTH, D_MODEL), MIX_WIDTH ** -0.5),
        "w_router": nrm(ks[20], (DEPTH, D_MODEL, N_EXPERTS), D_MODEL ** -0.5),
        "w_e1": nrm(ks[21], (DEPTH, N_EXPERTS, D_MODEL, EXPERT_FF), D_MODEL ** -0.5),
        "w_e3": nrm(ks[22], (DEPTH, N_EXPERTS, D_MODEL, EXPERT_FF), D_MODEL ** -0.5),
        "w_e2": nrm(ks[23], (DEPTH, N_EXPERTS, EXPERT_FF, D_MODEL), EXPERT_FF ** -0.5),
        "final_norm_g": 1.0 + nrm(ks[24], (D_MODEL,), 0.05),
    }

def reference(x_prompt, x_sample, cache_ckv, cache_krope, c, c_ctx, w_ada, b_ada, norm1_g, norm2_g,
              w_in, w_s, b_s, w_pool, pool_scale, q_norm_g, w_qb, kv_norm_g, w_kvb, w_out,
              w_router, w_e1, w_e3, w_e2, final_norm_g):
    P = {'w_ada': w_ada, 'b_ada': b_ada, 'norm1_g': norm1_g, 'norm2_g': norm2_g, 'w_in': w_in,
         'w_s': w_s, 'b_s': b_s, 'w_pool': w_pool, 'pool_scale': pool_scale, 'q_norm_g': q_norm_g,
         'w_qb': w_qb, 'kv_norm_g': kv_norm_g, 'w_kvb': w_kvb, 'w_out': w_out, 'w_router': w_router,
         'w_e1': w_e1, 'w_e3': w_e3, 'w_e2': w_e2}
    cond_ctx = c_ctx[None, :]
    xp = x_prompt
    ckvs = []
    kropes = []
    for l in range(DEPTH):
        xp, ckv_l, krope_l = trunk_layer(xp, cond_ctx, P, l)
        ckvs.append(ckv_l)
        kropes.append(krope_l)
    y_prompt = rmsnorm(xp, final_norm_g)
    new_ckv = jnp.stack(ckvs, axis=1)
    new_krope = jnp.stack(kropes, axis=1)
    xs = x_sample
    for l in range(DEPTH):
        xs, _, _ = trunk_layer(xs, c, P, l, ctx=(cache_ckv[:, l], cache_krope[:, l]))
    y_sample = rmsnorm(xs, final_norm_g)
    return (y_prompt, y_sample, new_ckv, new_krope)


_drawn_inputs = setup_inputs


def setup_inputs(seed=0):
    import zlib

    import numpy as np

    out = dict(_drawn_inputs(seed))
    spreads = {}
    factors = {'cache_ckv': 8.0,
     'cache_krope': 8.0,
     'b_ada': 4.416,
     'norm2_g': 5.258,
     'b_s': 4.629,
     'pool_scale': 4.017,
     'q_norm_g': 8.0}
    for name, (base, spread) in spreads.items():
        noise = np.random.default_rng([zlib.crc32(name.encode()), seed]).standard_normal(out[name].shape)
        drawn = base * np.exp(spread * noise) if base else spread * noise
        out[name] = __import__('jax').numpy.asarray(drawn.astype(out[name].dtype))
    for name, factor in factors.items():
        out[name] = (out[name] * factor).astype(out[name].dtype)
    return out
```

```python
from contextlib import ExitStack

import numpy as np

import concourse.bass as bass
from concourse import mybir

ALU = mybir.AluOpType
ACT = mybir.ActivationFunctionType
F32 = mybir.dt.float32
U32 = mybir.dt.uint32
AX_X = mybir.AxisListType.X

P = 128
D = 1024
KD = D // P
NS, NPR = 1024, 128
T = NS + NPR
NT = T // P
GROUPS = [(0, 512), (512, 512), (1024, 128)]
GTILES = [range(0, 4), range(4, 8), range(8, 9)]
PAST = 256
KEYS = NS + PAST
ALLK = KEYS + NPR
HEADS, NOPE, ROPE, VD = 8, 64, 32, 64
QK = NOPE + ROPE
QL, KVL = 384, 256
SCALE = float(QK) ** -0.5
OFF_V, OFF_P, OFF_CQ, OFF_CKV, OFF_KR, COLS = 256, 512, 768, 1152, 1408, 1440
NE, FF = 16, 1024
CAPS, CAPP = 2 * NS // NE, 2 * NPR // NE
CAP = CAPS + CAPP
EPS = 1e-6
PAD = 8
FLAT = NS + NPR + 4 * PAD
FLAT_AT = [PAD, PAD + 512, NS + 3 * PAD]
RING = 6
V_N1, V_N2, V_C, V_PS, V_QN, V_KN, V_ROWS = 0, 8, 16, 32, 34, 37, 39


def tables():
    eye_ones = np.concatenate([np.eye(P), np.ones((P, P))], 1).astype(np.float32)
    inv = np.zeros((P, 2, FLAT), np.float32)
    for g, w in enumerate((2, 4, 8, 16)):
        left, right = w // 2, w - 1 - w // 2
        for n, at in ((NS, FLAT_AT[0]), (NPR, FLAT_AT[2])):
            t = np.arange(n)
            count = np.clip(t + right + 1, 0, n) - np.clip(t - left, 0, n)
            inv[64 * (g % 2):64 * (g % 2) + 64, g // 2, at:at + n] = 1.0 / count.astype(np.float32)
    axis = ROPE // 2
    freq = (1.0 / (10000.0 ** (np.arange(0, axis, 2, dtype=np.float32) / axis))).astype(np.float32)
    tok = np.arange(NS)
    pos = [(tok // 64).astype(np.float32), (tok % 64).astype(np.float32)]
    cos = np.ones((ROPE, T), np.float32)
    sin = np.zeros((ROPE, T), np.float32)
    for r in range(ROPE):
        ang = pos[r // axis] * freq[r % 8]
        cos[r, :NS] = np.cos(ang)
        sin[r, :NS] = np.sin(ang) * (-1.0 if r % axis < 8 else 1.0)
    q_rope = np.concatenate([np.ones((NOPE, T), np.float32), cos, sin])
    k_rope = np.concatenate([sin, sin, cos, cos])
    return {
        "eye_ones": eye_ones,
        "inv_count": inv.reshape(P, 2 * FLAT),
        "q_rope": q_rope,
        "k_rope": k_rope,
    }


def plan_jobs():
    jobs = [("vecs", "D"), ("w_s", "D"), ("ada", 0, "D"), ("mod", 0, "D")]
    jobs += [("h", g, k, "DA"[k % 2]) for g in range(3) for k in range(KD)]
    jobs += [("va", t, "A") for t in range(NT)]
    jobs += [("u", 0, g, "A") for g in range(3)]
    jobs += [("ada", 1, "D"), ("mod", 1, "D")] + [("g1", c, hf, "D") for c in range(2) for hf in range(2)]
    jobs += [("u", 1, g, "A") for g in range(3)]
    jobs += [("ada", 2, "D"), ("mod", 2, "D")]
    jobs += [("pin", m, g, "D") for m in range(2) for g in range(3)]
    for g in range(3):
        jobs += [("ckv", m, g, "D") for m in range(2)] + [("sskv", g, "D")]
    for g in range(3):
        jobs += [("cq", m, g, "D") for m in range(3)] + [("ssq", g, "D")]
    jobs += [("kr", g, "D") for g in range(3)]
    jobs += [("gate", m, g, "D") for m in range(2) for g in range(3)]
    jobs += [("pool", m, g, "A") for m in range(2) for g in range(3)]
    jobs += [("cache_c", "D"), ("cache_r", "D"), ("new", "D")]
    return jobs


def build(nc, x_prompt, x_sample, cache_ckv, cache_krope, c, c_ctx, w_ada, b_ada, norm1_g, norm2_g,
          w_in, w_s, b_s, w_pool, pool_scale, q_norm_g, w_qb, kv_norm_g, w_kvb, w_out, w_router,
          w_e1, w_e3, w_e2, final_norm_g, eye_ones, inv_count, q_rope, k_rope,
          y_prompt, y_sample, new_ckv, new_krope):
    JOBS = plan_jobs()
    NUM = {j[:-1]: n for n, j in enumerate(JOBS)}
    OUT = [sum(j[-1] == JOBS[n][-1] for j in JOBS[:n + 1]) for n in range(len(JOBS))]

    ctx = ExitStack()
    with ctx:
        def sb(name, shape, dt=F32):
            return ctx.enter_context(nc.sbuf_tensor(name, shape, dt))

        def sem(name):
            return ctx.enter_context(nc.semaphore(name))

        ps = ctx.enter_context(nc.psum_tensor("ps", [P, 8, 512], F32))
        bank = [ps[:, b, :] for b in range(8)]

        wreg = sb("wreg", [P, 24576])
        hreg = sb("hreg", [P, 9216])
        mreg = sb("mreg", [P, 9216])
        creg = sb("creg", [P, 2 * ALLK])

        def view(region, at, *dims):
            n = int(np.prod(dims))
            v = region[:, at:at + n]
            if len(dims) == 2:
                return v.rearrange("p (a b) -> p a b", a=dims[0])
            if len(dims) == 3:
                return v.rearrange("p (a b c) -> p a b c", a=dims[0], b=dims[1])
            return v

        w_in_sb = view(wreg, 0, KD, COLS)
        ada_ring = [view(wreg, 11520 + s * 2048, 2048) for s in range(RING)]
        pin = view(wreg, 11520, 2, FLAT)
        win_sum = [view(wreg, 13888 + s * FLAT, FLAT) for s in range(4)]
        cqT = view(wreg, 18624, 3, T)
        q_mul = view(wreg, 22080, T)
        kr_mul = view(wreg, 23232, T)
        qT = view(wreg, 0, 2, T)
        kT = view(wreg, 2304, 2, ALLK)
        v_sb = view(wreg, 5120, 11, P)
        w_out_sb = view(wreg, 8192, KD, D)
        x_again = [view(wreg, 16384 + s * D, D) for s in range(2)]
        x2 = [view(wreg, 18432 + s * D, D) for s in range(2)]
        x2n = [view(wreg, 20480 + s * D, D) for s in range(2)]
        w1 = [view(wreg, s * 4096, KD, 512) for s in range(2)]
        w3 = [view(wreg, 8192 + s * 4096, KD, 512) for s in range(2)]
        w2 = [view(wreg, 16384 + s * 4096, 4, D) for s in range(2)]
        hT = view(hreg, 0, KD, T)
        prob = [view(hreg, s * KEYS, KEYS) for s in range(2)]
        probT = view(hreg, 2 * KEYS, 4, KEYS)
        cache_c = view(hreg, 2 * KEYS, 2, KVL)
        cache_r = view(hreg, 2 * KEYS + 512, 2, P)
        new_out = view(hreg, 2 * KEYS + 768, KVL + NOPE)
        wq_raw = view(hreg, 7680, 3, 2 * QK)
        wq = view(hreg, 8256, 3, 2, P)
        h2T = hT
        y_rows = [view(hreg, s * D, D) for s in range(2)]
        y_rows_p = [view(hreg, 2048 + s * D, D) for s in range(2)]
        final_row = view(hreg, 4096, D)
        x_fin = [view(hreg, 5120 + s * D, D) for s in range(4)]
        x_sb = view(mreg, 0, NT, D)
        mixT = view(mreg, 0, KD, T)
        inv_sb = view(mreg, 2304, 2, FLAT)
        va = view(mreg, 6912, NT, 256)
        x_rows = [view(mreg, s * D, D) for s in range(2)]
        x_rows_p = [view(mreg, 2048 + s * D, D) for s in range(2)]
        xsT = [view(mreg, 4096 + s * KD * CAP, KD, CAP) for s in range(2)]
        yT = view(mreg, 6400, KD, CAP)
        hidT = view(mreg, 7552, KD, CAP)
        silu_h = view(mreg, 8704, 2, CAP)
        fin_junk = view(mreg, 0, D)
        b_rows = view(creg, 0, 3, 512)
        ckvT = view(creg, 0, 2, ALLK)
        aff = view(creg, 0, T)
        logit = view(creg, T, NT, NE)
        prob_e = view(creg, T + 144, NT, NE)
        r_stat = view(creg, T + 288, 4, NT)
        top_val = view(creg, T + 324, CAP)
        top_idx_f = view(creg, T + 468, CAP)
        picked = view(creg, T + 612, 4, NE)
        const = sb("const", [P, 2 * P])
        ident, ones = const[:, 0:P], const[:, P:2 * P]
        vecs = sb("vecs", [P, P])
        vT = sb("vT", [P, V_ROWS])
        cond = sb("cond", [P, KD, 32])
        modT = sb("modT", [P, 2, 48])
        gain1 = sb("gain1", [P, 2, KD])
        gain2 = sb("gain2", [P, 2, KD])
        g1_rows = sb("g1_rows", [P, 2, D])
        bs_sb = sb("bs_sb", [P, 2, P])
        wsT = sb("wsT", [P, 4, P])
        share = sb("share", [P, 512])
        ws_raw = share[:].rearrange("p (h q) -> p h q", h=4)
        wkv = share[:].rearrange("p (k c f) -> p k c f", k=2, c=2)
        w_pool_sb = sb("w_pool_sb", [P, 2, P])
        w_r = sb("w_r", [P, KD, NE])
        sq = sb("sq", [P, 2, 512])
        rt = sb("rt", [P, 2, 512])
        mod_rows = rt[:, 0, :]
        w_rot = sb("w_rot", [P, KD, ROPE])
        stat = sb("stat", [P, 48])
        top_idx = sb("top_idx", [NE, CAP], U32)
        pick_s = sb("pick_s", [P, NE], U32)
        pick_p = sb("pick_p", [P, NE], U32)
        idx_g = [sb(f"idx_g{s}", [P, 1], U32) for s in range(2)]
        idx_gp = [sb(f"idx_gp{s}", [P, 1], U32) for s in range(2)]
        idx_s = sb("idx_s", [P, 1], U32)
        idx_sp = sb("idx_sp", [P, 1], U32)
        ss_x, rs_x, rx = stat[:, 0:9], stat[:, 9:18], stat[:, 18:27]
        a_max, a_neg, a_sum, a_rec = (stat[:, 28 + 4 * s:32 + 4 * s] for s in range(4))
        ss2, rs2 = stat[:, 44:46], stat[:, 46:48]

        x2_dram = nc.dram_tensor("x2_rows", [T, D], F32, kind="Internal").ap()
        xn_dram = nc.dram_tensor("xn_rows", [T, D], F32, kind="Internal").ap()

        def tok_rows(sample, prompt, t):
            return sample[0, t * P:(t + 1) * P, :] if t < NT - 1 else prompt[0]

        const_in, vecs_in, ws_in, bs_in = sem("const_in"), sem("vecs_in"), sem("ws_in"), sem("bs_in")
        brows_in, wpool_in, w_r_in = sem("brows_in"), sem("wpool_in"), sem("w_r_in")
        x_in = [sem(f"x_in{t}") for t in range(NT)]
        ada_in = [sem(f"ada_in{s}") for s in range(RING)]
        w_in_in, inv_in, rope_in = sem("w_in_in"), sem("inv_in"), sem("rope_in")
        cleared, pool_cleared = sem("cleared"), sem("pool_cleared")
        ada_mm, job_mm = sem("ada_mm"), sem("job_mm")
        out_d, out_a = sem("out_d"), sem("out_a")
        cond_ok, gain_ok = sem("cond_ok"), sem("gain_ok")
        ssx_ok, var_ok, sqrt_ok, rx_ok, xn_ok = (sem(s) for s in ("ssx_ok", "var_ok", "sqrt_ok", "rx_ok", "xn_ok"))
        wrot_ok, sq_ok, nvar_ok, nsqrt_ok = (sem(s) for s in (
            "wrot_ok", "sq_ok", "nvar_ok", "nsqrt_ok"))
        dve_step, raw_used = sem("dve_step"), sem("raw_used")
        pool_step, diff_ok = sem("pool_step"), sem("diff_ok")
        cache_in, new_st = sem("cache_in"), sem("new_st")
        crope_zero = sem("crope_zero")
        w_out_in = sem("w_out_in")
        wq_in, wkv_in, wq_ok = sem("wq_in"), sem("wkv_in"), sem("wq_ok")
        proj_mm, q_out, k_out, v_out = sem("proj_mm"), sem("q_out"), sem("k_out"), sem("v_out")
        s_mm, max_ok, neg_ok, exp_ok, rec_ok, norm_ok = (sem(s) for s in (
            "s_mm", "max_ok", "neg_ok", "exp_ok", "rec_ok", "norm_ok"))
        t_mm, t_out_a, t_out_d, pv_mm, pv_out = (sem(s) for s in ("t_mm", "t_out_a", "t_out_d", "pv_mm", "pv_out"))
        xa_in = [sem(f"xa_in{s}") for s in range(2)]
        x2_st = [sem(f"x2_st{s}") for s in range(2)]
        xn_st = [sem(f"xn_st{s}") for s in range(2)]
        o_mm, o_out, x2_ok, ss2_ok, var2_ok, sqrt2_ok, rec2_ok, x2n_ok = (sem(s) for s in (
            "o_mm", "o_out", "x2_ok", "ss2_ok", "var2_ok", "sqrt2_ok", "rec2_ok", "x2n_ok"))
        h2_mm, h2_out_a, h2_out_d, lg_mm, lg_out = (sem(s) for s in (
            "h2_mm", "h2_out_a", "h2_out_d", "lg_mm", "lg_out"))
        r_mm, r_step, r_exp = sem("r_mm"), sem("r_step"), sem("r_exp")
        w1_in = [sem(f"w1_in{s}") for s in range(2)]
        w3_in = [sem(f"w3_in{s}") for s in range(2)]
        w2_in = [sem(f"w2_in{s}") for s in range(2)]
        idx_ok, sidx_ok = sem("idx_ok"), sem("sidx_ok")
        rows_in = [sem(f"rows_in{s}") for s in range(2)]
        rows_p_in = [sem(f"rows_p_in{s}") for s in range(2)]
        h_mm, silu_ok, hid_ok, y_mm, y_out, tr_mm, tr_out = (sem(s) for s in (
            "h_mm", "silu_ok", "hid_ok", "y_mm", "y_out", "tr_mm", "tr_out"))
        added, added_p = sem("added"), sem("added_p")
        fin_in = [sem(f"fin_in{s}") for s in range(4)]
        fin_st = [sem(f"fin_st{s}") for s in range(4)]
        frow_in = sem("frow_in")
        fss_ok, fvar_ok, fsqrt_ok, frec_ok, fin_ok = (sem(s) for s in (
            "fss_ok", "fvar_ok", "fsqrt_ok", "frec_ok", "fin_ok"))

        def evicted(eng, n):
            eng.wait_ge(out_d if JOBS[n][-1] == "D" else out_a, OUT[n])

        def computed(eng, n):
            if JOBS[n][0] == "ada":
                eng.wait_ge(ada_mm, (JOBS[n][1] + 1) * KD)
            else:
                eng.wait_ge(job_mm, sum(j[0] != "ada" for j in JOBS[:n + 1]))

        block = ctx.enter_context(nc.Block())

        @block.sync
        def _(sp):
            sp.dma_start(const[:], eye_ones).then_inc(const_in, 16)
            for row, src, n in ((V_N1, norm1_g[0], 8), (V_N2, norm2_g[0], 8), (V_C, c[0], 8), (V_C + 8, c_ctx, 8),
                                (V_PS, pool_scale[0], 2), (V_QN, q_norm_g[0], 3), (V_KN, kv_norm_g[0], 2)):
                sp.dma_start(vecs[row:row + n, :], src.rearrange("(n p) -> n p", p=P)).then_inc(vecs_in, 16)
            sp.dma_start(ws_raw, w_s[0].rearrange("h p q -> p h q")).then_inc(ws_in, 16)
            sp.wait_ge(cleared, 1)
            for r in range(3):
                for g in range(4):
                    at = r * 2048 + g * 512
                    sp.dma_start(b_rows[32 * g:32 * g + 2, r, :],
                                 b_ada[0:1, at:at + 512].to_broadcast([2, 512])).then_inc(brows_in, 16)
            for t in range(3):
                sp.dma_start(x_sb[:, t, :], tok_rows(x_sample, x_prompt, t)).then_inc(x_in[t], 16)

            def ada_chunk(n):
                r, k = divmod(n, KD)
                if n >= RING:
                    sp.wait_ge(ada_mm, n - RING + 1)
                sp.dma_start(ada_ring[n % RING],
                             w_ada[0, k * P:(k + 1) * P, r * 2048:(r + 1) * 2048]).then_inc(ada_in[n % RING], 16)
            for n in range(6):
                ada_chunk(n)
            for t in range(3, NT):
                sp.dma_start(x_sb[:, t, :], tok_rows(x_sample, x_prompt, t)).then_inc(x_in[t], 16)
            for n in range(6, 8):
                ada_chunk(n)
            sp.dma_start(w_in_sb, w_in[0].rearrange("(k p) f -> p k f", p=P)).then_inc(w_in_in, 16)
            for h in range(4):
                j = h % 2
                sp.dma_start(bs_sb[64 * j:64 * j + 64, h // 2, :],
                             b_s[0, h:h + 1, :].to_broadcast([64, P])).then_inc(bs_in, 16)
                sp.dma_start(w_pool_sb[64 * j:64 * j + 64, h // 2, 64 * j:64 * j + 64],
                             w_pool[0, h]).then_inc(wpool_in, 16)
            sp.dma_start(w_r[:], w_router[0].rearrange("(k p) e -> p k e", p=P)).then_inc(w_r_in, 16)
            for n in range(8, 24):
                ada_chunk(n)
            evicted(sp, NUM[("h", 2, KD - 1)])
            evicted(sp, NUM[("h", 2, KD - 2)])
            sp.dma_start(inv_sb, inv_count.rearrange("p (m f) -> p m f", m=2)).then_inc(inv_in, 16)
            sp.wait_ge(ada_mm, 24)
            sp.dma_start(q_mul, q_rope).then_inc(rope_in, 16)
            sp.dma_start(kr_mul, k_rope).then_inc(rope_in, 16)
            computed(sp, NUM[("kr", 2)])
            for s in range(2):
                sp.dma_start(cache_c[:, s, :], cache_ckv[0, 0, s * P:(s + 1) * P, :]).then_inc(cache_in, 16)
            sp.wait_ge(crope_zero, 1)
            for s in range(2):
                for at in (64, 96):
                    sp.dma_start(cache_r[:, s, at:at + ROPE],
                                 cache_krope[0, 0, s * P:(s + 1) * P, :]).then_inc(cache_in, 16)

            def head_weights(i):
                sp.dma_start(wq_raw, w_qb[0, :, i * 2 * QK:(i + 1) * 2 * QK].rearrange(
                    "(k p) f -> p k f", p=P)).then_inc(wq_in, 16)
                for k in range(2):
                    for part in range(2):
                        src = w_kvb[0, k * P:(k + 1) * P, i * 2 * P:(i + 1) * 2 * P]
                        src = src.rearrange("p (j c e) -> p j c e", j=2, c=2)[:, :, part, :]
                        sp.dma_start(wkv[:, k, part, :].rearrange("p (j e) -> p j e", j=2), src).then_inc(wkv_in, 16)
            head_weights(0)
            computed(sp, NUM[("pool", 1, 2)])
            sp.dma_start(w_out_sb, w_out[0].rearrange("(k p) f -> p k f", p=P)).then_inc(w_out_in, 16)
            evicted(sp, NUM[("new",)])
            sp.dma_start(new_ckv[0, 0], new_out[:, 0:KVL]).then_inc(new_st, 16)
            sp.dma_start(new_krope[0, 0], new_out[:, KVL:KVL + ROPE]).then_inc(new_st, 16)
            for i in range(1, 4):
                sp.wait_ge(wq_ok, i)
                sp.wait_ge(proj_mm, i * 12)
                head_weights(i)
            sp.wait_ge(pv_mm, 4 * NT)
            for s in range(2):
                sp.dma_start(w1[s], w_e1[0, 0, :, s * 512:(s + 1) * 512].rearrange(
                    "(k p) f -> p k f", p=P)).then_inc(w1_in[s], 16)
            for t in range(2):
                sp.dma_start(x_again[t], tok_rows(x_sample, x_prompt, t)).then_inc(xa_in[t], 16)
            for t in range(NT):
                s = t % 2
                sp.wait_ge(x2_ok, t + 1)
                sp.dma_start(x2_dram[t * P:(t + 1) * P, :], x2[s]).then_inc(x2_st[s], 16)
                if t + 2 < NT:
                    sp.dma_start(x_again[s], tok_rows(x_sample, x_prompt, t + 2)).then_inc(xa_in[s], 16)
                sp.wait_ge(x2n_ok, t + 1)
                sp.dma_start(xn_dram[t * P:(t + 1) * P, :], x2n[s]).then_inc(xn_st[s], 16)
            sp.wait_ge(o_mm, 2 * NT)
            for s in range(2):
                sp.dma_start(w3[s], w_e3[0, 0, :, s * 512:(s + 1) * 512].rearrange(
                    "(k p) f -> p k f", p=P)).then_inc(w3_in[s], 16)
            for s in range(2):
                sp.wait_ge(x2_st[s], 16 * (5 - s))
                sp.wait_ge(xn_st[s], 16 * (5 - s))
            sp.wait_ge(h2_mm, 2 * NT)
            for s in range(2):
                sp.dma_start(w2[s], w_e2[0, 0, s * 512:(s + 1) * 512, :].rearrange(
                    "(k p) f -> p k f", p=P)).then_inc(w2_in[s], 16)
            sp.wait_ge(lg_mm, 3)
            sp.dma_start(final_row, final_norm_g.rearrange("(a d) -> a d", a=1).to_broadcast([P, D])).then_inc(frow_in, 16)
            with sp.Fori(0, NE - 1) as e:
                for s in range(2):
                    sp.wait_ge(h_mm, e * 16 + 8 * s + 8)
                    sp.dma_start(w1[s], w_e1[0, bass.ds(e + 1, 1), :, s * 512:(s + 1) * 512].rearrange(
                        "e (k p) f -> p (e k) f", p=P)).then_inc(w1_in[s], 16)
                    sp.dma_start(w3[s], w_e3[0, bass.ds(e + 1, 1), :, s * 512:(s + 1) * 512].rearrange(
                        "e (k p) f -> p (e k) f", p=P)).then_inc(w3_in[s], 16)
                sp.wait_ge(y_mm, e * 8 + 8)
                for s in range(2):
                    sp.dma_start(w2[s], w_e2[0, bass.ds(e + 1, 1), s * 512:(s + 1) * 512, :].rearrange(
                        "e (k p) f -> p (e k) f", p=P)).then_inc(w2_in[s], 16)
            sp.wait_ge(added, 16 * NE)
            sp.wait_ge(added_p, 16 * NE)
            for t in range(4):
                sp.dma_start(x_fin[t], x2_dram[t * P:(t + 1) * P, :]).then_inc(fin_in[t], 16)
            for t in range(NT):
                s = t % 4
                sp.wait_ge(fin_ok, t + 1)
                sp.dma_start(tok_rows(y_sample, y_prompt, t), x_fin[s]).then_inc(fin_st[s], 16)
                if t + 4 < NT:
                    sp.wait_ge(fin_st[s], 16 * (t // 4 + 1))
                    sp.dma_start(x_fin[s], x2_dram[(t + 4) * P:(t + 5) * P, :]).then_inc(fin_in[s], 16)
            for s in range(4):
                sp.wait_ge(fin_st[s], 16 * (3 if s == 0 else 2))
            sp.wait_ge(new_st, 32)

        @block.tensor
        def _(pe):
            def project(n, w_at, m, g):
                g0, gn = GROUPS[g]
                for k in range(KD):
                    mm = pe.matmul(bank[n % 8][:, 0:gn], w_in_sb[:, k, w_at + m * P:w_at + (m + 1) * P],
                                   hT[:, k, g0:g0 + gn], start=(k == 0), stop=(k == KD - 1))
                return mm

            for n, job in enumerate(JOBS):
                kind = job[0]
                o = bank[n % 8]
                if n >= 8:
                    evicted(pe, n - 8)
                if kind == "vecs":
                    pe.wait_ge(const_in, 16)
                    pe.wait_ge(vecs_in, 16 * 7)
                    mm = pe.transpose(o[:, 0:V_ROWS], vecs[0:V_ROWS, :], ident[0:V_ROWS, 0:V_ROWS])
                elif kind == "w_s":
                    pe.wait_ge(ws_in, 16)
                    for h in range(4):
                        mm = pe.transpose(o[:, h * P:(h + 1) * P], ws_raw[:, h, :], ident)
                elif kind == "ada":
                    r = job[1]
                    pe.wait_ge(cond_ok, 1)
                    for k in range(KD):
                        ch = r * KD + k
                        pe.wait_ge(ada_in[ch % RING], 16 * (ch // RING + 1))
                        for g in range(4):
                            mm = pe.matmul(o[32 * g:32 * g + 32, :], cond[:, k, :],
                                           ada_ring[ch % RING][:, g * 512:(g + 1) * 512],
                                           start=(k == 0), stop=(k == KD - 1))
                        mm.then_inc(ada_mm, 1)
                elif kind == "mod":
                    evicted(pe, NUM[("ada", job[1])])
                    for j in range(4):
                        mm = pe.transpose(o[:, j * P:(j + 1) * P], mod_rows[:, j * P:(j + 1) * P], ident)
                elif kind == "g1":
                    cnd, hf = job[1], job[2]
                    row = 32 * hf + cnd
                    mm = pe.matmul(o, ident[:, row:row + 1].to_broadcast([P, P]), mod_rows,
                                   start=True, stop=True)
                elif kind == "h":
                    g, k = job[1], job[2]
                    if k == 0:
                        pe.wait_ge(xn_ok, GTILES[g][-1] + 1)
                    for a, t in enumerate(GTILES[g]):
                        mm = pe.transpose(o[:, a * P:(a + 1) * P], x_sb[:, t, k * P:(k + 1) * P], ident)
                elif kind == "va":
                    t = job[1]
                    if t == 0:
                        pe.wait_ge(w_in_in, 16)
                        evicted(pe, NUM[("h", 2, KD - 1)])
                        evicted(pe, NUM[("h", 2, KD - 2)])
                    for k in range(KD):
                        mm = pe.matmul(o[:, 0:256], hT[:, k, t * P:(t + 1) * P], w_in_sb[:, k, OFF_V:OFF_P],
                                       start=(k == 0), stop=(k == KD - 1))
                elif kind == "u":
                    mm = project(n, 0, job[1], job[2])
                elif kind == "pin":
                    mm = project(n, OFF_P, job[1], job[2])
                elif kind == "ckv":
                    mm = project(n, OFF_CKV, job[1], job[2])
                elif kind == "cq":
                    mm = project(n, OFF_CQ, job[1], job[2])
                elif kind in ("sskv", "ssq"):
                    g = job[1]
                    gn = GROUPS[g][1]
                    parts = 2 if kind == "sskv" else 3
                    base = (2 * g if kind == "sskv" else 6 + 3 * g)
                    for m in range(parts):
                        pe.wait_ge(sq_ok, base + m + 1)
                        mm = pe.matmul(o[:, 0:gn], ones, sq[:, (base + m) % 2, 0:gn],
                                       start=(m == 0), stop=(m == parts - 1))
                        if m < parts - 1:
                            mm.then_inc(raw_used, 1)
                elif kind == "kr":
                    g0, gn = GROUPS[job[1]]
                    pe.wait_ge(wrot_ok, 1)
                    for k in range(KD):
                        for q in range(4):
                            w_k = w_rot[:, k, :] if q < 2 else w_in_sb[:, k, OFF_KR:COLS]
                            mm = pe.matmul(o[32 * q:32 * q + 32, 0:gn], w_k, hT[:, k, g0:g0 + gn],
                                           start=(k == 0), stop=(k == KD - 1))
                elif kind == "gate":
                    m, g = job[1], job[2]
                    if (m, g) == (0, 0):
                        evicted(pe, NUM[("w_s",)])
                        evicted(pe, NUM[("va", NT - 1)])
                    for a, t in enumerate(GTILES[g]):
                        for j in range(2):
                            h = 2 * m + j
                            mm = pe.matmul(o[64 * j:64 * j + 64, a * P:(a + 1) * P], va[:, t, h * 64:(h + 1) * 64],
                                           wsT[:, h, :], start=True, stop=True)
                elif kind == "pool":
                    m, g = job[1], job[2]
                    pe.wait_ge(wpool_in, 16 * 4)
                    pe.wait_ge(diff_ok, 2)
                    gn, at = GROUPS[g][1], FLAT_AT[g]
                    mm = pe.matmul(o[:, 0:gn], w_pool_sb[:, m, :], win_sum[2 * m][:, at:at + gn],
                                   start=True, stop=True)
                elif kind == "cache_c":
                    pe.wait_ge(cache_in, 16 * 6)
                    for k in range(2):
                        for s in range(2):
                            mm = pe.transpose(o[:, (2 * k + s) * P:(2 * k + s + 1) * P],
                                              cache_c[:, s, k * P:(k + 1) * P], ident)
                elif kind == "cache_r":
                    for s in range(2):
                        mm = pe.transpose(o[:, s * P:(s + 1) * P], cache_r[:, s, :], ident)
                elif kind == "new":
                    evicted(pe, NUM[("sskv", 2)])
                    for k in range(2):
                        pe.transpose(o[:, k * P:(k + 1) * P], ckvT[:, k, KEYS:ALLK], ident)
                    evicted(pe, NUM[("kr", 2)])
                    mm = pe.transpose(o[:, KVL:KVL + NOPE], kT[64:128, 0, KEYS:ALLK], ident[64:128, 64:128])
                if kind != "ada":
                    mm.then_inc(job_mm, 1)

            last = len(JOBS) - 1
            for n in range(last - 7, last + 1):
                evicted(pe, n)
            with pe.Fori(0, 4) as i:
                pe.wait_ge(wq_ok, i + 1)
                for j in range(2):
                    for g, (g0, gn) in enumerate(GROUPS):
                        for k in range(3):
                            mm = pe.matmul(bank[3 * j + g][:, 0:gn], wq[:, k, j, :], cqT[:, k, g0:g0 + gn],
                                           start=(k == 0), stop=(k == 2))
                        mm.then_inc(proj_mm, 1)
                pe.wait_ge(wkv_in, i * 64 + 64)
                for g, (k0, kn) in enumerate(((0, 512), (512, 512), (1024, 384))):
                    pe.wait_ge(q_out, i * 6 + g + 1)
                    for k in range(2):
                        mm = pe.matmul(bank[g][:, 0:kn], wkv[:, k, 0, :], ckvT[:, k, k0:k0 + kn],
                                       start=(k == 0), stop=(k == 1))
                    mm.then_inc(proj_mm, 1)
                for g, tiles in enumerate((range(0, 4), range(4, 8), range(8, 11))):
                    pe.wait_ge(q_out, i * 6 + 3 + g + 1)
                    for a, kt in enumerate(tiles):
                        for k in range(2):
                            mm = pe.matmul(bank[3 + g][:, a * P:(a + 1) * P], ckvT[:, k, kt * P:(kt + 1) * P], wkv[:, k, 1, :],
                                           start=(k == 0), stop=(k == 1))
                    mm.then_inc(proj_mm, 1)

                def score(n, ch):
                    t, j = divmod(n, 2)
                    slot = 3 * (n % 2)
                    q = qT[:, j, t * P:(t + 1) * P]
                    if ch == 0:
                        if n == 0:
                            pe.wait_ge(k_out, i * 3 + 3)
                            pe.wait_ge(q_out, i * 6 + 6)
                        if n == 1:
                            pe.wait_ge(v_out, i * 3 + 3)
                        if n >= 2:
                            pe.wait_ge(exp_ok, i * 18 + n - 1)
                    if t < NT - 1:
                        k0, kn = ((0, 512), (512, 512), (1024, 256))[ch]
                    else:
                        k0, kn = KEYS, NPR
                    mm = pe.matmul(bank[slot + ch][:, 0:kn], q, kT[:, j, k0:k0 + kn], start=True, stop=True)
                    if ch == 2 or t == NT - 1:
                        mm.then_inc(s_mm, 1)

                def turn(n, ch):
                    t = n // 2
                    if ch == 0:
                        pe.wait_ge(norm_ok, i * 18 + n + 1)
                        if n == 17:
                            pe.wait_ge(t_out_a, i * 34 + 33)
                        elif n > 0:
                            pe.wait_ge(t_out_d, i * 16 + n)
                    else:
                        pe.wait_ge(t_out_a, i * 34 + 2 * n + ch)
                    tiles = (4, 4, 2)[ch] if t < NT - 1 else 1
                    for a in range(tiles):
                        kt = 4 * ch + a
                        mm = pe.transpose(bank[6][:, a * P:(a + 1) * P], prob[n % 2][:, kt * P:(kt + 1) * P], ident)
                    mm.then_inc(t_mm, 1)

                def weigh(t):
                    if t < NT - 1:
                        pe.wait_ge(t_out_a, i * 34 + 4 * t + 4)
                        pe.wait_ge(t_out_d, i * 16 + 2 * t + 2)
                        tiles = range(10)
                    else:
                        pe.wait_ge(t_out_a, i * 34 + 34)
                        tiles = range(10, 11)
                    if t > 0:
                        pe.wait_ge(pv_out, i * NT + t)
                    for kt in tiles:
                        for j in range(2):
                            src = kt if t < NT - 1 else 0
                            mm = pe.matmul(bank[7][64 * j:64 * j + 64, 0:P], v_sb[:, kt, 64 * j:64 * j + 64],
                                           probT[:, 2 * (t % 2) + j, src * P:(src + 1) * P],
                                           start=(kt == tiles[0]), stop=(kt == tiles[-1]))
                    mm.then_inc(pv_mm, 1)

                units = 2 * NT
                for n in range(units + 3):
                    chunks = 3 if n < 16 else 1
                    turned = 0 <= n - 2 < units
                    if n < units:
                        score(n, 0)
                    if turned:
                        turn(n - 2, 0)
                    if n % 2 == 0 and n >= 4:
                        weigh((n - 4) // 2)
                    for ch in (1, 2):
                        if n < units and ch < chunks:
                            score(n, ch)
                        if turned and n - 2 < 16:
                            turn(n - 2, ch)

            pe.wait_ge(w_out_in, 16)
            pe.wait_ge(exp_ok, 72)
            pe.wait_ge(pv_out, 4 * NT)
            evicted(pe, NUM[("pool", 1, 2)])

            def h2_turn(t):
                pe.wait_ge(x2n_ok, t + 1)
                for hf in range(2):
                    if t >= 1:
                        pe.wait_ge(h2_out_d if hf else h2_out_a, t)
                    for a in range(4):
                        kk = 4 * hf + a
                        mm = pe.transpose(bank[4 + hf][:, a * P:(a + 1) * P], x2n[t % 2][:, kk * P:(kk + 1) * P], ident)
                    mm.then_inc(h2_mm, 1)

            def logits(g):
                g0, gn = GROUPS[g]
                pe.wait_ge(h2_out_a, GTILES[g][-1] + 1)
                pe.wait_ge(h2_out_d, GTILES[g][-1] + 1)
                if g:
                    pe.wait_ge(lg_out, g)
                else:
                    pe.wait_ge(w_r_in, 16)
                    pe.wait_ge(t_out_a, 4 * 34)
                for k in range(KD):
                    mm = pe.matmul(bank[6][0:NE, 0:gn], w_r[:, k, :], h2T[:, k, g0:g0 + gn],
                                   start=(k == 0), stop=(k == KD - 1))
                mm.then_inc(lg_mm, 1)

            for t in range(NT):
                for hf in range(2):
                    x = 2 * t + hf
                    if x >= 4:
                        pe.wait_ge(o_out, x - 3)
                    for k in range(KD):
                        mm = pe.matmul(bank[x % 4], mixT[:, k, t * P:(t + 1) * P],
                                       w_out_sb[:, k, hf * 512:(hf + 1) * 512], start=(k == 0), stop=(k == KD - 1))
                    mm.then_inc(o_mm, 1)
                if t >= 1:
                    h2_turn(t - 1)
                if t in (5,):
                    logits(0)
            h2_turn(NT - 1)
            logits(1)
            logits(2)

            pe.wait_ge(lg_out, 3)
            for t in range(NT):
                mm = pe.transpose(bank[7][:, t * NE:(t + 1) * NE], aff[0:NE, t * P:(t + 1) * P], ident[0:NE, 0:NE])
            mm.then_inc(r_mm, 1)
            pe.wait_ge(r_step, R_PROB)
            for t in range(NT):
                mm = pe.transpose(bank[t // 4][0:NE, (t % 4) * P:(t % 4 + 1) * P], prob_e[:, t, :], ident)
            mm.then_inc(r_mm, 1)
            pe.wait_ge(r_step, R_TOP)
            pe.transpose(bank[4][:, 0:NE], top_val[0:NE, 0:CAPS], ident[0:NE, 0:NE])
            pe.transpose(bank[4][:, NE:2 * NE], top_idx_f[0:NE, 0:CAPS], ident[0:NE, 0:NE])
            pe.transpose(bank[4][0:CAPP, 2 * NE:3 * NE], top_val[0:NE, CAPS:CAP], ident[0:NE, 0:NE])
            pe.transpose(bank[4][0:CAPP, 3 * NE:4 * NE], top_idx_f[0:NE, CAPS:CAP],
                         ident[0:NE, 0:NE]).then_inc(r_mm, 1)

            def gathered(half, b, k, q, first=False):
                if k == 0:
                    pe.wait_ge(rows_in[b], half * 16 + 16)
                    pe.wait_ge(rows_p_in[b], half * 16 + 16)
                if not (first and k < 2):
                    pe.wait_ge(tr_out, q - 1)
                o = bank[6 + k % 2]
                pe.transpose(o[:, 0:CAPS], x_rows[b][:, k * P:(k + 1) * P], ident)
                pe.transpose(o[:, CAPS:CAP], x_rows_p[b][0:CAPP, k * P:(k + 1) * P],
                             ident[0:CAPP, 0:CAPP]).then_inc(tr_mm, 1)

            def back(e, k, q):
                if k == 0:
                    pe.wait_ge(y_out, e * 8 + 8)
                pe.wait_ge(tr_out, q - 1)
                o = bank[6 + k % 2]
                pe.transpose(o[:, 0:P], yT[:, k, 0:CAPS], ident)
                pe.transpose(o[0:CAPP, P:2 * P], yT[:, k, CAPS:CAP], ident).then_inc(tr_mm, 1)

            def expert(half, b, first=False, final=False):
                e = half * 2 + b
                for f in range(8):
                    s = f // 4
                    if f % 4 == 0:
                        pe.wait_ge(w1_in[s], e * 16 + 16)
                        pe.wait_ge(w3_in[s], e * 16 + 16)
                    if f == 0:
                        pe.wait_ge(tr_out, e * 16 + (8 if first else 0))
                    for w, o, freed in ((w1, bank[f % 2], silu_ok), (w3, bank[2 + f % 2], hid_ok)):
                        if not (first and f < 2):
                            pe.wait_ge(freed, e * 8 + f - 1)
                        for k in range(KD):
                            mm = pe.matmul(o[:, 0:CAP], w[s][:, k, (f % 4) * P:(f % 4 + 1) * P], xsT[b][:, k, :],
                                           start=(k == 0), stop=(k == KD - 1))
                        mm.then_inc(h_mm, 1)
                    if not first:
                        back(e - 1, f, e * 16 + f)
                for dm in range(8):
                    if dm == 0:
                        pe.wait_ge(w2_in[0], e * 16 + 16)
                        pe.wait_ge(w2_in[1], e * 16 + 16)
                        pe.wait_ge(hid_ok, e * 8 + 8)
                    if not (first and dm < 2):
                        pe.wait_ge(y_out, e * 8 + dm - 1)
                    for f in range(8):
                        mm = pe.matmul(bank[4 + dm % 2][:, 0:CAP], w2[f // 4][:, f % 4, dm * P:(dm + 1) * P],
                                       hidT[:, f, :], start=(f == 0), stop=(f == 7))
                    mm.then_inc(y_mm, 1)
                    if not final:
                        gathered(half + b, 1 - b, dm, e * 16 + 8 + dm)

            pe.wait_ge(r_step, R_PICK)
            for k in range(KD):
                gathered(0, 0, k, k, first=True)
            expert(0, 0, first=True)
            with pe.Fori(0, NE // 2 - 1) as i2:
                expert(i2, 1)
                expert(i2 + 1, 0)
            expert(NE // 2 - 1, 1, final=True)
            for k in range(KD):
                back(NE - 1, k, NE * 16 - 8 + k)

        @block.scalar
        def _(act):
            act.wait_ge(cleared, 1)
            act.wait_ge(out_d, 1)
            for cnd in range(2):
                a = act.activation(cond[:, :, cnd], vT[:, V_C + 8 * cnd:V_C + 8 * cnd + 8], ACT.Silu)
            a.then_inc(cond_ok, 1)
            for t in range(NT):
                act.wait_ge(x_in[t], 16)
                a = act.activation(hreg[:, t * D:(t + 1) * D], x_sb[:, t, :], ACT.Square, accum_out=ss_x[:, t:t + 1])
                if t in (3, 7, 8):
                    a.then_inc(ssx_ok, 1)
            act.wait_ge(var_ok, 1)
            act.activation(rs_x, rs_x, ACT.Sqrt).then_inc(sqrt_ok, 1)
            squares = 0
            for n, job in enumerate(JOBS):
                kind = job[0]
                o = bank[n % 8]
                if kind in ("ckv", "cq"):
                    g0, gn = GROUPS[job[2]]
                    src = ckvT if kind == "ckv" else cqT
                    at = g0 if job[2] < 2 or kind == "cq" else KEYS
                    evicted(act, n)
                    if squares >= 2:
                        m = squares - 2
                        if m in LAST_SQ:
                            computed(act, NUM[LAST_SQ[m]])
                        else:
                            act.wait_ge(raw_used, 1 + sum(x not in LAST_SQ for x in range(m)))
                    act.activation(sq[:, squares % 2, 0:gn], src[:, job[1], at:at + gn], ACT.Square).then_inc(sq_ok, 1)
                    squares += 1
                if kind in ("sskv", "ssq"):
                    gn = GROUPS[job[1]][1]
                    m = job[1] + (3 if kind == "ssq" else 0)
                    act.wait_ge(nvar_ok, m + 1)
                    act.activation(rt[:, m % 2, 0:gn], rt[:, m % 2, 0:gn], ACT.Sqrt).then_inc(nsqrt_ok, 1)
                if job[-1] != "A":
                    continue
                computed(act, n)
                if kind == "h":
                    g, k = job[1], job[2]
                    g0, gn = GROUPS[g]
                    cnd = g // 2
                    act.wait_ge(gain_ok, 1)
                    a = act.activation(hT[:, k, g0:g0 + gn], o[:, 0:gn], ACT.Identity,
                                       bias=modT[:, cnd, k:k + 1], scale=gain1[:, cnd, k:k + 1])
                elif kind == "va":
                    a = act.activation(va[:, job[1], :], o[:, 0:256], ACT.Gelu_apprx_tanh)
                elif kind == "u":
                    g0, gn = GROUPS[job[2]]
                    a = act.activation(mixT[:, job[1], g0:g0 + gn], o[:, 0:gn], ACT.Gelu_apprx_tanh)
                elif kind == "pool":
                    g0, gn = GROUPS[job[2]]
                    a = act.activation(mixT[:, 2 + job[1], g0:g0 + gn], o[:, 0:gn], ACT.Copy,
                                       scale=vT[:, V_PS + job[1]:V_PS + job[1] + 1])
                a.then_inc(out_a, 1)

            act.wait_ge(new_st, 32)
            with act.Fori(0, 4) as i:
                for g, (k0, kn) in enumerate(((0, 512), (512, 512), (1024, 384))):
                    act.wait_ge(proj_mm, i * 12 + 7 + g)
                    act.activation(kT[0:64, 0, k0:k0 + kn], bank[g][0:64, 0:kn], ACT.Copy)
                    act.activation(kT[0:64, 1, k0:k0 + kn], bank[g][64:128, 0:kn], ACT.Copy).then_inc(k_out, 1)

                def turned(n, ch):
                    t, j = divmod(n, 2)
                    act.wait_ge(t_mm, i * 50 + 3 * n + ch + 1 if n < 16 else i * 50 + 48 + (n - 16) + 1)
                    w = 512 if n < 16 else P
                    act.activation(probT[:, 2 * (t % 2) + j, ch * 512:ch * 512 + w], bank[6][:, 0:w],
                                   ACT.Copy).then_inc(t_out_a, 1)

                units = 2 * NT
                for n in range(units + 1):
                    if n >= 1:
                        turned(n - 1, 0)
                    if n < units:
                        act.wait_ge(neg_ok, i * 18 + n + 1)
                        if n >= 2:
                            act.wait_ge(t_mm, i * 50 + 3 * (n - 1))
                        w = KEYS if n < 16 else NPR
                        s = 3 * (n % 2)
                        src = ps[:, s:s + 3, :].rearrange("p b f -> p (b f)")[:, 0:w]
                        act.activation(prob[n % 2][:, 0:w], src, ACT.Exp, bias=a_neg[:, n % 4:n % 4 + 1], scale=SCALE,
                                       accum_out=a_sum[:, n % 4:n % 4 + 1]).then_inc(exp_ok, 1)
                    if 1 <= n <= 16:
                        turned(n - 1, 1)

            def h2_evict(t):
                act.wait_ge(h2_mm, 2 * t + 1)
                cnd = t // 8
                for a in range(4):
                    ins = act.activation(h2T[:, a, t * P:(t + 1) * P], bank[4][:, a * P:(a + 1) * P], ACT.Identity,
                                         bias=modT[:, cnd, 24 + a:25 + a], scale=gain2[:, cnd, a:a + 1])
                ins.then_inc(h2_out_a, 1)

            act.wait_ge(gain_ok, 2)
            for t in range(NT):
                act.wait_ge(x2_ok, t + 1)
                if t >= 2:
                    act.wait_ge(xn_st[t % 2], 16 * (t // 2))
                    act.wait_ge(h2_mm, 2 * (t - 1))
                act.activation(x2n[t % 2], x2[t % 2], ACT.Square, accum_out=ss2[:, t % 2:t % 2 + 1]).then_inc(ss2_ok, 1)
                act.wait_ge(var2_ok, t + 1)
                act.activation(rs2[:, t % 2:t % 2 + 1], ss2[:, t % 2:t % 2 + 1], ACT.Sqrt).then_inc(sqrt2_ok, 1)
                if t >= 1:
                    h2_evict(t - 1)
            h2_evict(NT - 1)

            act.wait_ge(r_step, R_SHIFT)
            act.activation(prob_e, logit, ACT.Exp).then_inc(r_exp, 1)

            def expert(e, first=False):
                for f in range(8):
                    act.wait_ge(h_mm, e * 16 + 2 * f + 1)
                    if not (first and f < 2):
                        act.wait_ge(hid_ok, e * 8 + f - 1)
                    act.activation(silu_h[:, f % 2, :], bank[f % 2][:, 0:CAP], ACT.Silu).then_inc(silu_ok, 1)
                for dm in range(8):
                    act.wait_ge(y_mm, e * 8 + dm + 1)
                    for cnd, (a, z) in enumerate(((0, CAPS), (CAPS, CAP))):
                        ins = act.activation(yT[:, dm, a:z], bank[4 + dm % 2][:, a:z], ACT.Copy,
                                             scale=modT[:, cnd, 40 + dm:41 + dm])
                    ins.then_inc(y_out, 1)

            expert(0, first=True)
            with act.Fori(1, NE) as e:
                expert(e)

            for t in range(NT):
                s = t % 4
                act.wait_ge(fin_in[s], 16 * (t // 4 + 1))
                act.activation(fin_junk, x_fin[s], ACT.Square, accum_out=ss_x[:, t:t + 1]).then_inc(fss_ok, 1)
                act.wait_ge(fvar_ok, t + 1)
                act.activation(rs_x[:, t:t + 1], rs_x[:, t:t + 1], ACT.Sqrt).then_inc(fsqrt_ok, 1)

        @block.vector
        def _(dve):
            steps = [0]

            def then(ins):
                steps[0] += 1
                ins.then_inc(dve_step, 1)
                dve.wait_ge(dve_step, steps[0])

            dve.memset(cond[:], 0.0)
            dve.memset(w_pool_sb[:], 0.0)
            dve.memset(b_rows, 0.0).then_inc(cleared, 1)
            normed = 0
            for n, job in enumerate(JOBS):
                kind = job[0]
                o = bank[n % 8]
                if job[-1] != "D":
                    continue
                computed(dve, n)
                if kind == "vecs":
                    dve.tensor_copy(vT[:], o[:, 0:V_ROWS]).then_inc(out_d, 1)
                elif kind == "w_s":
                    dve.tensor_copy(wsT[:].rearrange("p h q -> p (h q)"), o).then_inc(out_d, 1)
                elif kind == "ada":
                    r = job[1]
                    if r == 0:
                        dve.wait_ge(brows_in, 16 * 12)
                    dve.tensor_tensor(mod_rows, o, b_rows[:, r, :], ALU.add).then_inc(out_d, 1)
                elif kind == "mod":
                    r = job[1]
                    v = o.rearrange("p (j g c) -> p g j c", j=4, g=4)
                    for cnd in range(2):
                        ins = dve.tensor_copy(modT[:, cnd, 16 * r:16 * r + 16].rearrange("p (g j) -> p g j", g=4),
                                              v[:, :, :, cnd])
                    ins.then_inc(out_d, 1)
                    if r in (0, 2):
                        evicted(dve, n)
                        gain, at, vn = (gain1, 8, V_N1) if r == 0 else (gain2, 32, V_N2)
                        for cnd in range(2):
                            ins = dve.scalar_tensor_tensor(out=gain[:, cnd, :], in0=modT[:, cnd, at:at + 8], scalar=1.0,
                                                           in1=vT[:, vn:vn + 8], op0=ALU.add, op1=ALU.mult)
                        ins.then_inc(gain_ok, 1)
                    if r == 0:
                        dve.wait_ge(ssx_ok, 3)
                        dve.tensor_scalar(rs_x, ss_x, 1.0 / D, EPS, ALU.mult, ALU.add).then_inc(var_ok, 1)
                        dve.wait_ge(sqrt_ok, 1)
                        dve.reciprocal(rx, rs_x).then_inc(rx_ok, 1)
                        dve.wait_ge(rx_ok, 1)
                        for t in range(NT):
                            dve.tensor_scalar(x_sb[:, t, :], x_sb[:, t, :], rx[:, t:t + 1], None,
                                              ALU.mult).then_inc(xn_ok, 1)
                        dve.wait_ge(gain_ok, 1)
                elif kind == "g1":
                    dve.tensor_copy(g1_rows[:, job[1], job[2] * 512:job[2] * 512 + 512], o).then_inc(out_d, 1)
                elif kind == "h":
                    g, k = job[1], job[2]
                    g0, gn = GROUPS[g]
                    dve.tensor_scalar(hT[:, k, g0:g0 + gn], o[:, 0:gn], gain1[:, g // 2, k:k + 1],
                                      modT[:, g // 2, k:k + 1], ALU.mult, ALU.add).then_inc(out_d, 1)
                elif kind == "pin":
                    m, g = job[1], job[2]
                    gn = GROUPS[g][1]
                    if (m, g) == (0, 0):
                        dve.wait_ge(pool_cleared, 1)
                        dve.wait_ge(w_in_in, 16)
                        src = w_in_sb[:, :, OFF_KR:COLS].rearrange("p k (b s e) -> p k b s e", b=2, s=2)
                        dst = w_rot[:].rearrange("p k (b s e) -> p k b s e", b=2, s=2)
                        for s in range(2):
                            ins = dve.tensor_copy(dst[:, :, :, s, :], src[:, :, :, 1 - s, :])
                        ins.then_inc(wrot_ok, 1)
                    dve.tensor_copy(pin[:, m, FLAT_AT[g]:FLAT_AT[g] + gn], o[:, 0:gn]).then_inc(out_d, 1)
                elif kind == "ckv":
                    g0, gn = GROUPS[job[2]]
                    at = g0 if job[2] < 2 else KEYS
                    dve.tensor_copy(ckvT[:, job[1], at:at + gn], o[:, 0:gn]).then_inc(out_d, 1)
                elif kind == "cq":
                    g0, gn = GROUPS[job[2]]
                    dve.tensor_copy(cqT[:, job[1], g0:g0 + gn], o[:, 0:gn]).then_inc(out_d, 1)
                elif kind in ("sskv", "ssq"):
                    g = job[1]
                    g0, gn = GROUPS[g]
                    width = KVL if kind == "sskv" else QL
                    r = rt[:, normed % 2, 0:gn]
                    dve.tensor_scalar(r, o[:, 0:gn], 1.0 / width, EPS, ALU.mult, ALU.add).then_inc(nvar_ok, 1)
                    dve.wait_ge(nvar_ok, normed + 1)
                    dve.wait_ge(nsqrt_ok, normed + 1)
                    then(dve.reciprocal(r, r))
                    normed += 1
                    if kind == "sskv":
                        at = g0 if g < 2 else KEYS
                        for m in range(2):
                            ins = dve.scalar_tensor_tensor(out=ckvT[:, m, at:at + gn], in0=ckvT[:, m, at:at + gn],
                                                           scalar=vT[:, V_KN + m:V_KN + m + 1], in1=r,
                                                           op0=ALU.mult, op1=ALU.mult)
                        ins.then_inc(out_d, 1)
                    else:
                        dve.wait_ge(rope_in, 32)
                        dve.tensor_tensor(q_mul[:, g0:g0 + gn], q_mul[:, g0:g0 + gn], r, ALU.mult).then_inc(out_d, 1)
                elif kind == "kr":
                    g0, gn = GROUPS[job[1]]
                    at = g0 if job[1] < 2 else KEYS
                    if job[1] == 0:
                        computed(dve, NUM[("kr", 2)])
                    evicted(dve, n - 1)
                    tmp = rt[64:128, 0, 0:gn]
                    main = rt[64:128, 1, 0:gn]
                    dve.tensor_tensor(tmp, o[0:64, 0:gn], kr_mul[0:64, g0:g0 + gn], ALU.mult)
                    then(dve.tensor_tensor(main, o[64:128, 0:gn], kr_mul[64:128, g0:g0 + gn], ALU.mult))
                    dve.tensor_tensor(kT[64:128, 0, at:at + gn], tmp, main, ALU.add)
                    dve.tensor_tensor(kT[64:128, 1, at:at + gn], tmp, main, ALU.add).then_inc(out_d, 1)
                elif kind == "gate":
                    m, g = job[1], job[2]
                    g0, gn = GROUPS[g]
                    if (m, g) == (0, 0):
                        dve.wait_ge(bs_in, 16 * 4)
                        evicted(dve, NUM[("u", 1, 2)])
                    a = gn // P
                    tmp = sq[:, n % 2, 0:gn]
                    then(dve.tensor_tensor(tmp.rearrange("p (a q) -> p a q", a=a),
                                           o[:, 0:gn].rearrange("p (a q) -> p a q", a=a),
                                           bs_sb[:, m:m + 1, :].to_broadcast([P, a, P]), ALU.add))
                    dve.tensor_tensor(mixT[:, m, g0:g0 + gn], mixT[:, m, g0:g0 + gn], tmp, ALU.mult).then_inc(out_d, 1)
                elif kind == "cache_c":
                    dve.tensor_copy(ckvT[:, :, NS:KEYS], o.rearrange("p (k s) -> p k s", k=2)).then_inc(out_d, 1)
                elif kind == "cache_r":
                    dve.tensor_copy(kT[64:128, 0, NS:KEYS], o[64:128, 0:PAST])
                    dve.tensor_copy(kT[64:128, 1, NS:KEYS], o[64:128, 0:PAST]).then_inc(out_d, 1)
                elif kind == "new":
                    dve.tensor_copy(new_out, o[:, 0:KVL + NOPE]).then_inc(out_d, 1)

            dve.wait_ge(new_st, 32)
            evicted(dve, max(n for n in range(len(JOBS)) if JOBS[n][-1] == "D"))
            with dve.Fori(0, 4) as i:
                dve.wait_ge(wq_in, i * 16 + 16)
                for k in range(3):
                    g = vT[:, V_QN + k:V_QN + k + 1]
                    raw = wq_raw[:, k, :].rearrange("p (j f) -> p j f", j=2)
                    dve.tensor_scalar(wq[:, k, :, 0:QK], raw, g, None, ALU.mult)
                    src = raw[:, :, NOPE:QK].rearrange("p j (b s e) -> p j b s e", b=2, s=2)
                    dst = wq[:, k, :, QK:P].rearrange("p j (b s e) -> p j b s e", b=2, s=2)
                    for s in range(2):
                        ins = dve.tensor_scalar(dst[:, :, :, s, :], src[:, :, :, 1 - s, :], g, None, ALU.mult)
                ins.then_inc(wq_ok, 1)
                for j in range(2):
                    for g, (g0, gn) in enumerate(GROUPS):
                        dve.wait_ge(proj_mm, i * 12 + 3 * j + g + 1)
                        dve.tensor_tensor(qT[:, j, g0:g0 + gn], bank[3 * j + g][:, 0:gn], q_mul[:, g0:g0 + gn],
                                          ALU.mult).then_inc(q_out, 1)
                for g, (k0, kn) in enumerate(((0, 4), (4, 4), (8, 3))):
                    dve.wait_ge(proj_mm, i * 12 + 10 + g)
                    dve.tensor_copy(v_sb[:, k0:k0 + kn, :].rearrange("p a f -> p (a f)"),
                                    bank[3 + g][:, 0:kn * P]).then_inc(v_out, 1)
                units = 2 * NT

                def weighed(t):
                    dve.wait_ge(pv_mm, i * NT + t + 1)
                    dve.tensor_copy(mreg[:, bass.ds(i * T + 4 * T + t * P, P)], bank[7][:, 0:P]).then_inc(pv_out, 1)

                for n in range(units):
                    w = KEYS if n < 16 else NPR
                    s = 3 * (n % 2)
                    r = n % 4
                    src = ps[:, s:s + 3, :].rearrange("p b f -> p (b f)")[:, 0:w]
                    dve.wait_ge(s_mm, i * 18 + n + 1)
                    dve.tensor_reduce(a_max[:, r:r + 1], src, AX_X, ALU.max).then_inc(max_ok, 1)
                    dve.wait_ge(max_ok, i * 18 + n + 1)
                    dve.tensor_scalar(a_neg[:, r:r + 1], a_max[:, r:r + 1], -SCALE, None, ALU.mult).then_inc(neg_ok, 1)
                    if n % 2 and n >= 3:
                        weighed((n - 3) // 2)
                    dve.wait_ge(exp_ok, i * 18 + n + 1)
                    dve.reciprocal(a_rec[:, r:r + 1], a_sum[:, r:r + 1]).then_inc(rec_ok, 1)
                    dve.wait_ge(rec_ok, i * 18 + n + 1)
                    dve.tensor_scalar(prob[n % 2][:, 0:w], prob[n % 2][:, 0:w], a_rec[:, r:r + 1], None,
                                      ALU.mult).then_inc(norm_ok, 1)
                    if 1 <= n <= 16:
                        t, j = divmod(n - 1, 2)
                        dve.wait_ge(t_mm, i * 50 + 3 * n)
                        dve.tensor_copy(probT[:, 2 * (t % 2) + j, 1024:KEYS], bank[6][:, 0:256]).then_inc(t_out_d, 1)
                weighed(NT - 1)

            def h2_evict(t):
                dve.wait_ge(h2_mm, 2 * t + 2)
                cnd = t // 8
                for a in range(4):
                    kk = 4 + a
                    ins = dve.tensor_scalar(h2T[:, kk, t * P:(t + 1) * P], bank[5][:, a * P:(a + 1) * P],
                                            gain2[:, cnd, kk:kk + 1], modT[:, cnd, 24 + kk:25 + kk], ALU.mult, ALU.add)
                ins.then_inc(h2_out_d, 1)

            def logits_out(g):
                g0, gn = GROUPS[g]
                dve.wait_ge(lg_mm, g + 1)
                dve.tensor_copy(aff[0:NE, g0:g0 + gn], bank[6][0:NE, 0:gn]).then_inc(lg_out, 1)

            dve.wait_ge(gain_ok, 2)
            for t in range(NT):
                s, cnd = t % 2, t // 8
                if t >= 2:
                    dve.wait_ge(x2_st[s], 16 * (t // 2))
                    dve.wait_ge(ss2_ok, t - 1)
                for hf in range(2):
                    x = 2 * t + hf
                    dve.wait_ge(o_mm, x + 1)
                    dve.tensor_tensor(x2[s][:, hf * 512:(hf + 1) * 512], bank[x % 4],
                                      g1_rows[:, cnd, hf * 512:(hf + 1) * 512], ALU.mult).then_inc(o_out, 1)
                dve.wait_ge(o_out, 2 * t + 2)
                dve.wait_ge(xa_in[s], 16 * (t // 2 + 1))
                dve.tensor_tensor(x2[s], x2[s], x_again[s], ALU.add).then_inc(x2_ok, 1)
                dve.wait_ge(ss2_ok, t + 1)
                dve.tensor_scalar(ss2[:, s:s + 1], ss2[:, s:s + 1], 1.0 / D, EPS, ALU.mult, ALU.add).then_inc(var2_ok, 1)
                dve.wait_ge(sqrt2_ok, t + 1)
                dve.reciprocal(rs2[:, s:s + 1], rs2[:, s:s + 1]).then_inc(rec2_ok, 1)
                dve.wait_ge(rec2_ok, t + 1)
                dve.tensor_scalar(x2n[s], x2[s], rs2[:, s:s + 1], None, ALU.mult).then_inc(x2n_ok, 1)
                if t >= 1:
                    h2_evict(t - 1)
                if t == 5:
                    logits_out(0)
            h2_evict(NT - 1)
            logits_out(1)
            logits_out(2)

            done = [0]

            def routed(ins):
                done[0] += 1
                ins.then_inc(r_step, 1)
                dve.wait_ge(r_step, done[0])

            dve.wait_ge(r_mm, 1)
            routed(dve.tensor_copy(logit.rearrange("p t e -> p (t e)"), bank[7][:, 0:NT * NE]))
            routed(dve.tensor_reduce(r_stat[:, 0, :], logit, AX_X, ALU.max))
            routed(dve.tensor_tensor(logit, logit, r_stat[:, 0, :].unsqueeze(2).to_broadcast([P, NT, NE]), ALU.subtract))
            assert done[0] == R_SHIFT
            dve.wait_ge(r_exp, 1)
            routed(dve.tensor_reduce(r_stat[:, 1, :], prob_e, AX_X, ALU.add))
            routed(dve.reciprocal(r_stat[:, 2, :], r_stat[:, 1, :]))
            routed(dve.tensor_tensor(prob_e, prob_e, r_stat[:, 2, :].unsqueeze(2).to_broadcast([P, NT, NE]), ALU.mult))
            assert done[0] == R_PROB
            dve.wait_ge(r_mm, 2)
            routed(dve.tensor_copy(aff[0:NE, :], ps[0:NE, 0:3, :].rearrange("p b f -> p (b f)")[:, 0:T]))
            for cnd, (a, z, at, cap) in enumerate(((0, NS, 0, CAPS), (NS, T, CAPS, CAPP))):
                for r in range(cap // 8):
                    v = top_val[0:NE, at + 8 * r:at + 8 * r + 8]
                    routed(dve.max(v, aff[0:NE, a:z]))
                    dve.max_index(top_idx[:, at + 8 * r:at + 8 * r + 8], v, aff[0:NE, a:z])
                    routed(dve.match_replace(aff[0:NE, a:z], v, aff[0:NE, a:z], -1.0))
            routed(dve.tensor_copy(top_idx_f[0:NE, :], top_idx[:]))
            routed(dve.tensor_scalar(top_idx_f[0:NE, CAPS:CAP], top_idx_f[0:NE, CAPS:CAP], float(NS), None, ALU.add))
            assert done[0] == R_TOP
            dve.wait_ge(r_mm, 3)
            dve.tensor_copy(picked[:, 0, :], bank[4][:, 0:NE])
            dve.tensor_copy(picked[0:CAPP, 2, :], bank[4][0:CAPP, 2 * NE:3 * NE])
            dve.tensor_copy(pick_s[:], bank[4][:, NE:2 * NE])
            routed(dve.tensor_copy(pick_p[0:CAPP, :], bank[4][0:CAPP, 3 * NE:4 * NE]))
            assert done[0] == R_PICK

            def gathered(b, k, q):
                dve.wait_ge(tr_mm, q + 1)
                for cnd, (a, z) in enumerate(((0, CAPS), (CAPS, CAP))):
                    ins = dve.tensor_scalar(xsT[b][:, k, a:z], bank[6 + k % 2][:, a:z], gain2[:, cnd, k:k + 1],
                                            modT[:, cnd, 24 + k:25 + k], ALU.mult, ALU.add)
                ins.then_inc(tr_out, 1)

            def back(e, b, k, q, first=False):
                if k == 0 and not first:
                    dve.wait_ge(added, (e - 1) * 16)
                    dve.wait_ge(added_p, (e - 1) * 16)
                dve.wait_ge(tr_mm, q + 1)
                o = bank[6 + k % 2]
                dve.tensor_scalar(y_rows[b][:, k * P:(k + 1) * P], o[:, 0:P],
                                  creg[:, bass.ds(T + 612 + e, 1)], None, ALU.mult)
                dve.tensor_scalar(y_rows_p[b][0:CAPP, k * P:(k + 1) * P], o[0:CAPP, P:2 * P],
                                  creg[0:CAPP, bass.ds(T + 612 + 2 * NE + e, 1)], None, ALU.mult).then_inc(tr_out, 1)

            def expert(e, b, first=False, unscattered=False, final=False):
                for f in range(8):
                    dve.wait_ge(silu_ok, e * 8 + f + 1)
                    dve.wait_ge(h_mm, e * 16 + 2 * f + 2)
                    dve.tensor_tensor(hidT[:, f, :], bank[2 + f % 2][:, 0:CAP], silu_h[:, f % 2, :],
                                      ALU.mult).then_inc(hid_ok, 1)
                    if not first:
                        back(e - 1, 1 - b, f, e * 16 + f, first=unscattered)
                for dm in range(8):
                    if not final:
                        gathered(1 - b, dm, e * 16 + 8 + dm)

            for k in range(KD):
                gathered(0, k, k)
            expert(0, 0, first=True)
            expert(1, 1, unscattered=True)
            expert(2, 0, unscattered=True)
            with dve.Fori(1, NE // 2 - 1) as i2:
                expert(i2 * 2 + 1, 1)
                expert(i2 * 2 + 2, 0)
            expert(NE - 1, 1, final=True)
            for k in range(KD):
                back(NE - 1, 1, k, NE * 16 - 8 + k)

            for t in range(NT):
                s = t % 4
                dve.wait_ge(fss_ok, t + 1)
                dve.tensor_scalar(rs_x[:, t:t + 1], ss_x[:, t:t + 1], 1.0 / D, EPS, ALU.mult, ALU.add).then_inc(fvar_ok, 1)
                dve.wait_ge(fsqrt_ok, t + 1)
                dve.reciprocal(rx[:, t:t + 1], rs_x[:, t:t + 1]).then_inc(frec_ok, 1)
                dve.wait_ge(frec_ok, t + 1)
                if t == 0:
                    dve.wait_ge(frow_in, 16)
                dve.scalar_tensor_tensor(out=x_fin[s], in0=x_fin[s], scalar=rx[:, t:t + 1], in1=final_row,
                                         op0=ALU.mult, op1=ALU.mult).then_inc(fin_ok, 1)

        @block.gpsimd
        def _(pool):
            steps = [0]

            def then(ins):
                steps[0] += 1
                ins.then_inc(pool_step, 1)
                pool.wait_ge(pool_step, steps[0])

            pool.wait_ge(ada_mm, 24)
            pool.memset(pin, 0.0).then_inc(pool_cleared, 1)
            pool.wait_ge(inv_in, 16)
            for m in range(2):
                evicted(pool, NUM[("pin", m, 2)])
                p, a, b = pin[:, m, :], win_sum[2 * m], win_sum[2 * m + 1]
                then(pool.memset(b[:, 0:FLAT], 0.0))
                then(pool.memset(a[:, 0:FLAT], 0.0))
                then(pool.tensor_tensor(a[:, 1:FLAT], p[:, 1:FLAT], p[:, 0:FLAT - 1], ALU.add))
                lo = 64 if m == 0 else 0
                then(pool.tensor_tensor(b[lo:, 2:FLAT - 1], a[lo:, 1:FLAT - 2], a[lo:, 3:FLAT], ALU.add))
                if m == 1:
                    then(pool.tensor_tensor(a[:, 4:FLAT - 4], b[:, 2:FLAT - 6], b[:, 6:FLAT - 2], ALU.add))
                    then(pool.tensor_tensor(b[64:, 8:FLAT - 8], a[64:, 4:FLAT - 12], a[64:, 12:FLAT - 4], ALU.add))
                then(pool.tensor_tensor(a[0:64, :], a[0:64, :], inv_sb[0:64, m, :], ALU.mult))
                then(pool.tensor_tensor(a[64:, :], b[64:, :], inv_sb[64:, m, :], ALU.mult))
                pool.tensor_tensor(a, a, p, ALU.subtract).then_inc(diff_ok, 1)
            computed(pool, NUM[("kr", 2)])
            pool.memset(cache_r, 0.0).then_inc(crope_zero, 1)

            def gather(e, b, later=True):
                if later:
                    pool.wait_ge(h_mm, (e - 2) * 16 + 1)
                pool.tensor_copy(idx_g[b][:], pick_s[:, e:e + 1])
                pool.tensor_copy(idx_gp[b][0:CAPP, :], pick_p[0:CAPP, e:e + 1]).then_inc(idx_ok, 1)
                pool.wait_ge(idx_ok, e + 1)
                pool.indirect_dma_start(out=x_rows[b], out_offset=None, in_=xn_dram,
                                        in_offset=bass.IndirectOffsetOnAxis(ap=idx_g[b][:], axis=0)
                                        ).then_inc(rows_in[b], 16)
                pool.indirect_dma_start(out=x_rows_p[b][0:CAPP, :], out_offset=None, in_=xn_dram,
                                        in_offset=bass.IndirectOffsetOnAxis(ap=idx_gp[b][0:CAPP, :], axis=0)
                                        ).then_inc(rows_p_in[b], 16)

            def scatter(e, b, ready):
                pool.tensor_copy(idx_s[:], pick_s[:, e:e + 1])
                pool.tensor_copy(idx_sp[0:CAPP, :], pick_p[0:CAPP, e:e + 1]).then_inc(sidx_ok, 1)
                pool.wait_ge(sidx_ok, e + 1)
                pool.wait_ge(tr_out, ready)
                pool.indirect_dma_start(out=x2_dram, out_offset=bass.IndirectOffsetOnAxis(ap=idx_s[:], axis=0),
                                        in_=y_rows[b], in_offset=None, compute_op=ALU.add).then_inc(added, 16)
                pool.indirect_dma_start(out=x2_dram,
                                        out_offset=bass.IndirectOffsetOnAxis(ap=idx_sp[0:CAPP, :], axis=0),
                                        in_=y_rows_p[b][0:CAPP, :], in_offset=None,
                                        compute_op=ALU.add).then_inc(added_p, 16)
                pool.wait_ge(added, (e + 1) * 16)
                pool.wait_ge(added_p, (e + 1) * 16)

            pool.wait_ge(r_step, R_PICK)
            for s in range(2):
                pool.wait_ge(xn_st[s], 16 * (5 - s))
                pool.wait_ge(x2_st[s], 16 * (5 - s))
            gather(0, 0, later=False)
            gather(1, 1, later=False)
            for e in range(NE):
                if e + 2 < NE:
                    gather(e + 2, e % 2)
                scatter(e, e % 2, min(e * 16 + 24, NE * 16))


R_SHIFT, R_PROB = 3, 6
R_TOP = R_PROB + 1 + 2 * (CAP // 8) + 2
R_PICK = R_TOP + 1
LAST_SQ = {2 * g + 1: ("sskv", g) for g in range(3)} | {6 + 3 * g + 2: ("ssq", g) for g in range(3)}


_INS = ['x_prompt', 'x_sample', 'cache_ckv', 'cache_krope', 'c', 'c_ctx', 'w_ada', 'b_ada', 'norm1_g', 'norm2_g',
        'w_in', 'w_s', 'b_s', 'w_pool', 'pool_scale', 'q_norm_g', 'w_qb', 'kv_norm_g', 'w_kvb', 'w_out', 'w_router',
        'w_e1', 'w_e3', 'w_e2', 'final_norm_g']
_OUTS = [(1, NPR, D), (1, NS, D), (1, 1, NPR, KVL), (1, 1, NPR, ROPE)]


def kernel(**inputs):
    import concourse.bacc as _bacc
    from concourse.bass_utils import run_bass_kernel_spmd as _run

    nc = _bacc.Bacc("TRN2", target_bir_lowering=False, num_devices=1)
    arrays, args = {}, []
    for name, a in [(n, inputs[n]) for n in _INS] + list(tables().items()):
        a = np.ascontiguousarray(a)
        arrays[f"in_{name}_dram"] = a
        args.append(nc.dram_tensor(f"in_{name}_dram", a.shape, mybir.dt.from_np(a.dtype), kind="ExternalInput").ap())
    for i, shape in enumerate(_OUTS):
        args.append(nc.dram_tensor(f"out_{i}_dram", shape, F32, kind="ExternalOutput").ap())
    build(nc, *args)
    r = _run(nc, [arrays], core_ids=[0])
    return tuple(r.results[0][f"out_{i}_dram"] for i in range(len(_OUTS)))
```

```python
from contextlib import ExitStack

import numpy as np

import concourse.bass as bass
from concourse import mybir

ALU = mybir.AluOpType
ACT = mybir.ActivationFunctionType
F32 = mybir.dt.float32
U32 = mybir.dt.uint32
AX_X = mybir.AxisListType.X

P = 128
D = 1024
KD = D // P
NS, NPR = 1024, 128
T = NS + NPR
NT = T // P
GROUPS = [(0, 512), (512, 512), (1024, 128)]
GTILES = [range(0, 4), range(4, 8), range(8, 9)]
PAST = 256
KEYS = NS + PAST
ALLK = KEYS + NPR
HEADS, NOPE, ROPE, VD = 8, 64, 32, 64
QK = NOPE + ROPE
QL, KVL = 384, 256
SCALE = float(QK) ** -0.5
OFF_V, OFF_P, OFF_CQ, OFF_CKV, OFF_KR, COLS = 256, 512, 768, 1152, 1408, 1440
NE, FF = 16, 1024
CAPS, CAPP = 2 * NS // NE, 2 * NPR // NE
CAP = CAPS + CAPP
EPS = 1e-6
PAD = 8
FLAT = NS + NPR + 4 * PAD
FLAT_AT = [PAD, PAD + 512, NS + 3 * PAD]
RING = 6
V_N1, V_N2, V_C, V_PS, V_QN, V_KN, V_ROWS = 0, 8, 16, 32, 34, 37, 39


def tables():
    eye_ones = np.concatenate([np.eye(P), np.ones((P, P))], 1).astype(np.float32)
    inv = np.zeros((P, 2, FLAT), np.float32)
    for g, w in enumerate((2, 4, 8, 16)):
        left, right = w // 2, w - 1 - w // 2
        for n, at in ((NS, FLAT_AT[0]), (NPR, FLAT_AT[2])):
            t = np.arange(n)
            count = np.clip(t + right + 1, 0, n) - np.clip(t - left, 0, n)
            inv[64 * (g % 2):64 * (g % 2) + 64, g // 2, at:at + n] = 1.0 / count.astype(np.float32)
    axis = ROPE // 2
    freq = (1.0 / (10000.0 ** (np.arange(0, axis, 2, dtype=np.float32) / axis))).astype(np.float32)
    tok = np.arange(NS)
    pos = [(tok // 64).astype(np.float32), (tok % 64).astype(np.float32)]
    cos = np.ones((ROPE, T), np.float32)
    sin = np.zeros((ROPE, T), np.float32)
    for r in range(ROPE):
        ang = pos[r // axis] * freq[r % 8]
        cos[r, :NS] = np.cos(ang)
        sin[r, :NS] = np.sin(ang) * (-1.0 if r % axis < 8 else 1.0)
    q_rope = np.concatenate([np.ones((NOPE, T), np.float32), cos, sin])
    k_rope = np.concatenate([sin, sin, cos, cos])
    return {
        "eye_ones": eye_ones,
        "inv_count": inv.reshape(P, 2 * FLAT),
        "q_rope": q_rope,
        "k_rope": k_rope,
    }


def plan_jobs():
    jobs = [("vecs", "D"), ("w_s", "D")]
    jobs += [("h", g, k, "DA"[k % 2]) for g in range(3) for k in range(KD)]
    jobs += [("ada", 0, "D"), ("mod", 0, "D")]
    jobs += [("va", t, "A") for t in range(NT)]
    jobs += [("u", 0, g, "A") for g in range(3)]
    jobs += [("ada", 1, "D"), ("mod", 1, "D")] + [("g1", c, hf, "D") for c in range(2) for hf in range(2)]
    jobs += [("u", 1, g, "A") for g in range(3)]
    jobs += [("ada", 2, "D"), ("mod", 2, "D")]
    jobs += [("pin", m, g, "D") for m in range(2) for g in range(3)]
    latent = [("ckv", m, g, "D") for g in range(3) for m in range(2)]
    latent += [("cq", m, g, "D") for g in range(3) for m in range(3)] + [("kr", 0, "D")]
    for n, job in enumerate(latent):
        jobs.append(job)
        if n and latent[n - 1][:2] in (("ckv", 1), ("cq", 2)):
            jobs.append(("sskv" if latent[n - 1][0] == "ckv" else "ssq", latent[n - 1][2], "D"))
    jobs += [("kr", g, "D") for g in (1, 2)]
    jobs += [("gate", m, g, "D") for m in range(2) for g in range(3)]
    jobs += [("pool", m, g, "A") for m in range(2) for g in range(3)]
    jobs += [("cache_c", "D"), ("cache_r", "D"), ("new", "D")]
    return jobs


def build(nc, x_prompt, x_sample, cache_ckv, cache_krope, c, c_ctx, w_ada, b_ada, norm1_g, norm2_g,
          w_in, w_s, b_s, w_pool, pool_scale, q_norm_g, w_qb, kv_norm_g, w_kvb, w_out, w_router,
          w_e1, w_e3, w_e2, final_norm_g, eye_ones, inv_count, q_rope, k_rope,
          y_prompt, y_sample, new_ckv, new_krope):
    JOBS = plan_jobs()
    NUM = {j[:-1]: n for n, j in enumerate(JOBS)}
    OUT = [sum(j[-1] == JOBS[n][-1] for j in JOBS[:n + 1]) for n in range(len(JOBS))]

    ctx = ExitStack()
    with ctx:
        def sb(name, shape, dt=F32):
            return ctx.enter_context(nc.sbuf_tensor(name, shape, dt))

        def sem(name):
            return ctx.enter_context(nc.semaphore(name))

        ps = ctx.enter_context(nc.psum_tensor("ps", [P, 8, 512], F32))
        bank = [ps[:, b, :] for b in range(8)]

        wreg = sb("wreg", [P, 24576])
        hreg = sb("hreg", [P, 9216])
        mreg = sb("mreg", [P, 9216])
        creg = sb("creg", [P, 2 * ALLK])

        def view(region, at, *dims):
            n = int(np.prod(dims))
            v = region[:, at:at + n]
            if len(dims) == 2:
                return v.rearrange("p (a b) -> p a b", a=dims[0])
            if len(dims) == 3:
                return v.rearrange("p (a b c) -> p a b c", a=dims[0], b=dims[1])
            return v

        w_in_sb = view(wreg, 0, KD, COLS)
        ada_ring = [view(wreg, 11520 + s * 2048, 2048) for s in range(RING)]
        pin = view(wreg, 11520, 2, FLAT)
        win_sum = [view(wreg, 13888 + s * FLAT, FLAT) for s in range(4)]
        cqT = view(wreg, 18624, 3, T)
        q_mul = view(wreg, 22080, T)
        kr_mul = view(wreg, 23232, T)
        qT = view(wreg, 0, 2, T)
        kT = view(wreg, 2304, 2, ALLK)
        v_sb = view(wreg, 5120, 11, P)
        new_out = view(wreg, 6528, KVL + NOPE)
        cache_c = view(wreg, 6848, 2, KVL)
        cache_r = view(wreg, 7360, 2, P)
        w_out_sb = view(wreg, 8192, KD, D)
        x_again = [view(wreg, 16384 + s * D, D) for s in range(2)]
        x2 = [view(wreg, 18432 + s * D, D) for s in range(2)]
        x2n = [view(wreg, 20480 + s * D, D) for s in range(2)]
        w1 = [view(wreg, s * 4096, KD, 512) for s in range(2)]
        w3 = [view(wreg, 8192 + s * 4096, KD, 512) for s in range(2)]
        w2 = [view(wreg, 16384 + s * 4096, 4, D) for s in range(2)]
        x_fin = [view(wreg, t * D, D) for t in range(NT)]
        hT = view(hreg, 0, KD, T)
        prob = [view(hreg, s * KEYS, KEYS) for s in range(2)]
        probT = view(hreg, 2 * KEYS, 4, KEYS)
        wq_raw = view(hreg, 7680, 3, 2 * QK)
        wq = view(hreg, 8256, 3, 2, P)
        h2T = hT
        y_rows = [view(hreg, s * D, D) for s in range(2)]
        y_rows_p = [view(hreg, 2048 + s * D, D) for s in range(2)]
        final_row = view(hreg, 4096, D)
        x_sb = view(mreg, 0, NT, D)
        mixT = view(mreg, 0, KD, T)
        inv_sb = view(mreg, 2304, 2, FLAT)
        sq = view(mreg, 4864, 4, 512)
        va = view(mreg, 6912, NT, 256)
        x_rows = [view(mreg, s * D, D) for s in range(2)]
        x_rows_p = [view(mreg, 2048 + s * D, D) for s in range(2)]
        xsT = [view(mreg, 4096 + s * KD * CAP, KD, CAP) for s in range(2)]
        yT = view(mreg, 6400, KD, CAP)
        hidT = view(mreg, 7552, KD, CAP)
        silu_h = view(mreg, 8704, 2, CAP)
        fin_squares = [view(mreg, s * D, D) for s in range(2)]
        b_rows = view(creg, 0, 3, 512)
        ckvT = view(creg, 0, 2, ALLK)
        aff = view(creg, 0, T)
        logit = view(creg, T, NT, NE)
        prob_e = view(creg, T + 144, NT, NE)
        r_stat = view(creg, T + 288, 4, NT)
        top_val = view(creg, T + 324, CAP)
        top_idx_f = view(creg, T + 468, CAP)
        picked = view(creg, T + 612, 4, NE)
        const = sb("const", [P, 2 * P])
        ident, ones = const[:, 0:P], const[:, P:2 * P]
        vecs = sb("vecs", [P, P])
        vT = sb("vT", [P, V_ROWS])
        cond = sb("cond", [P, KD, 32])
        modT = sb("modT", [P, 2, 48])
        gain1 = sb("gain1", [P, 2, KD])
        gain2 = sb("gain2", [P, 2, KD])
        g1_rows = sb("g1_rows", [P, 2, D])
        bs_sb = sb("bs_sb", [P, 2, P])
        wsT = sb("wsT", [P, 4, P])
        share = sb("share", [P, 512])
        ws_raw = share[:].rearrange("p (h q) -> p h q", h=4)
        wkv = share[:].rearrange("p (k c f) -> p k c f", k=2, c=2)
        w_pool_sb = sb("w_pool_sb", [P, 2, P])
        w_r = sb("w_r", [P, KD, NE])
        rt = sb("rt", [P, 2, 512])
        mod_rows = rt[:, 0, :]
        w_rot = sb("w_rot", [P, KD, ROPE])
        stat = sb("stat", [P, 48])
        top_idx = sb("top_idx", [NE, CAP], U32)
        pick_s = sb("pick_s", [P, NE], U32)
        pick_p = sb("pick_p", [P, NE], U32)
        idx_g = [sb(f"idx_g{s}", [P, 1], U32) for s in range(2)]
        idx_gp = [sb(f"idx_gp{s}", [P, 1], U32) for s in range(2)]
        idx_s = sb("idx_s", [P, 1], U32)
        idx_sp = sb("idx_sp", [P, 1], U32)
        ss_x, rs_x, rx = stat[:, 0:9], stat[:, 9:18], stat[:, 18:27]
        a_max, a_neg, a_sum, a_rec = (stat[:, 28 + 4 * s:32 + 4 * s] for s in range(4))
        ss2, rs2 = stat[:, 44:46], stat[:, 46:48]

        x2_dram = nc.dram_tensor("x2_rows", [T, D], F32, kind="Internal").ap()
        xn_dram = nc.dram_tensor("xn_rows", [T, D], F32, kind="Internal").ap()

        def tok_rows(sample, prompt, t):
            return sample[0, t * P:(t + 1) * P, :] if t < NT - 1 else prompt[0]

        const_in, vecs_in, ws_in, bs_in = sem("const_in"), sem("vecs_in"), sem("ws_in"), sem("bs_in")
        brows_in, wpool_in, w_r_in = sem("brows_in"), sem("wpool_in"), sem("w_r_in")
        x_in = [sem(f"x_in{t}") for t in range(NT)]
        ada_in = [sem(f"ada_in{s}") for s in range(RING)]
        w_in_in = [sem(f"w_in_in{s}") for s in range(3)]
        inv_in, rope_in = sem("inv_in"), sem("rope_in")
        mod_h_d, mod_h_a = sem("mod_h_d"), sem("mod_h_a")
        cleared, pool_cleared = sem("cleared"), sem("pool_cleared")
        ada_mm, job_mm = sem("ada_mm"), sem("job_mm")
        out_d, out_a = sem("out_d"), sem("out_a")
        cond_ok, gain_ok = sem("cond_ok"), sem("gain_ok")
        ssx_ok, var_ok, sqrt_ok, rx_ok, xn_ok = (sem(s) for s in ("ssx_ok", "var_ok", "sqrt_ok", "rx_ok", "xn_ok"))
        wrot_ok, sq_ok, nvar_ok, nsqrt_ok = (sem(s) for s in (
            "wrot_ok", "sq_ok", "nvar_ok", "nsqrt_ok"))
        dve_step, raw_used = sem("dve_step"), sem("raw_used")
        pool_step, diff_ok = sem("pool_step"), sem("diff_ok")
        cache_in, new_st = sem("cache_in"), sem("new_st")
        crope_zero = sem("crope_zero")
        w_out_in = sem("w_out_in")
        wq_in, wkv_in, wq_ok = sem("wq_in"), sem("wkv_in"), sem("wq_ok")
        proj_mm, q_out, k_out, v_out = sem("proj_mm"), sem("q_out"), sem("k_out"), sem("v_out")
        s_mm, max_ok, neg_ok, exp_ok, rec_ok, norm_ok = (sem(s) for s in (
            "s_mm", "max_ok", "neg_ok", "exp_ok", "rec_ok", "norm_ok"))
        t_mm, t_out, pv_mm, pv_out = (sem(s) for s in ("t_mm", "t_out", "pv_mm", "pv_out"))
        xa_in = [sem(f"xa_in{s}") for s in range(2)]
        x2_st = [sem(f"x2_st{s}") for s in range(2)]
        xn_st = [sem(f"xn_st{s}") for s in range(2)]
        o_mm, o_out, x2_ok, ss2_ok, var2_ok, sqrt2_ok, rec2_ok, x2n_ok = (sem(s) for s in (
            "o_mm", "o_out", "x2_ok", "ss2_ok", "var2_ok", "sqrt2_ok", "rec2_ok", "x2n_ok"))
        h2_mm, h2_out_a, h2_out_d, lg_mm, lg_out = (sem(s) for s in (
            "h2_mm", "h2_out_a", "h2_out_d", "lg_mm", "lg_out"))
        r_mm, r_step, r_exp = sem("r_mm"), sem("r_step"), sem("r_exp")
        w1_in = [sem(f"w1_in{s}") for s in range(2)]
        w3_in = [sem(f"w3_in{s}") for s in range(2)]
        w2_in = [sem(f"w2_in{s}") for s in range(2)]
        idx_ok, sidx_ok = sem("idx_ok"), sem("sidx_ok")
        rows_in = [sem(f"rows_in{s}") for s in range(2)]
        rows_p_in = [sem(f"rows_p_in{s}") for s in range(2)]
        h_mm, silu_ok, hid_ok, y_mm, y_out, tr_mm, tr_out = (sem(s) for s in (
            "h_mm", "silu_ok", "hid_ok", "y_mm", "y_out", "tr_mm", "tr_out"))
        added, added_p = sem("added"), sem("added_p")
        fin_in = [sem(f"fin_in{t}") for t in range(NT)]
        fin_st = sem("fin_st")
        frow_in = sem("frow_in")
        fss_ok, fvar_ok, fsqrt_ok, frec_ok, fin_ok = (sem(s) for s in (
            "fss_ok", "fvar_ok", "fsqrt_ok", "frec_ok", "fin_ok"))

        def evicted(eng, n):
            eng.wait_ge(out_d if JOBS[n][-1] == "D" else out_a, OUT[n])

        def computed(eng, n):
            if JOBS[n][0] == "ada":
                eng.wait_ge(ada_mm, (JOBS[n][1] + 1) * KD)
            else:
                eng.wait_ge(job_mm, sum(j[0] != "ada" for j in JOBS[:n + 1]))

        block = ctx.enter_context(nc.Block())

        @block.sync
        def _(sp):
            sp.dma_start(const[:], eye_ones).then_inc(const_in, 16)
            for row, src, n in ((V_N1, norm1_g[0], 8), (V_N2, norm2_g[0], 8), (V_C, c[0], 8), (V_C + 8, c_ctx, 8),
                                (V_PS, pool_scale[0], 2), (V_QN, q_norm_g[0], 3), (V_KN, kv_norm_g[0], 2)):
                sp.dma_start(vecs[row:row + n, :], src.rearrange("(n p) -> n p", p=P)).then_inc(vecs_in, 16)
            sp.dma_start(ws_raw, w_s[0].rearrange("h p q -> p h q")).then_inc(ws_in, 16)
            for t in range(NT):
                sp.dma_start(x_sb[:, t, :], tok_rows(x_sample, x_prompt, t)).then_inc(x_in[t], 16)

            def ada_chunk(n):
                r, k = divmod(n, KD)
                if n >= RING:
                    sp.wait_ge(ada_mm, n - RING + 1)
                sp.dma_start(ada_ring[n % RING],
                             w_ada[0, k * P:(k + 1) * P, r * 2048:(r + 1) * 2048]).then_inc(ada_in[n % RING], 16)
            for n in range(6):
                ada_chunk(n)
            sp.wait_ge(cleared, 1)
            for r in range(3):
                for g in range(4):
                    at = r * 2048 + g * 512
                    sp.dma_start(b_rows[32 * g:32 * g + 2, r, :],
                                 b_ada[0:1, at:at + 512].to_broadcast([2, 512])).then_inc(brows_in, 16)
            for n in range(6, 8):
                ada_chunk(n)
            for s, (a, z) in enumerate(((OFF_V, OFF_P), (0, OFF_V), (OFF_P, COLS))):
                sp.dma_start(w_in_sb[:, :, a:z],
                             w_in[0, :, a:z].rearrange("(k p) f -> p k f", p=P)).then_inc(w_in_in[s], 16)
            for h in range(4):
                j = h % 2
                sp.dma_start(bs_sb[64 * j:64 * j + 64, h // 2, :],
                             b_s[0, h:h + 1, :].to_broadcast([64, P])).then_inc(bs_in, 16)
                sp.dma_start(w_pool_sb[64 * j:64 * j + 64, h // 2, 64 * j:64 * j + 64],
                             w_pool[0, h]).then_inc(wpool_in, 16)
            sp.dma_start(w_r[:], w_router[0].rearrange("(k p) e -> p k e", p=P)).then_inc(w_r_in, 16)
            for n in range(8, 24):
                ada_chunk(n)
            evicted(sp, NUM[("h", 2, KD - 1)])
            evicted(sp, NUM[("h", 2, KD - 2)])
            sp.dma_start(inv_sb, inv_count.rearrange("p (m f) -> p m f", m=2)).then_inc(inv_in, 16)
            sp.wait_ge(ada_mm, 24)
            sp.dma_start(q_mul, q_rope).then_inc(rope_in, 16)
            sp.dma_start(kr_mul, k_rope).then_inc(rope_in, 16)
            computed(sp, NUM[("kr", 2)])
            for s in range(2):
                sp.dma_start(cache_c[:, s, :], cache_ckv[0, 0, s * P:(s + 1) * P, :]).then_inc(cache_in, 16)
            sp.wait_ge(crope_zero, 1)
            for s in range(2):
                for at in (64, 96):
                    sp.dma_start(cache_r[:, s, at:at + ROPE],
                                 cache_krope[0, 0, s * P:(s + 1) * P, :]).then_inc(cache_in, 16)

            def head_weights(i):
                sp.dma_start(wq_raw, w_qb[0, :, i * 2 * QK:(i + 1) * 2 * QK].rearrange(
                    "(k p) f -> p k f", p=P)).then_inc(wq_in, 16)
                for k in range(2):
                    for part in range(2):
                        src = w_kvb[0, k * P:(k + 1) * P, i * 2 * P:(i + 1) * 2 * P]
                        src = src.rearrange("p (j c e) -> p j c e", j=2, c=2)[:, :, part, :]
                        sp.dma_start(wkv[:, k, part, :].rearrange("p (j e) -> p j e", j=2), src).then_inc(wkv_in, 16)
            head_weights(0)
            computed(sp, NUM[("pool", 1, 2)])
            sp.dma_start(w_out_sb, w_out[0].rearrange("(k p) f -> p k f", p=P)).then_inc(w_out_in, 16)
            for t in range(2):
                sp.dma_start(x_again[t], tok_rows(x_sample, x_prompt, t)).then_inc(xa_in[t], 16)
            evicted(sp, NUM[("new",)])
            sp.dma_start(new_ckv[0, 0], new_out[:, 0:KVL]).then_inc(new_st, 16)
            sp.dma_start(new_krope[0, 0], new_out[:, KVL:KVL + ROPE]).then_inc(new_st, 16)
            for i in range(1, 4):
                sp.wait_ge(wq_ok, i)
                sp.wait_ge(proj_mm, i * 12)
                head_weights(i)
            sp.wait_ge(pv_mm, 4 * NT)
            sp.wait_ge(new_st, 32)
            for s in range(2):
                sp.dma_start(w1[s], w_e1[0, 0, :, s * 512:(s + 1) * 512].rearrange(
                    "(k p) f -> p k f", p=P)).then_inc(w1_in[s], 16)
            for t in range(NT):
                s = t % 2
                sp.wait_ge(x2_ok, t + 1)
                sp.dma_start(x2_dram[t * P:(t + 1) * P, :], x2[s]).then_inc(x2_st[s], 16)
                if t + 2 < NT:
                    sp.dma_start(x_again[s], tok_rows(x_sample, x_prompt, t + 2)).then_inc(xa_in[s], 16)
                sp.wait_ge(x2n_ok, t + 1)
                sp.dma_start(xn_dram[t * P:(t + 1) * P, :], x2n[s]).then_inc(xn_st[s], 16)
            sp.wait_ge(o_mm, 2 * NT)
            for s in range(2):
                sp.dma_start(w3[s], w_e3[0, 0, :, s * 512:(s + 1) * 512].rearrange(
                    "(k p) f -> p k f", p=P)).then_inc(w3_in[s], 16)
            for s in range(2):
                sp.wait_ge(x2_st[s], 16 * (5 - s))
                sp.wait_ge(xn_st[s], 16 * (5 - s))
            sp.wait_ge(h2_mm, 2 * NT)
            for s in range(2):
                sp.dma_start(w2[s], w_e2[0, 0, s * 512:(s + 1) * 512, :].rearrange(
                    "(k p) f -> p k f", p=P)).then_inc(w2_in[s], 16)
            sp.wait_ge(lg_mm, 3)
            sp.dma_start(final_row, final_norm_g.rearrange("(a d) -> a d", a=1).to_broadcast([P, D])).then_inc(frow_in, 16)
            with sp.Fori(0, NE - 1) as e:
                for s in range(2):
                    sp.wait_ge(h_mm, e * 16 + 8 * s + 8)
                    sp.dma_start(w1[s], w_e1[0, bass.ds(e + 1, 1), :, s * 512:(s + 1) * 512].rearrange(
                        "e (k p) f -> p (e k) f", p=P)).then_inc(w1_in[s], 16)
                    sp.dma_start(w3[s], w_e3[0, bass.ds(e + 1, 1), :, s * 512:(s + 1) * 512].rearrange(
                        "e (k p) f -> p (e k) f", p=P)).then_inc(w3_in[s], 16)
                sp.wait_ge(y_mm, e * 8 + 8)
                for s in range(2):
                    sp.dma_start(w2[s], w_e2[0, bass.ds(e + 1, 1), s * 512:(s + 1) * 512, :].rearrange(
                        "e (k p) f -> p (e k) f", p=P)).then_inc(w2_in[s], 16)
            sp.wait_ge(added, 16 * NE)
            sp.wait_ge(added_p, 16 * NE)
            for t in range(NT):
                sp.dma_start(x_fin[t], x2_dram[t * P:(t + 1) * P, :]).then_inc(fin_in[t], 16)
            for t in range(NT):
                sp.wait_ge(fin_ok, t + 1)
                sp.dma_start(tok_rows(y_sample, y_prompt, t), x_fin[t]).then_inc(fin_st, 16)
            sp.wait_ge(fin_st, 16 * NT)

        @block.tensor
        def _(pe):
            def project(n, w_at, m, g):
                g0, gn = GROUPS[g]
                for k in range(KD):
                    mm = pe.matmul(bank[n % 8][:, 0:gn], w_in_sb[:, k, w_at + m * P:w_at + (m + 1) * P],
                                   hT[:, k, g0:g0 + gn], start=(k == 0), stop=(k == KD - 1))
                return mm

            for n, job in enumerate(JOBS):
                kind = job[0]
                o = bank[n % 8]
                if n >= 8:
                    evicted(pe, n - 8)
                if kind == "vecs":
                    pe.wait_ge(const_in, 16)
                    pe.wait_ge(vecs_in, 16 * 7)
                    mm = pe.transpose(o[:, 0:V_ROWS], vecs[0:V_ROWS, :], ident[0:V_ROWS, 0:V_ROWS])
                elif kind == "w_s":
                    pe.wait_ge(ws_in, 16)
                    for h in range(4):
                        mm = pe.transpose(o[:, h * P:(h + 1) * P], ws_raw[:, h, :], ident)
                elif kind == "ada":
                    r = job[1]
                    pe.wait_ge(cond_ok, 1)
                    for k in range(KD):
                        ch = r * KD + k
                        pe.wait_ge(ada_in[ch % RING], 16 * (ch // RING + 1))
                        for g in range(4):
                            mm = pe.matmul(o[32 * g:32 * g + 32, :], cond[:, k, :],
                                           ada_ring[ch % RING][:, g * 512:(g + 1) * 512],
                                           start=(k == 0), stop=(k == KD - 1))
                        mm.then_inc(ada_mm, 1)
                elif kind == "mod":
                    evicted(pe, NUM[("ada", job[1])])
                    for j in range(4):
                        mm = pe.transpose(o[:, j * P:(j + 1) * P], mod_rows[:, j * P:(j + 1) * P], ident)
                elif kind == "g1":
                    cnd, hf = job[1], job[2]
                    row = 32 * hf + cnd
                    mm = pe.matmul(o, ident[:, row:row + 1].to_broadcast([P, P]), mod_rows,
                                   start=True, stop=True)
                elif kind == "h":
                    g, k = job[1], job[2]
                    if k == 0:
                        pe.wait_ge(xn_ok, GTILES[g][-1] + 1)
                    for a, t in enumerate(GTILES[g]):
                        mm = pe.transpose(o[:, a * P:(a + 1) * P], x_sb[:, t, k * P:(k + 1) * P], ident)
                elif kind == "va":
                    t = job[1]
                    if t == 0:
                        pe.wait_ge(w_in_in[0], 16)
                        pe.wait_ge(mod_h_d, 1)
                        pe.wait_ge(mod_h_a, 1)
                    for k in range(KD):
                        mm = pe.matmul(o[:, 0:256], hT[:, k, t * P:(t + 1) * P], w_in_sb[:, k, OFF_V:OFF_P],
                                       start=(k == 0), stop=(k == KD - 1))
                elif kind == "u":
                    pe.wait_ge(w_in_in[1], 16)
                    mm = project(n, 0, job[1], job[2])
                elif kind == "pin":
                    pe.wait_ge(w_in_in[2], 16)
                    mm = project(n, OFF_P, job[1], job[2])
                elif kind == "ckv":
                    mm = project(n, OFF_CKV, job[1], job[2])
                elif kind == "cq":
                    mm = project(n, OFF_CQ, job[1], job[2])
                elif kind in ("sskv", "ssq"):
                    g = job[1]
                    gn = GROUPS[g][1]
                    parts = 2 if kind == "sskv" else 3
                    base = (2 * g if kind == "sskv" else 6 + 3 * g)
                    for m in range(parts):
                        pe.wait_ge(sq_ok, base + m + 1)
                        mm = pe.matmul(o[:, 0:gn], ones, sq[:, (base + m) % 4, 0:gn],
                                       start=(m == 0), stop=(m == parts - 1))
                        if m < parts - 1:
                            mm.then_inc(raw_used, 1)
                elif kind == "kr":
                    g0, gn = GROUPS[job[1]]
                    pe.wait_ge(wrot_ok, 1)
                    for k in range(KD):
                        for q in range(4):
                            w_k = w_rot[:, k, :] if q < 2 else w_in_sb[:, k, OFF_KR:COLS]
                            mm = pe.matmul(o[32 * q:32 * q + 32, 0:gn], w_k, hT[:, k, g0:g0 + gn],
                                           start=(k == 0), stop=(k == KD - 1))
                elif kind == "gate":
                    m, g = job[1], job[2]
                    if (m, g) == (0, 0):
                        evicted(pe, NUM[("w_s",)])
                        evicted(pe, NUM[("va", NT - 1)])
                    for a, t in enumerate(GTILES[g]):
                        for j in range(2):
                            h = 2 * m + j
                            mm = pe.matmul(o[64 * j:64 * j + 64, a * P:(a + 1) * P], va[:, t, h * 64:(h + 1) * 64],
                                           wsT[:, h, :], start=True, stop=True)
                elif kind == "pool":
                    m, g = job[1], job[2]
                    pe.wait_ge(wpool_in, 16 * 4)
                    pe.wait_ge(diff_ok, 2)
                    gn, at = GROUPS[g][1], FLAT_AT[g]
                    mm = pe.matmul(o[:, 0:gn], w_pool_sb[:, m, :], win_sum[2 * m][:, at:at + gn],
                                   start=True, stop=True)
                elif kind == "cache_c":
                    pe.wait_ge(cache_in, 16 * 6)
                    for k in range(2):
                        for s in range(2):
                            mm = pe.transpose(o[:, (2 * k + s) * P:(2 * k + s + 1) * P],
                                              cache_c[:, s, k * P:(k + 1) * P], ident)
                elif kind == "cache_r":
                    for s in range(2):
                        mm = pe.transpose(o[:, s * P:(s + 1) * P], cache_r[:, s, :], ident)
                elif kind == "new":
                    evicted(pe, NUM[("sskv", 2)])
                    for k in range(2):
                        pe.transpose(o[:, k * P:(k + 1) * P], ckvT[:, k, KEYS:ALLK], ident)
                    evicted(pe, NUM[("kr", 2)])
                    mm = pe.transpose(o[:, KVL:KVL + NOPE], kT[64:128, 0, KEYS:ALLK], ident[64:128, 64:128])
                if kind != "ada":
                    mm.then_inc(job_mm, 1)

            last = len(JOBS) - 1
            for n in range(last - 7, last + 1):
                evicted(pe, n)
            def queries(i, x):
                j, g = divmod(x, 3)
                g0, gn = GROUPS[g]
                if x == 0:
                    pe.wait_ge(wq_ok, i + 1)
                if x >= 4 and not (isinstance(i, int) and i == 0):
                    pe.wait_ge(exp_ok, i * 18 - 5 + x)
                for k in range(3):
                    mm = pe.matmul(bank[Q_BANK[x]][:, 0:gn], wq[:, k, j, :], cqT[:, k, g0:g0 + gn],
                                   start=(k == 0), stop=(k == 2))
                mm.then_inc(proj_mm, 1)

            def values(i, g):
                pe.wait_ge(q_out, i * 6 + (4, 6, 6)[g])
                if g == 2:
                    pe.wait_ge(k_out, i * 3 + 3)
                for a in range(V_TILES[g]):
                    kt = 4 * g + a
                    for k in range(2):
                        mm = pe.matmul(bank[V_BANK[g]][:, a * P:(a + 1) * P], ckvT[:, k, kt * P:(kt + 1) * P],
                                       wkv[:, k, 1, :], start=(k == 0), stop=(k == 1))
                mm.then_inc(proj_mm, 1)

            def score(i, n, ch):
                t, j = divmod(n, 2)
                if n == 0:
                    pe.wait_ge(k_out, i * 3 + ch + 1)
                if n == 1 and ch < 2:
                    pe.wait_ge(v_out, i * 3 + 2 + ch)
                if n >= 2 and ch == 0:
                    pe.wait_ge(exp_ok, i * 18 + n - 1)
                if t < NT - 1:
                    k0, kn = ((0, 512), (512, 512), (1024, 256))[ch]
                else:
                    k0, kn = KEYS, NPR
                mm = pe.matmul(bank[3 * (n % 2) + ch][:, 0:kn], qT[:, j, t * P:(t + 1) * P], kT[:, j, k0:k0 + kn],
                               start=True, stop=True)
                if ch == 2 or t == NT - 1:
                    mm.then_inc(s_mm, 1)

            def keys_values(i):
                pe.wait_ge(wkv_in, i * 64 + 64)
                for g, (k0, kn) in enumerate(K_GROUPS):
                    pe.wait_ge(q_out, i * 6 + g + 1)
                    for k in range(2):
                        mm = pe.matmul(bank[Q_BANK[g]][:, 0:kn], wkv[:, k, 0, :], ckvT[:, k, k0:k0 + kn],
                                       start=(k == 0), stop=(k == 1))
                    mm.then_inc(proj_mm, 1)
                values(i, 0)
                pe.wait_ge(q_out, i * 6 + 5)
                for ch in range(3):
                    score(i, 0, ch)
                values(i, 1)
                values(i, 2)

            def attend(i, fill):
                def turn(n, ch):
                    if ch == 0:
                        pe.wait_ge(norm_ok, i * 18 + n + 1)
                    if (n, ch) != (0, 0):
                        pe.wait_ge(t_out, i * 50 + turns_before(n, ch))
                    for a in range(CHUNK_TILES[ch] if n < 16 else 1):
                        kt = 4 * ch + a
                        mm = pe.transpose(bank[6][:, a * P:(a + 1) * P], prob[n % 2][:, kt * P:(kt + 1) * P], ident)
                    mm.then_inc(t_mm, 1)

                def weigh(t, half):
                    if t < NT - 1:
                        pe.wait_ge(t_out, i * 50 + turns_before(2 * t + 1, 1 + half) + 1)
                        tiles = range(5 * half, 5 * half + 5)
                    else:
                        pe.wait_ge(t_out, i * 50 + 50)
                        tiles = range(10, 11)
                    if t > 0 and half == 0:
                        pe.wait_ge(pv_out, i * NT + t)
                    for kt in tiles:
                        for j in range(2):
                            src = kt if t < NT - 1 else 0
                            mm = pe.matmul(bank[7][64 * j:64 * j + 64, 0:P], v_sb[:, kt, 64 * j:64 * j + 64],
                                           probT[:, 2 * (t % 2) + j, src * P:(src + 1) * P],
                                           start=(kt in (0, 10)), stop=(kt in (9, 10)))
                    if kt >= 9:
                        mm.then_inc(pv_mm, 1)

                for n in range(1, 16):
                    score(i, n, 0)
                    if n >= 2:
                        turn(n - 2, 0)
                    score(i, n, 1)
                    if n >= 2:
                        turn(n - 2, 1)
                    if n >= 4:
                        weigh((n - 4) // 2, n % 2)
                    score(i, n, 2)
                    if n >= 2:
                        turn(n - 2, 2)
                for n in (16, 17):
                    score(i, n, 0)
                    turn(n - 2, 0)
                    weigh(6, n % 2)
                    turn(n - 2, 1)
                    fill(n - 16)
                    turn(n - 2, 2)
                for n in (16, 17):
                    turn(n, 0)
                    weigh(7, n % 2)
                    fill(n - 14)
                weigh(8, 0)
                fill(4)
                fill(5)

            def out_proj(x):
                t, hf = divmod(x, 2)
                if x == 0:
                    pe.wait_ge(w_out_in, 16)
                    evicted(pe, NUM[("pool", 1, 2)])
                if hf == 0:
                    pe.wait_ge(pv_out, 3 * NT + t + 1)
                if x >= 4:
                    pe.wait_ge(o_out, x - 3)
                elif x >= 2:
                    pe.wait_ge(exp_ok, 69 + x)
                for k in range(KD):
                    mm = pe.matmul(bank[O_BANK[x % 4]], mixT[:, k, t * P:(t + 1) * P],
                                   w_out_sb[:, k, hf * 512:(hf + 1) * 512], start=(k == 0), stop=(k == KD - 1))
                mm.then_inc(o_mm, 1)

            for x in range(6):
                queries(0, x)
            keys_values(0)
            with pe.Fori(0, 3) as i:
                attend(i, lambda x: queries(i + 1, x))
                keys_values(i + 1)
            attend(3, lambda x: out_proj(x) if x < 4 else None)

            def h2_turn(t):
                pe.wait_ge(x2n_ok, t + 1)
                for hf in range(2):
                    if t >= 1:
                        pe.wait_ge(h2_out_d if hf else h2_out_a, t)
                    for a in range(4):
                        kk = 4 * hf + a
                        mm = pe.transpose(bank[4 + hf][:, a * P:(a + 1) * P], x2n[t % 2][:, kk * P:(kk + 1) * P], ident)
                    mm.then_inc(h2_mm, 1)

            def logits(g):
                g0, gn = GROUPS[g]
                pe.wait_ge(h2_out_a, GTILES[g][-1] + 1)
                pe.wait_ge(h2_out_d, GTILES[g][-1] + 1)
                if g:
                    pe.wait_ge(lg_out, g)
                else:
                    pe.wait_ge(w_r_in, 16)
                    pe.wait_ge(t_out, 4 * 50)
                for k in range(KD):
                    mm = pe.matmul(bank[6][0:NE, 0:gn], w_r[:, k, :], h2T[:, k, g0:g0 + gn],
                                   start=(k == 0), stop=(k == KD - 1))
                mm.then_inc(lg_mm, 1)

            for t in range(2, NT):
                out_proj(2 * t)
                if t == 3:
                    h2_turn(1)
                out_proj(2 * t + 1)
                h2_turn(0 if t == 2 else t - 1)
                if t == 5:
                    logits(0)
            h2_turn(NT - 1)
            logits(1)
            logits(2)

            pe.wait_ge(lg_out, 3)
            for t in range(NT):
                mm = pe.transpose(bank[7][:, t * NE:(t + 1) * NE], aff[0:NE, t * P:(t + 1) * P], ident[0:NE, 0:NE])
            mm.then_inc(r_mm, 1)
            pe.wait_ge(r_step, R_PROB)
            for t in range(NT):
                mm = pe.transpose(bank[t // 4][0:NE, (t % 4) * P:(t % 4 + 1) * P], prob_e[:, t, :], ident)
            mm.then_inc(r_mm, 1)
            pe.wait_ge(r_step, R_TOP)
            pe.transpose(bank[4][:, 0:NE], top_val[0:NE, 0:CAPS], ident[0:NE, 0:NE])
            pe.transpose(bank[4][:, NE:2 * NE], top_idx_f[0:NE, 0:CAPS], ident[0:NE, 0:NE])
            pe.transpose(bank[4][0:CAPP, 2 * NE:3 * NE], top_val[0:NE, CAPS:CAP], ident[0:NE, 0:NE])
            pe.transpose(bank[4][0:CAPP, 3 * NE:4 * NE], top_idx_f[0:NE, CAPS:CAP],
                         ident[0:NE, 0:NE]).then_inc(r_mm, 1)

            def gathered(half, b, k, q, first=False):
                if k == 0:
                    pe.wait_ge(rows_in[b], half * 16 + 16)
                    pe.wait_ge(rows_p_in[b], half * 16 + 16)
                if not (first and k < 2):
                    pe.wait_ge(tr_out, q - 1)
                o = bank[6 + k % 2]
                pe.transpose(o[:, 0:CAPS], x_rows[b][:, k * P:(k + 1) * P], ident)
                pe.transpose(o[:, CAPS:CAP], x_rows_p[b][0:CAPP, k * P:(k + 1) * P],
                             ident[0:CAPP, 0:CAPP]).then_inc(tr_mm, 1)

            def back(e, k, q):
                if k == 0:
                    pe.wait_ge(y_out, e * 8 + 8)
                pe.wait_ge(tr_out, q - 1)
                o = bank[6 + k % 2]
                pe.transpose(o[:, 0:P], yT[:, k, 0:CAPS], ident)
                pe.transpose(o[0:CAPP, P:2 * P], yT[:, k, CAPS:CAP], ident).then_inc(tr_mm, 1)

            def expert(half, b, first=False, final=False):
                e = half * 2 + b
                for f in range(8):
                    s = f // 4
                    if f % 4 == 0:
                        pe.wait_ge(w1_in[s], e * 16 + 16)
                        pe.wait_ge(w3_in[s], e * 16 + 16)
                    for w, o, freed in ((w1, bank[f % 2], silu_ok), (w3, bank[2 + f % 2], hid_ok)):
                        if not (first and f < 2):
                            pe.wait_ge(freed, e * 8 + f - 1)
                        for k in range(KD):
                            if f == 0 and w is w1 and k in (0, KD - 1):
                                pe.wait_ge(tr_out, e * 16 + (8 if first else 0) - (k == 0))
                            mm = pe.matmul(o[:, 0:CAP], w[s][:, k, (f % 4) * P:(f % 4 + 1) * P], xsT[b][:, k, :],
                                           start=(k == 0), stop=(k == KD - 1))
                        mm.then_inc(h_mm, 1)
                    if not first:
                        back(e - 1, f, e * 16 + f)
                for dm in range(8):
                    if not (first and dm < 2):
                        pe.wait_ge(y_out, e * 8 + dm - 1)
                    for f in range(8):
                        if dm == 0 and f % 4 == 0:
                            pe.wait_ge(w2_in[f // 4], e * 16 + 16)
                        if dm == 0 and f in (0, 7):
                            pe.wait_ge(hid_ok, e * 8 + 7 + f // 7)
                        mm = pe.matmul(bank[4 + dm % 2][:, 0:CAP], w2[f // 4][:, f % 4, dm * P:(dm + 1) * P],
                                       hidT[:, f, :], start=(f == 0), stop=(f == 7))
                    mm.then_inc(y_mm, 1)
                    if not final:
                        gathered(half + b, 1 - b, dm, e * 16 + 8 + dm)

            pe.wait_ge(r_step, R_PICK)
            for k in range(KD):
                gathered(0, 0, k, k, first=True)
            expert(0, 0, first=True)
            with pe.Fori(0, NE // 2 - 1) as i2:
                expert(i2, 1)
                expert(i2 + 1, 0)
            expert(NE // 2 - 1, 1, final=True)
            for k in range(KD):
                back(NE - 1, k, NE * 16 - 8 + k)

        @block.scalar
        def _(act):
            act.wait_ge(cleared, 1)
            act.wait_ge(out_d, 1)
            for cnd in range(2):
                a = act.activation(cond[:, :, cnd], vT[:, V_C + 8 * cnd:V_C + 8 * cnd + 8], ACT.Silu)
            a.then_inc(cond_ok, 1)
            for t in range(NT):
                act.wait_ge(x_in[t], 16)
                a = act.activation(hreg[:, t * D:(t + 1) * D], x_sb[:, t, :], ACT.Square, accum_out=ss_x[:, t:t + 1])
                if t in (3, 7, 8):
                    a.then_inc(ssx_ok, 1)
            act.wait_ge(var_ok, 1)
            act.activation(rs_x, rs_x, ACT.Sqrt).then_inc(sqrt_ok, 1)
            squares = 0
            for n, job in enumerate(JOBS):
                kind = job[0]
                o = bank[n % 8]
                if kind in ("ckv", "cq"):
                    g0, gn = GROUPS[job[2]]
                    src = ckvT if kind == "ckv" else cqT
                    at = g0 if job[2] < 2 or kind == "cq" else KEYS
                    evicted(act, n)
                    if squares >= 4:
                        m = squares - 4
                        if m in LAST_SQ:
                            computed(act, NUM[LAST_SQ[m]])
                        else:
                            act.wait_ge(raw_used, 1 + sum(x not in LAST_SQ for x in range(m)))
                    act.activation(sq[:, squares % 4, 0:gn], src[:, job[1], at:at + gn], ACT.Square).then_inc(sq_ok, 1)
                    squares += 1
                if kind in ("sskv", "ssq"):
                    gn = GROUPS[job[1]][1]
                    m = job[1] + (3 if kind == "ssq" else 0)
                    act.wait_ge(nvar_ok, m + 1)
                    act.activation(rt[:, m % 2, 0:gn], rt[:, m % 2, 0:gn], ACT.Sqrt).then_inc(nsqrt_ok, 1)
                if job[-1] != "A":
                    continue
                if kind != "va":
                    computed(act, n)
                if kind == "h":
                    g, k = job[1], job[2]
                    g0, gn = GROUPS[g]
                    a = act.activation(hT[:, k, g0:g0 + gn], o[:, 0:gn], ACT.Copy)
                elif kind == "va":
                    if job[1] == 0:
                        act.wait_ge(gain_ok, 1)
                        evicted(act, NUM[("h", 2, KD - 1)])
                        for k in range(1, KD, 2):
                            for cnd, (x, z) in enumerate(((0, NS), (NS, T))):
                                a = act.activation(hT[:, k, x:z], hT[:, k, x:z], ACT.Identity,
                                                   bias=modT[:, cnd, k:k + 1], scale=gain1[:, cnd, k:k + 1])
                        a.then_inc(mod_h_a, 1)
                    computed(act, n)
                    a = act.activation(va[:, job[1], :], o[:, 0:256], ACT.Gelu_apprx_tanh)
                elif kind == "u":
                    g0, gn = GROUPS[job[2]]
                    a = act.activation(mixT[:, job[1], g0:g0 + gn], o[:, 0:gn], ACT.Gelu_apprx_tanh)
                elif kind == "pool":
                    g0, gn = GROUPS[job[2]]
                    a = act.activation(mixT[:, 2 + job[1], g0:g0 + gn], o[:, 0:gn], ACT.Copy,
                                       scale=vT[:, V_PS + job[1]:V_PS + job[1] + 1])
                a.then_inc(out_a, 1)

            def keys_out(i):
                for g, (k0, kn) in enumerate(K_GROUPS):
                    act.wait_ge(proj_mm, i * 12 + 7 + g)
                    o = bank[Q_BANK[g]]
                    act.activation(kT[0:64, 0, k0:k0 + kn], o[0:64, 0:kn], ACT.Copy)
                    act.activation(kT[0:64, 1, k0:k0 + kn], o[64:128, 0:kn], ACT.Copy).then_inc(k_out, 1)

            def attend(i):
                def turned(n, ch):
                    t, j = divmod(n, 2)
                    act.wait_ge(t_mm, i * 50 + turns_before(n, ch) + 1)
                    w = CHUNK_TILES[ch] * P if n < 16 else P
                    act.activation(probT[:, 2 * (t % 2) + j, ch * 512:ch * 512 + w], bank[6][:, 0:w],
                                   ACT.Copy).then_inc(t_out, 1)

                for n in range(18):
                    if n >= 2:
                        turned(n - 2, 2)
                    if 1 <= n <= 16:
                        turned(n - 1, 0)
                    act.wait_ge(neg_ok, i * 18 + n + 1)
                    if n >= 2:
                        act.wait_ge(t_mm, i * 50 + 3 * (n - 1))
                    w = KEYS if n < 16 else NPR
                    s = 3 * (n % 2)
                    src = ps[:, s:s + 3, :].rearrange("p b f -> p (b f)")[:, 0:w]
                    act.activation(prob[n % 2][:, 0:w], src, ACT.Exp, bias=a_neg[:, n % 4:n % 4 + 1], scale=SCALE,
                                   accum_out=a_sum[:, n % 4:n % 4 + 1]).then_inc(exp_ok, 1)
                    if 1 <= n <= 16:
                        turned(n - 1, 1)
                turned(16, 0)
                turned(17, 0)

            keys_out(0)
            with act.Fori(0, 3) as i:
                attend(i)
                keys_out(i + 1)
            attend(3)

            def h2_evict(t):
                act.wait_ge(h2_mm, 2 * t + 1)
                cnd = t // 8
                for a in range(4):
                    ins = act.activation(h2T[:, a, t * P:(t + 1) * P], bank[4][:, a * P:(a + 1) * P], ACT.Identity,
                                         bias=modT[:, cnd, 24 + a:25 + a], scale=gain2[:, cnd, a:a + 1])
                ins.then_inc(h2_out_a, 1)

            act.wait_ge(gain_ok, 2)
            for t in range(NT):
                act.wait_ge(x2_ok, t + 1)
                if t >= 2:
                    act.wait_ge(xn_st[t % 2], 16 * (t // 2))
                    act.wait_ge(h2_mm, 2 * (t - 1))
                act.activation(x2n[t % 2], x2[t % 2], ACT.Square, accum_out=ss2[:, t % 2:t % 2 + 1]).then_inc(ss2_ok, 1)
                act.wait_ge(var2_ok, t + 1)
                act.activation(rs2[:, t % 2:t % 2 + 1], ss2[:, t % 2:t % 2 + 1], ACT.Sqrt).then_inc(sqrt2_ok, 1)
                if t >= 1:
                    h2_evict(t - 1)
            h2_evict(NT - 1)

            act.wait_ge(r_step, R_SHIFT)
            act.activation(prob_e, logit, ACT.Exp).then_inc(r_exp, 1)

            def expert(e, first=False):
                for f in range(8):
                    act.wait_ge(h_mm, e * 16 + 2 * f + 1)
                    if not (first and f < 2):
                        act.wait_ge(hid_ok, e * 8 + f - 1)
                    act.activation(silu_h[:, f % 2, :], bank[f % 2][:, 0:CAP], ACT.Silu).then_inc(silu_ok, 1)
                for dm in range(8):
                    act.wait_ge(y_mm, e * 8 + dm + 1)
                    for cnd, (a, z) in enumerate(((0, CAPS), (CAPS, CAP))):
                        ins = act.activation(yT[:, dm, a:z], bank[4 + dm % 2][:, a:z], ACT.Copy,
                                             scale=modT[:, cnd, 40 + dm:41 + dm])
                    ins.then_inc(y_out, 1)

            expert(0, first=True)
            with act.Fori(1, NE) as e:
                expert(e)

            for t in range(NT + 1):
                if t < NT:
                    act.wait_ge(fin_in[t], 16)
                    if t >= 2:
                        act.wait_ge(fss_ok, t - 1)
                    act.activation(fin_squares[t % 2], x_fin[t], ACT.Square, accum_out=ss_x[:, t:t + 1]).then_inc(fss_ok, 1)
                if t > 0:
                    act.wait_ge(fvar_ok, t)
                    act.activation(rs_x[:, t - 1:t], rs_x[:, t - 1:t], ACT.Sqrt).then_inc(fsqrt_ok, 1)

        @block.vector
        def _(dve):
            steps = [0]

            def then(ins):
                steps[0] += 1
                ins.then_inc(dve_step, 1)
                dve.wait_ge(dve_step, steps[0])

            dve.memset(cond[:], 0.0)
            dve.memset(w_pool_sb[:], 0.0)
            dve.memset(b_rows, 0.0).then_inc(cleared, 1)

            def fold_wq(i):
                dve.wait_ge(wq_in, i * 16 + 16)
                for k in range(3):
                    g = vT[:, V_QN + k:V_QN + k + 1]
                    raw = wq_raw[:, k, :].rearrange("p (j f) -> p j f", j=2)
                    dve.tensor_scalar(wq[:, k, :, 0:QK], raw, g, None, ALU.mult)
                    src = raw[:, :, NOPE:QK].rearrange("p j (b s e) -> p j b s e", b=2, s=2)
                    dst = wq[:, k, :, QK:P].rearrange("p j (b s e) -> p j b s e", b=2, s=2)
                    for s in range(2):
                        ins = dve.tensor_scalar(dst[:, :, :, s, :], src[:, :, :, 1 - s, :], g, None, ALU.mult)
                ins.then_inc(wq_ok, 1)

            normed = 0
            for n, job in enumerate(JOBS):
                kind = job[0]
                o = bank[n % 8]
                if job[-1] != "D":
                    continue
                if kind == "cache_c":
                    fold_wq(0)
                computed(dve, n)
                if kind == "vecs":
                    dve.tensor_copy(vT[:], o[:, 0:V_ROWS]).then_inc(out_d, 1)
                elif kind == "w_s":
                    dve.tensor_copy(wsT[:].rearrange("p h q -> p (h q)"), o).then_inc(out_d, 1)
                    dve.wait_ge(ssx_ok, 3)
                    dve.tensor_scalar(rs_x, ss_x, 1.0 / D, EPS, ALU.mult, ALU.add).then_inc(var_ok, 1)
                    dve.wait_ge(sqrt_ok, 1)
                    dve.reciprocal(rx, rs_x).then_inc(rx_ok, 1)
                    dve.wait_ge(rx_ok, 1)
                    for t in range(NT):
                        dve.tensor_scalar(x_sb[:, t, :], x_sb[:, t, :], rx[:, t:t + 1], None,
                                          ALU.mult).then_inc(xn_ok, 1)
                elif kind == "ada":
                    r = job[1]
                    if r == 0:
                        dve.wait_ge(brows_in, 16 * 12)
                    dve.tensor_tensor(mod_rows, o, b_rows[:, r, :], ALU.add).then_inc(out_d, 1)
                elif kind == "mod":
                    r = job[1]
                    v = o.rearrange("p (j g c) -> p g j c", j=4, g=4)
                    for cnd in range(2):
                        ins = dve.tensor_copy(modT[:, cnd, 16 * r:16 * r + 16].rearrange("p (g j) -> p g j", g=4),
                                              v[:, :, :, cnd])
                    ins.then_inc(out_d, 1)
                    if r in (0, 2):
                        evicted(dve, n)
                        gain, at, vn = (gain1, 8, V_N1) if r == 0 else (gain2, 32, V_N2)
                        for cnd in range(2):
                            ins = dve.scalar_tensor_tensor(out=gain[:, cnd, :], in0=modT[:, cnd, at:at + 8], scalar=1.0,
                                                           in1=vT[:, vn:vn + 8], op0=ALU.add, op1=ALU.mult)
                        ins.then_inc(gain_ok, 1)
                    if r == 0:
                        dve.wait_ge(gain_ok, 1)
                        evicted(dve, NUM[("h", 2, KD - 2)])
                        for k in range(0, KD, 2):
                            for cnd, (x, z) in enumerate(((0, NS), (NS, T))):
                                ins = dve.tensor_scalar(hT[:, k, x:z], hT[:, k, x:z], gain1[:, cnd, k:k + 1],
                                                        modT[:, cnd, k:k + 1], ALU.mult, ALU.add)
                        ins.then_inc(mod_h_d, 1)
                elif kind == "g1":
                    dve.tensor_copy(g1_rows[:, job[1], job[2] * 512:job[2] * 512 + 512], o).then_inc(out_d, 1)
                elif kind == "h":
                    g, k = job[1], job[2]
                    g0, gn = GROUPS[g]
                    dve.tensor_copy(hT[:, k, g0:g0 + gn], o[:, 0:gn]).then_inc(out_d, 1)
                elif kind == "pin":
                    m, g = job[1], job[2]
                    gn = GROUPS[g][1]
                    if (m, g) == (0, 0):
                        dve.wait_ge(pool_cleared, 1)
                        dve.wait_ge(w_in_in[2], 16)
                        src = w_in_sb[:, :, OFF_KR:COLS].rearrange("p k (b s e) -> p k b s e", b=2, s=2)
                        dst = w_rot[:].rearrange("p k (b s e) -> p k b s e", b=2, s=2)
                        for s in range(2):
                            ins = dve.tensor_copy(dst[:, :, :, s, :], src[:, :, :, 1 - s, :])
                        ins.then_inc(wrot_ok, 1)
                    dve.tensor_copy(pin[:, m, FLAT_AT[g]:FLAT_AT[g] + gn], o[:, 0:gn]).then_inc(out_d, 1)
                elif kind == "ckv":
                    g0, gn = GROUPS[job[2]]
                    at = g0 if job[2] < 2 else KEYS
                    dve.tensor_copy(ckvT[:, job[1], at:at + gn], o[:, 0:gn]).then_inc(out_d, 1)
                elif kind == "cq":
                    g0, gn = GROUPS[job[2]]
                    dve.tensor_copy(cqT[:, job[1], g0:g0 + gn], o[:, 0:gn]).then_inc(out_d, 1)
                elif kind in ("sskv", "ssq"):
                    g = job[1]
                    g0, gn = GROUPS[g]
                    width = KVL if kind == "sskv" else QL
                    evicted(dve, max(x for x in range(n) if JOBS[x][-1] == "D"))
                    r = rt[:, normed % 2, 0:gn]
                    dve.tensor_scalar(r, o[:, 0:gn], 1.0 / width, EPS, ALU.mult, ALU.add).then_inc(nvar_ok, 1)
                    dve.wait_ge(nvar_ok, normed + 1)
                    dve.wait_ge(nsqrt_ok, normed + 1)
                    then(dve.reciprocal(r, r))
                    normed += 1
                    if kind == "sskv":
                        at = g0 if g < 2 else KEYS
                        for m in range(2):
                            ins = dve.scalar_tensor_tensor(out=ckvT[:, m, at:at + gn], in0=ckvT[:, m, at:at + gn],
                                                           scalar=vT[:, V_KN + m:V_KN + m + 1], in1=r,
                                                           op0=ALU.mult, op1=ALU.mult)
                        ins.then_inc(out_d, 1)
                    else:
                        dve.wait_ge(rope_in, 32)
                        dve.tensor_tensor(q_mul[:, g0:g0 + gn], q_mul[:, g0:g0 + gn], r, ALU.mult).then_inc(out_d, 1)
                elif kind == "kr":
                    g0, gn = GROUPS[job[1]]
                    at = g0 if job[1] < 2 else KEYS
                    if job[1] == 0:
                        computed(dve, NUM[("kr", 2)])
                    evicted(dve, n - 1)
                    tmp = rt[64:128, 0, 0:gn]
                    main = rt[64:128, 1, 0:gn]
                    dve.tensor_tensor(tmp, o[0:64, 0:gn], kr_mul[0:64, g0:g0 + gn], ALU.mult)
                    then(dve.tensor_tensor(main, o[64:128, 0:gn], kr_mul[64:128, g0:g0 + gn], ALU.mult))
                    dve.tensor_tensor(kT[64:128, 0, at:at + gn], tmp, main, ALU.add)
                    dve.tensor_tensor(kT[64:128, 1, at:at + gn], tmp, main, ALU.add).then_inc(out_d, 1)
                elif kind == "gate":
                    m, g = job[1], job[2]
                    g0, gn = GROUPS[g]
                    if (m, g) == (0, 0):
                        dve.wait_ge(bs_in, 16 * 4)
                        evicted(dve, NUM[("u", 1, 2)])
                    a = gn // P
                    tmp = sq[:, n % 4, 0:gn]
                    then(dve.tensor_tensor(tmp.rearrange("p (a q) -> p a q", a=a),
                                           o[:, 0:gn].rearrange("p (a q) -> p a q", a=a),
                                           bs_sb[:, m:m + 1, :].to_broadcast([P, a, P]), ALU.add))
                    dve.tensor_tensor(mixT[:, m, g0:g0 + gn], mixT[:, m, g0:g0 + gn], tmp, ALU.mult).then_inc(out_d, 1)
                elif kind == "cache_c":
                    dve.tensor_copy(ckvT[:, :, NS:KEYS], o.rearrange("p (k s) -> p k s", k=2)).then_inc(out_d, 1)
                elif kind == "cache_r":
                    dve.tensor_copy(kT[64:128, 0, NS:KEYS], o[64:128, 0:PAST])
                    dve.tensor_copy(kT[64:128, 1, NS:KEYS], o[64:128, 0:PAST]).then_inc(out_d, 1)
                elif kind == "new":
                    dve.tensor_copy(new_out, o[:, 0:KVL + NOPE]).then_inc(out_d, 1)

            evicted(dve, max(n for n in range(len(JOBS)) if JOBS[n][-1] == "D"))
            def queries_out(i, x):
                j, g = divmod(x, 3)
                g0, gn = GROUPS[g]
                dve.wait_ge(proj_mm, i * 12 + x + 1)
                dve.tensor_tensor(qT[:, j, g0:g0 + gn], bank[Q_BANK[x]][:, 0:gn], q_mul[:, g0:g0 + gn],
                                  ALU.mult).then_inc(q_out, 1)

            def values_out(i, g):
                dve.wait_ge(proj_mm, i * 12 + 10 + g)
                w = V_TILES[g]
                dve.tensor_copy(v_sb[:, 4 * g:4 * g + w, :].rearrange("p a f -> p (a f)"),
                                bank[V_BANK[g]][:, 0:w * P]).then_inc(v_out, 1)

            def highest(i, n):
                w = KEYS if n < 16 else NPR
                s = 3 * (n % 2)
                r = n % 4
                src = ps[:, s:s + 3, :].rearrange("p b f -> p (b f)")[:, 0:w]
                dve.wait_ge(s_mm, i * 18 + n + 1)
                dve.tensor_reduce(a_max[:, r:r + 1], src, AX_X, ALU.max).then_inc(max_ok, 1)
                dve.wait_ge(max_ok, i * 18 + n + 1)
                dve.tensor_scalar(a_neg[:, r:r + 1], a_max[:, r:r + 1], -SCALE, None, ALU.mult).then_inc(neg_ok, 1)

            def keys_values(i):
                values_out(i, 0)
                highest(i, 0)
                values_out(i, 1)
                values_out(i, 2)

            def attend(i, more):
                def weighed(t):
                    dve.wait_ge(pv_mm, i * NT + t + 1)
                    dve.tensor_copy(mreg[:, bass.ds(i * T + 4 * T + t * P, P)], bank[7][:, 0:P]).then_inc(pv_out, 1)

                for n in range(18):
                    w = KEYS if n < 16 else NPR
                    r = n % 4
                    if n > 0:
                        highest(i, n)
                    if n % 2 and n >= 5:
                        weighed((n - 5) // 2)
                    dve.wait_ge(exp_ok, i * 18 + n + 1)
                    dve.reciprocal(a_rec[:, r:r + 1], a_sum[:, r:r + 1]).then_inc(rec_ok, 1)
                    dve.wait_ge(rec_ok, i * 18 + n + 1)
                    dve.tensor_scalar(prob[n % 2][:, 0:w], prob[n % 2][:, 0:w], a_rec[:, r:r + 1], None,
                                      ALU.mult).then_inc(norm_ok, 1)
                    if more and n == 8:
                        fold_wq(i + 1)
                for x in range(6):
                    if more:
                        queries_out(i + 1, x)
                    if x in (1, 3):
                        weighed(7 + x // 2)

            for x in range(6):
                queries_out(0, x)
            keys_values(0)
            with dve.Fori(0, 3) as i:
                attend(i, True)
                keys_values(i + 1)
            attend(3, False)

            def h2_evict(t):
                dve.wait_ge(h2_mm, 2 * t + 2)
                cnd = t // 8
                for a in range(4):
                    kk = 4 + a
                    ins = dve.tensor_scalar(h2T[:, kk, t * P:(t + 1) * P], bank[5][:, a * P:(a + 1) * P],
                                            gain2[:, cnd, kk:kk + 1], modT[:, cnd, 24 + kk:25 + kk], ALU.mult, ALU.add)
                ins.then_inc(h2_out_d, 1)

            def logits_out(g):
                g0, gn = GROUPS[g]
                dve.wait_ge(lg_mm, g + 1)
                dve.tensor_copy(aff[0:NE, g0:g0 + gn], bank[6][0:NE, 0:gn]).then_inc(lg_out, 1)

            dve.wait_ge(gain_ok, 2)
            for t in range(NT):
                s, cnd = t % 2, t // 8
                if t >= 2:
                    dve.wait_ge(x2_st[s], 16 * (t // 2))
                    dve.wait_ge(ss2_ok, t - 1)
                for hf in range(2):
                    x = 2 * t + hf
                    dve.wait_ge(o_mm, x + 1)
                    dve.tensor_tensor(x2[s][:, hf * 512:(hf + 1) * 512], bank[O_BANK[x % 4]],
                                      g1_rows[:, cnd, hf * 512:(hf + 1) * 512], ALU.mult).then_inc(o_out, 1)
                dve.wait_ge(o_out, 2 * t + 2)
                dve.wait_ge(xa_in[s], 16 * (t // 2 + 1))
                dve.tensor_tensor(x2[s], x2[s], x_again[s], ALU.add).then_inc(x2_ok, 1)
                dve.wait_ge(ss2_ok, t + 1)
                dve.tensor_scalar(ss2[:, s:s + 1], ss2[:, s:s + 1], 1.0 / D, EPS, ALU.mult, ALU.add).then_inc(var2_ok, 1)
                dve.wait_ge(sqrt2_ok, t + 1)
                dve.reciprocal(rs2[:, s:s + 1], rs2[:, s:s + 1]).then_inc(rec2_ok, 1)
                dve.wait_ge(rec2_ok, t + 1)
                dve.tensor_scalar(x2n[s], x2[s], rs2[:, s:s + 1], None, ALU.mult).then_inc(x2n_ok, 1)
                if t >= 1:
                    h2_evict(t - 1)
                if t == 5:
                    logits_out(0)
            h2_evict(NT - 1)
            logits_out(1)
            logits_out(2)

            done = [0]

            def routed(ins):
                done[0] += 1
                ins.then_inc(r_step, 1)
                dve.wait_ge(r_step, done[0])

            dve.wait_ge(r_mm, 1)
            routed(dve.tensor_copy(logit.rearrange("p t e -> p (t e)"), bank[7][:, 0:NT * NE]))
            routed(dve.tensor_reduce(r_stat[:, 0, :], logit, AX_X, ALU.max))
            routed(dve.tensor_tensor(logit, logit, r_stat[:, 0, :].unsqueeze(2).to_broadcast([P, NT, NE]), ALU.subtract))
            assert done[0] == R_SHIFT
            dve.wait_ge(r_exp, 1)
            routed(dve.tensor_reduce(r_stat[:, 1, :], prob_e, AX_X, ALU.add))
            routed(dve.reciprocal(r_stat[:, 2, :], r_stat[:, 1, :]))
            routed(dve.tensor_tensor(prob_e, prob_e, r_stat[:, 2, :].unsqueeze(2).to_broadcast([P, NT, NE]), ALU.mult))
            assert done[0] == R_PROB
            dve.wait_ge(r_mm, 2)
            routed(dve.tensor_copy(aff[0:NE, :], ps[0:NE, 0:3, :].rearrange("p b f -> p (b f)")[:, 0:T]))
            for cnd, (a, z, at, cap) in enumerate(((0, NS, 0, CAPS), (NS, T, CAPS, CAPP))):
                for r in range(cap // 8):
                    v = top_val[0:NE, at + 8 * r:at + 8 * r + 8]
                    routed(dve.max(v, aff[0:NE, a:z]))
                    dve.max_index(top_idx[:, at + 8 * r:at + 8 * r + 8], v, aff[0:NE, a:z])
                    routed(dve.match_replace(aff[0:NE, a:z], v, aff[0:NE, a:z], -1.0))
            routed(dve.tensor_copy(top_idx_f[0:NE, :], top_idx[:]))
            routed(dve.tensor_scalar(top_idx_f[0:NE, CAPS:CAP], top_idx_f[0:NE, CAPS:CAP], float(NS), None, ALU.add))
            assert done[0] == R_TOP
            dve.wait_ge(r_mm, 3)
            dve.tensor_copy(picked[:, 0, :], bank[4][:, 0:NE])
            dve.tensor_copy(picked[0:CAPP, 2, :], bank[4][0:CAPP, 2 * NE:3 * NE])
            dve.tensor_copy(pick_s[:], bank[4][:, NE:2 * NE])
            routed(dve.tensor_copy(pick_p[0:CAPP, :], bank[4][0:CAPP, 3 * NE:4 * NE]))
            assert done[0] == R_PICK

            def gathered(b, k, q):
                dve.wait_ge(tr_mm, q + 1)
                for cnd, (a, z) in enumerate(((0, CAPS), (CAPS, CAP))):
                    ins = dve.tensor_scalar(xsT[b][:, k, a:z], bank[6 + k % 2][:, a:z], gain2[:, cnd, k:k + 1],
                                            modT[:, cnd, 24 + k:25 + k], ALU.mult, ALU.add)
                ins.then_inc(tr_out, 1)

            def back(e, b, k, q, first=False):
                if k == 0 and not first:
                    dve.wait_ge(added, (e - 1) * 16)
                    dve.wait_ge(added_p, (e - 1) * 16)
                dve.wait_ge(tr_mm, q + 1)
                o = bank[6 + k % 2]
                dve.tensor_scalar(y_rows[b][:, k * P:(k + 1) * P], o[:, 0:P],
                                  creg[:, bass.ds(T + 612 + e, 1)], None, ALU.mult)
                dve.tensor_scalar(y_rows_p[b][0:CAPP, k * P:(k + 1) * P], o[0:CAPP, P:2 * P],
                                  creg[0:CAPP, bass.ds(T + 612 + 2 * NE + e, 1)], None, ALU.mult).then_inc(tr_out, 1)

            def expert(e, b, first=False, unscattered=False, final=False):
                for f in range(8):
                    dve.wait_ge(silu_ok, e * 8 + f + 1)
                    dve.wait_ge(h_mm, e * 16 + 2 * f + 2)
                    dve.tensor_tensor(hidT[:, f, :], bank[2 + f % 2][:, 0:CAP], silu_h[:, f % 2, :],
                                      ALU.mult).then_inc(hid_ok, 1)
                    if not first:
                        back(e - 1, 1 - b, f, e * 16 + f, first=unscattered)
                for dm in range(8):
                    if not final:
                        gathered(1 - b, dm, e * 16 + 8 + dm)

            for k in range(KD):
                gathered(0, k, k)
            expert(0, 0, first=True)
            expert(1, 1, unscattered=True)
            expert(2, 0, unscattered=True)
            with dve.Fori(1, NE // 2 - 1) as i2:
                expert(i2 * 2 + 1, 1)
                expert(i2 * 2 + 2, 0)
            expert(NE - 1, 1, final=True)
            for k in range(KD):
                back(NE - 1, 1, k, NE * 16 - 8 + k)

            dve.wait_ge(frow_in, 16)
            for t in range(NT + 1):
                if t < NT:
                    dve.wait_ge(fss_ok, t + 1)
                    dve.tensor_scalar(rs_x[:, t:t + 1], ss_x[:, t:t + 1], 1.0 / D, EPS, ALU.mult,
                                      ALU.add).then_inc(fvar_ok, 1)
                if t > 0:
                    dve.wait_ge(fsqrt_ok, t)
                    dve.reciprocal(rx[:, t - 1:t], rs_x[:, t - 1:t]).then_inc(frec_ok, 1)
                    dve.wait_ge(frec_ok, t)
                    dve.scalar_tensor_tensor(out=x_fin[t - 1], in0=x_fin[t - 1], scalar=rx[:, t - 1:t], in1=final_row,
                                             op0=ALU.mult, op1=ALU.mult).then_inc(fin_ok, 1)

        @block.gpsimd
        def _(pool):
            steps = [0]

            def then(ins):
                steps[0] += 1
                ins.then_inc(pool_step, 1)
                pool.wait_ge(pool_step, steps[0])

            pool.wait_ge(ada_mm, 24)
            pool.memset(pin, 0.0).then_inc(pool_cleared, 1)
            pool.wait_ge(inv_in, 16)
            for m in range(2):
                evicted(pool, NUM[("pin", m, 2)])
                p, a, b = pin[:, m, :], win_sum[2 * m], win_sum[2 * m + 1]
                then(pool.memset(b[:, 0:FLAT], 0.0))
                then(pool.memset(a[:, 0:FLAT], 0.0))
                then(pool.tensor_tensor(a[:, 1:FLAT], p[:, 1:FLAT], p[:, 0:FLAT - 1], ALU.add))
                lo = 64 if m == 0 else 0
                then(pool.tensor_tensor(b[lo:, 2:FLAT - 1], a[lo:, 1:FLAT - 2], a[lo:, 3:FLAT], ALU.add))
                if m == 1:
                    then(pool.tensor_tensor(a[:, 4:FLAT - 4], b[:, 2:FLAT - 6], b[:, 6:FLAT - 2], ALU.add))
                    then(pool.tensor_tensor(b[64:, 8:FLAT - 8], a[64:, 4:FLAT - 12], a[64:, 12:FLAT - 4], ALU.add))
                then(pool.tensor_tensor(a[0:64, :], a[0:64, :], inv_sb[0:64, m, :], ALU.mult))
                then(pool.tensor_tensor(a[64:, :], b[64:, :], inv_sb[64:, m, :], ALU.mult))
                pool.tensor_tensor(a, a, p, ALU.subtract).then_inc(diff_ok, 1)
            computed(pool, NUM[("kr", 2)])
            pool.memset(cache_r, 0.0).then_inc(crope_zero, 1)

            def gather(e, b, later=True):
                if later:
                    pool.wait_ge(h_mm, (e - 2) * 16 + 1)
                pool.tensor_copy(idx_g[b][:], pick_s[:, e:e + 1])
                pool.tensor_copy(idx_gp[b][0:CAPP, :], pick_p[0:CAPP, e:e + 1]).then_inc(idx_ok, 1)
                pool.wait_ge(idx_ok, e + 1)
                pool.indirect_dma_start(out=x_rows[b], out_offset=None, in_=xn_dram,
                                        in_offset=bass.IndirectOffsetOnAxis(ap=idx_g[b][:], axis=0)
                                        ).then_inc(rows_in[b], 16)
                pool.indirect_dma_start(out=x_rows_p[b][0:CAPP, :], out_offset=None, in_=xn_dram,
                                        in_offset=bass.IndirectOffsetOnAxis(ap=idx_gp[b][0:CAPP, :], axis=0)
                                        ).then_inc(rows_p_in[b], 16)

            def scatter(e, b, ready):
                pool.tensor_copy(idx_s[:], pick_s[:, e:e + 1])
                pool.tensor_copy(idx_sp[0:CAPP, :], pick_p[0:CAPP, e:e + 1]).then_inc(sidx_ok, 1)
                pool.wait_ge(sidx_ok, e + 1)
                pool.wait_ge(tr_out, ready)
                pool.indirect_dma_start(out=x2_dram, out_offset=bass.IndirectOffsetOnAxis(ap=idx_s[:], axis=0),
                                        in_=y_rows[b], in_offset=None, compute_op=ALU.add).then_inc(added, 16)
                pool.indirect_dma_start(out=x2_dram,
                                        out_offset=bass.IndirectOffsetOnAxis(ap=idx_sp[0:CAPP, :], axis=0),
                                        in_=y_rows_p[b][0:CAPP, :], in_offset=None,
                                        compute_op=ALU.add).then_inc(added_p, 16)
                pool.wait_ge(added, (e + 1) * 16)
                pool.wait_ge(added_p, (e + 1) * 16)

            pool.wait_ge(r_step, R_PICK)
            for s in range(2):
                pool.wait_ge(xn_st[s], 16 * (5 - s))
                pool.wait_ge(x2_st[s], 16 * (5 - s))
            gather(0, 0, later=False)
            gather(1, 1, later=False)
            for e in range(NE):
                if e + 2 < NE:
                    gather(e + 2, e % 2)
                scatter(e, e % 2, min(e * 16 + 24, NE * 16))


Q_BANK = (1, 2, 4, 5, 0, 3)
K_GROUPS = ((0, 512), (512, 512), (1024, 384))
V_BANK, V_TILES = (5, 3, 4), (4, 4, 3)
CHUNK_TILES = (4, 4, 2)
O_BANK = (1, 2, 0, 3)


def turns_before(n, ch):
    return 3 * n + ch if n < 16 else 32 + n


R_SHIFT, R_PROB = 3, 6
R_TOP = R_PROB + 1 + 2 * (CAP // 8) + 2
R_PICK = R_TOP + 1
LAST_SQ = {2 * g + 1: ("sskv", g) for g in range(3)} | {6 + 3 * g + 2: ("ssq", g) for g in range(3)}


_INS = ['x_prompt', 'x_sample', 'cache_ckv', 'cache_krope', 'c', 'c_ctx', 'w_ada', 'b_ada', 'norm1_g', 'norm2_g',
        'w_in', 'w_s', 'b_s', 'w_pool', 'pool_scale', 'q_norm_g', 'w_qb', 'kv_norm_g', 'w_kvb', 'w_out', 'w_router',
        'w_e1', 'w_e3', 'w_e2', 'final_norm_g']
_OUTS = [(1, NPR, D), (1, NS, D), (1, 1, NPR, KVL), (1, 1, NPR, ROPE)]


def kernel(**inputs):
    import concourse.bacc as _bacc
    from concourse.bass_utils import run_bass_kernel_spmd as _run

    nc = _bacc.Bacc("TRN2", target_bir_lowering=False, num_devices=1)
    arrays, args = {}, []
    for name, a in [(n, inputs[n]) for n in _INS] + list(tables().items()):
        a = np.ascontiguousarray(a)
        arrays[f"in_{name}_dram"] = a
        args.append(nc.dram_tensor(f"in_{name}_dram", a.shape, mybir.dt.from_np(a.dtype), kind="ExternalInput").ap())
    for i, shape in enumerate(_OUTS):
        args.append(nc.dram_tensor(f"out_{i}_dram", shape, F32, kind="ExternalOutput").ap())
    build(nc, *args)
    r = _run(nc, [arrays], core_ids=[0])
    return tuple(r.results[0][f"out_{i}_dram"] for i in range(len(_OUTS)))
```

```python
from contextlib import ExitStack

import numpy as np

import concourse.bass as bass
from concourse import mybir

ALU = mybir.AluOpType
ACT = mybir.ActivationFunctionType
F32 = mybir.dt.float32
U32 = mybir.dt.uint32
AX_X = mybir.AxisListType.X

P = 128
D = 1024
KD = D // P
NS, NPR = 1024, 128
T = NS + NPR
NT = T // P
GROUPS = [(0, 512), (512, 512), (1024, 128)]
GTILES = [range(0, 4), range(4, 8), range(8, 9)]
PAST = 256
KEYS = NS + PAST
ALLK = KEYS + NPR
NOPE, ROPE = 64, 32
QK = NOPE + ROPE
QL, KVL = 384, 256
SCALE = float(QK) ** -0.5
OFF_V, OFF_P, OFF_CQ, OFF_CKV, OFF_KR, COLS = 256, 512, 768, 1152, 1408, 1440
NE = 16
CAPS, CAPP = 2 * NS // NE, 2 * NPR // NE
CAP = CAPS + CAPP
PSLOTS = NE * CAPP
YPT = 5120
EPS = 1e-6
PAD = 8
FLAT = NS + NPR + 4 * PAD
FLAT_AT = [PAD, PAD + 512, NS + 3 * PAD]
RING = 6
R_TILES = (range(0, 4), range(4, 8), range(8, 9))
PICKED = T + 1124
V_N1, V_N2, V_C, V_PS, V_QN, V_KN, V_ROWS = 0, 8, 16, 32, 34, 37, 39


def tables():
    eye_ones = np.concatenate([np.eye(P), np.ones((P, P))], 1).astype(np.float32)
    inv = np.zeros((P, 2, FLAT), np.float32)
    for g, w in enumerate((2, 4, 8, 16)):
        left, right = w // 2, w - 1 - w // 2
        for n, at in ((NS, FLAT_AT[0]), (NPR, FLAT_AT[2])):
            t = np.arange(n)
            count = np.clip(t + right + 1, 0, n) - np.clip(t - left, 0, n)
            inv[64 * (g % 2):64 * (g % 2) + 64, g // 2, at:at + n] = 1.0 / count.astype(np.float32)
    axis = ROPE // 2
    freq = (1.0 / (10000.0 ** (np.arange(0, axis, 2, dtype=np.float32) / axis))).astype(np.float32)
    tok = np.arange(NS)
    pos = [(tok // 64).astype(np.float32), (tok % 64).astype(np.float32)]
    cos = np.ones((ROPE, T), np.float32)
    sin = np.zeros((ROPE, T), np.float32)
    for r in range(ROPE):
        ang = pos[r // axis] * freq[r % 8]
        cos[r, :NS] = np.cos(ang)
        sin[r, :NS] = np.sin(ang) * (-1.0 if r % axis < 8 else 1.0)
    q_rope = np.concatenate([np.ones((NOPE, T), np.float32), cos, sin])
    k_rope = np.concatenate([sin, sin, cos, cos])
    return {
        "eye_ones": eye_ones,
        "inv_count": inv.reshape(P, 2 * FLAT),
        "q_rope": q_rope,
        "k_rope": k_rope,
        "flip_count": np.concatenate([np.eye(P)[::-1], np.arange(P)[:, None]], 1).astype(np.float32),
    }


def plan_jobs():
    jobs = [("vecs", "D"), ("w_s", "D")]
    jobs += [("h", g, k, "DA"[k % 2]) for g in range(3) for k in range(KD)]
    jobs += [("ada", 0, "D"), ("mod", 0, "D")]
    jobs += [("va", t, "A") for t in range(NT)]
    jobs += [("u", 0, g, "A") for g in range(3)]
    jobs += [("ada", 1, "D"), ("u", 1, 0, "A"), ("mod", 1, "D")] + [("g1", c, hf, "D") for c in range(2) for hf in range(2)]
    jobs += [("u", 1, g, "A") for g in (1, 2)]
    pin = [("pin", m, g, "D") for m in range(2) for g in range(3)]
    jobs += [("ada", 2, "D"), pin[0], ("mod", 2, "D")] + pin[1:]
    latent = [("ckv", m, g, "D") for g in range(3) for m in range(2)]
    latent += [("cq", m, g, "D") for g in range(3) for m in range(3)] + [("kr", 0, "D")]
    gates = [("gate", m, g, "D") for m in range(2) for g in range(3)]
    for n, job in enumerate(latent):
        jobs.append(job)
        if n and latent[n - 1][:2] in (("ckv", 1), ("cq", 2)):
            jobs.append(("sskv" if latent[n - 1][0] == "ckv" else "ssq", latent[n - 1][2], "D"))
        if job[0] == "cq" and gates:
            jobs.append(gates.pop(0))
    jobs += [("kr", g, "D") for g in (1, 2)]
    jobs += [("pool", m, g, "A") for m in range(2) for g in range(3)]
    jobs += [("cache_c", "A"), ("cache_r", "A"), ("new", "A")]
    return jobs


def build(nc, x_prompt, x_sample, cache_ckv, cache_krope, c, c_ctx, w_ada, b_ada, norm1_g, norm2_g,
          w_in, w_s, b_s, w_pool, pool_scale, q_norm_g, w_qb, kv_norm_g, w_kvb, w_out, w_router,
          w_e1, w_e3, w_e2, final_norm_g, eye_ones, inv_count, q_rope, k_rope, flip_count,
          y_prompt, y_sample, new_ckv, new_krope):
    JOBS = plan_jobs()
    NUM = {j[:-1]: n for n, j in enumerate(JOBS)}
    OUT = [sum(j[-1] == JOBS[n][-1] for j in JOBS[:n + 1]) for n in range(len(JOBS))]

    ctx = ExitStack()
    with ctx:
        def sb(name, shape, dt=F32):
            return ctx.enter_context(nc.sbuf_tensor(name, shape, dt))

        def sem(name):
            return ctx.enter_context(nc.semaphore(name))

        ps = ctx.enter_context(nc.psum_tensor("ps", [P, 8, 512], F32))
        bank = [ps[:, b, :] for b in range(8)]

        wreg = sb("wreg", [P, 24576])
        hreg = sb("hreg", [P, 9216])
        mreg = sb("mreg", [P, 9216])
        creg = sb("creg", [P, 2 * ALLK])

        def view(region, at, *dims):
            n = int(np.prod(dims))
            v = region[:, at:at + n]
            if len(dims) == 2:
                return v.rearrange("p (a b) -> p a b", a=dims[0])
            if len(dims) == 3:
                return v.rearrange("p (a b c) -> p a b c", a=dims[0], b=dims[1])
            return v

        w_in_sb = view(wreg, 0, KD, COLS)
        ada_ring = [view(wreg, 11520 + s * 2048, 2048) for s in range(RING)]
        pin = view(wreg, 11520, 2, FLAT)
        win_sum = [view(wreg, 13888 + s * FLAT, FLAT) for s in range(4)]
        cqT = view(wreg, 18624, 3, T)
        q_mul = view(wreg, 22080, T)
        kr_mul = view(wreg, 23232, T)
        qT = view(wreg, 0, 2, T)
        kT = view(wreg, 2304, 2, ALLK)
        v_sb = view(wreg, 5120, 11, P)
        new_out = view(wreg, 6528, KVL + NOPE)
        cache_c = view(wreg, 6848, 2, KVL)
        cache_r = view(wreg, 7360, 2, P)
        w_out_sb = view(wreg, 8192, KD, D)
        x_again = [view(wreg, 16384 + s * D, D) for s in range(2)]
        x2 = [view(wreg, 18432 + s * D, D) for s in range(2)]
        x2n = [view(wreg, 20480 + s * D, D) for s in range(2)]
        w1 = [view(wreg, s * 4096, KD, 512) for s in range(2)]
        w3 = [view(wreg, 8192 + s * 4096, KD, 512) for s in range(2)]
        w2 = [view(wreg, 16384 + s * 4096, 4, D) for s in range(2)]
        x_fin = [view(wreg, (0, 8192)[t // 4] + t % 4 * D, D) for t in range(8)]
        p_fin = view(wreg, 12288, D)
        hT = view(hreg, 0, KD, T)
        prob = [view(hreg, s * KEYS, KEYS) for s in range(2)]
        probT = view(hreg, 2 * KEYS, 4, KEYS)
        wq_raw = view(hreg, 7680, 3, 2 * QK)
        wq = view(hreg, 8256, 3, 2, P)
        h2T = hT
        y_rows = [view(hreg, s * D, D) for s in range(2)]
        x2_p = view(hreg, 2048, D)
        pick_p = view(hreg, 3072, PSLOTS)
        pick_gate = view(hreg, 3328, PSLOTS)
        pick_gate_T = view(hreg, 3584, 2, P)
        diag_idx = view(hreg, 3840, PSLOTS)
        final_row = view(hreg, 4096, D)
        ypT = view(hreg, YPT, KD, PSLOTS)
        y_p = [view(hreg, 7168 + s * D, D) for s in range(2)]
        diag_gate = view(hreg, 7168, PSLOTS)
        x_sb = view(mreg, 0, NT, D)
        mixT = view(mreg, 0, KD, T)
        inv_sb = view(mreg, 2304, 2, FLAT)
        sq = view(mreg, 4864, 4, 512)
        va = view(mreg, 6912, NT, 256)
        x_rows = [view(mreg, s * D, D) for s in range(2)]
        xpT = view(mreg, 2048, KD, PSLOTS)
        xsT = [view(mreg, 4096 + s * KD * CAP, KD, CAP) for s in range(2)]
        yT = view(mreg, 6400, KD, CAPS)
        hidT = view(mreg, 7552, KD, CAP)
        silu_h = view(mreg, 8704, 2, CAP)
        fin_squares = [view(mreg, s * D, D) for s in range(2)]
        b_rows = view(creg, 0, 3, 512)
        ckvT = view(creg, 0, 2, ALLK)
        aff = view(creg, 0, T)
        logit = view(creg, T, NT, NE)
        prob_e = view(creg, T + 144, NT, NE)
        r_stat = view(creg, T + 288, 4, NT)
        merge_mask = view(creg, T, CAPS)
        merge_diff = view(creg, T + 144, CAPS)
        list_val = view(creg, T + 324, 2 * CAPS)
        list_idx_f = view(creg, T + 580, 2 * CAPS)
        top_val = view(creg, T + 836, CAP)
        top_idx_f = view(creg, T + 980, CAP)
        picked = view(creg, PICKED, NE)
        list_turned = view(creg, PICKED + 64, 2 * NE)
        flip_sb = view(creg, PICKED + 96, P + 1)
        const = sb("const", [P, 2 * P])
        ident, ones = const[:, 0:P], const[:, P:2 * P]
        vecs = sb("vecs", [P, P])
        vT = sb("vT", [P, V_ROWS])
        cond = sb("cond", [P, KD, 32])
        modT = sb("modT", [P, 2, 48])
        gain1 = sb("gain1", [P, 2, KD])
        gain2 = sb("gain2", [P, 2, KD])
        g1_rows = sb("g1_rows", [P, 2, D])
        bs_sb = sb("bs_sb", [P, 2, P])
        wsT = sb("wsT", [P, 4, P])
        share = sb("share", [P, 512])
        ws_raw = share[:].rearrange("p (h q) -> p h q", h=4)
        wkv = share[:].rearrange("p (k c f) -> p k c f", k=2, c=2)
        w_pool_sb = sb("w_pool_sb", [P, 2, P])
        w_r = sb("w_r", [P, KD, NE])
        rt = sb("rt", [P, 2, 512])
        mod_rows = rt[:, 0, :]
        w_rot = sb("w_rot", [P, KD, ROPE])
        stat = sb("stat", [P, 48])
        list_idx = sb("list_idx", [NE, CAPS + CAP], U32)
        pick_s = sb("pick_s", [P, NE], U32)
        idx_g = [sb(f"idx_g{s}", [P, 1], U32) for s in range(2)]
        idx_s = sb("idx_s", [P, 1], U32)
        ss_x, rs_x, rx = stat[:, 0:9], stat[:, 9:18], stat[:, 18:27]
        a_max, a_neg, a_sum, a_rec = (stat[:, 28 + 4 * s:32 + 4 * s] for s in range(4))
        ss2, rs2 = stat[:, 44:46], stat[:, 46:48]

        x2_dram = nc.dram_tensor("x2_rows", [NS, D], F32, kind="Internal").ap()
        xn_dram = nc.dram_tensor("xn_rows", [NS, D], F32, kind="Internal").ap()

        def tok_rows(sample, prompt, t):
            return sample[0, t * P:(t + 1) * P, :] if t < NT - 1 else prompt[0]

        const_in, vecs_in, ws_in, bs_in = sem("const_in"), sem("vecs_in"), sem("ws_in"), sem("bs_in")
        brows_in, wpool_in, w_r_in = sem("brows_in"), sem("wpool_in"), sem("w_r_in")
        x_in = [sem(f"x_in{t}") for t in range(NT)]
        ada_in = [sem(f"ada_in{s}") for s in range(RING)]
        w_in_in = [sem(f"w_in_in{s}") for s in range(3)]
        inv_in, rope_in = sem("inv_in"), sem("rope_in")
        mod_h_d, mod_h_a = sem("mod_h_d"), sem("mod_h_a")
        cleared, pool_cleared = sem("cleared"), sem("pool_cleared")
        ada_mm, job_mm = sem("ada_mm"), sem("job_mm")
        out_d, out_a = sem("out_d"), sem("out_a")
        cond_ok, gain_ok = sem("cond_ok"), sem("gain_ok")
        ssx_ok, var_ok, sqrt_ok, rx_ok, xn_ok = (sem(s) for s in ("ssx_ok", "var_ok", "sqrt_ok", "rx_ok", "xn_ok"))
        wrot_ok, sq_ok, nvar_ok, nsqrt_ok = (sem(s) for s in (
            "wrot_ok", "sq_ok", "nvar_ok", "nsqrt_ok"))
        dve_step, raw_used = sem("dve_step"), sem("raw_used")
        pool_step, diff_ok = sem("pool_step"), sem("diff_ok")
        cache_in, new_st = sem("cache_in"), sem("new_st")
        crope_zero = sem("crope_zero")
        w_out_in = sem("w_out_in")
        wq_in, wkv_in, wq_ok = sem("wq_in"), sem("wkv_in"), sem("wq_ok")
        proj_mm, q_out, k_out, v_out = sem("proj_mm"), sem("q_out"), sem("k_out"), sem("v_out")
        s_mm, max_ok, neg_ok, exp_ok, rec_ok, norm_ok = (sem(s) for s in (
            "s_mm", "max_ok", "neg_ok", "exp_ok", "rec_ok", "norm_ok"))
        t_mm, t_out, pv_mm, pv_out = (sem(s) for s in ("t_mm", "t_out", "pv_mm", "pv_out"))
        xa_in = [sem(f"xa_in{s}") for s in range(2)]
        x2_st = [sem(f"x2_st{s}") for s in range(2)]
        xn_st = [sem(f"xn_st{s}") for s in range(2)]
        o_mm, o_out, x2_ok, ss2_ok, var2_ok, sqrt2_ok, rec2_ok, x2n_ok = (sem(s) for s in (
            "o_mm", "o_out", "x2_ok", "ss2_ok", "var2_ok", "sqrt2_ok", "rec2_ok", "x2n_ok"))
        h2_mm, h2_out, lg_mm, lg_out = (sem(s) for s in ("h2_mm", "h2_out", "lg_mm", "lg_out"))
        tok_mm, shift_ok, r_exp, prob_ok, back_mm, aff_out = (sem(s) for s in (
            "tok_mm", "shift_ok", "r_exp", "prob_ok", "back_mm", "aff_out"))
        flip_in, list_ok, flip_mm, turned_ok, merged, picks_mm, picks_ok, r_step = (sem(s) for s in (
            "flip_in", "list_ok", "flip_mm", "turned_ok", "merged", "picks_mm", "picks_ok", "r_step"))
        diag_ok, row_mm, onehot_ok, xp_mm, xp_ok, turn_mm, pgt_ok, x2p_in = (sem(s) for s in (
            "diag_ok", "row_mm", "onehot_ok", "xp_mm", "xp_ok", "turn_mm", "pgt_ok", "x2p_in"))
        gated_ok = sem("gated_ok")
        xp_put, yp_mm, yp_out, prompt_mm, prompt_ok = (sem(s) for s in (
            "xp_put", "yp_mm", "yp_out", "prompt_mm", "prompt_ok"))
        w1_in = [sem(f"w1_in{s}") for s in range(2)]
        w3_in = [sem(f"w3_in{s}") for s in range(2)]
        w2_in = [sem(f"w2_in{s}") for s in range(2)]
        idx_ok, sidx_ok = sem("idx_ok"), sem("sidx_ok")
        rows_in = [sem(f"rows_in{s}") for s in range(2)]
        h_mm, silu_ok, hid_ok, y_mm, y_out, tr_mm, tr_out = (sem(s) for s in (
            "h_mm", "silu_ok", "hid_ok", "y_mm", "y_out", "tr_mm", "tr_out"))
        added = sem("added")
        fin_in = [sem(f"fin_in{t}") for t in range(NT - 1)]
        fin_st, frow_in, late_in, late_st, p_st = (sem(s) for s in ("fin_st", "frow_in", "late_in", "late_st", "p_st"))
        fss_ok, fvar_ok, fsqrt_ok, frec_ok, fin_ok = (sem(s) for s in (
            "fss_ok", "fvar_ok", "fsqrt_ok", "frec_ok", "fin_ok"))

        fin_sets = [(x_fin[t], ss_x[:, t:t + 1], rs_x[:, t:t + 1]) for t in range(8)]
        fin_sets += [(y_rows[1], ss2[:, 0:1], rs2[:, 0:1]), (p_fin, ss2[:, 1:2], rs2[:, 1:2])]
        LATE, PROMPT = 8, 9

        def evicted(eng, n):
            eng.wait_ge(out_d if JOBS[n][-1] == "D" else out_a, OUT[n])

        def computed(eng, n):
            if JOBS[n][0] == "ada":
                eng.wait_ge(ada_mm, (JOBS[n][1] + 1) * KD)
            else:
                eng.wait_ge(job_mm, sum(j[0] != "ada" for j in JOBS[:n + 1]))

        block = ctx.enter_context(nc.Block())

        @block.sync
        def _(sp):
            sp.dma_start(const[:], eye_ones).then_inc(const_in, 16)
            for row, src, n in ((V_N1, norm1_g[0], 8), (V_N2, norm2_g[0], 8), (V_C, c[0], 8), (V_C + 8, c_ctx, 8),
                                (V_PS, pool_scale[0], 2), (V_QN, q_norm_g[0], 3), (V_KN, kv_norm_g[0], 2)):
                sp.dma_start(vecs[row:row + n, :], src.rearrange("(n p) -> n p", p=P)).then_inc(vecs_in, 16)
            sp.dma_start(ws_raw, w_s[0].rearrange("h p q -> p h q")).then_inc(ws_in, 16)
            for t in range(NT):
                sp.dma_start(x_sb[:, t, :], tok_rows(x_sample, x_prompt, t)).then_inc(x_in[t], 16)

            def ada_chunk(n):
                r, k = divmod(n, KD)
                if n >= RING:
                    sp.wait_ge(ada_mm, n - RING + 1)
                sp.dma_start(ada_ring[n % RING],
                             w_ada[0, k * P:(k + 1) * P, r * 2048:(r + 1) * 2048]).then_inc(ada_in[n % RING], 16)
            for n in range(6):
                ada_chunk(n)
            sp.wait_ge(cleared, 1)
            for g in range(4):
                src = b_ada[0:1, :].rearrange("a (r g f) -> a g r f", r=3, g=4)[:, g, :, :]
                sp.dma_start(b_rows[32 * g:32 * g + 2, :, :], src.to_broadcast([2, 3, 512])).then_inc(brows_in, 16)
            for n in range(6, 8):
                ada_chunk(n)
            for s, (a, z) in enumerate(((OFF_V, OFF_P), (0, OFF_V), (OFF_P, COLS))):
                sp.dma_start(w_in_sb[:, :, a:z],
                             w_in[0, :, a:z].rearrange("(k p) f -> p k f", p=P)).then_inc(w_in_in[s], 16)
            for h in range(4):
                j = h % 2
                sp.dma_start(bs_sb[64 * j:64 * j + 64, h // 2, :],
                             b_s[0, h:h + 1, :].to_broadcast([64, P])).then_inc(bs_in, 16)
                sp.dma_start(w_pool_sb[64 * j:64 * j + 64, h // 2, 64 * j:64 * j + 64],
                             w_pool[0, h]).then_inc(wpool_in, 16)
            sp.dma_start(w_r[:], w_router[0].rearrange("(k p) e -> p k e", p=P)).then_inc(w_r_in, 16)
            for n in range(8, 24):
                ada_chunk(n)
            evicted(sp, NUM[("h", 2, KD - 1)])
            evicted(sp, NUM[("h", 2, KD - 2)])
            sp.dma_start(inv_sb, inv_count.rearrange("p (m f) -> p m f", m=2)).then_inc(inv_in, 16)
            sp.wait_ge(ada_mm, 24)
            sp.dma_start(q_mul, q_rope).then_inc(rope_in, 16)
            sp.dma_start(kr_mul, k_rope).then_inc(rope_in, 16)
            computed(sp, NUM[("kr", 2)])
            for s in range(2):
                sp.dma_start(cache_c[:, s, :], cache_ckv[0, 0, s * P:(s + 1) * P, :]).then_inc(cache_in, 16)
            sp.wait_ge(crope_zero, 1)
            for s in range(2):
                for at in (64, 96):
                    sp.dma_start(cache_r[:, s, at:at + ROPE],
                                 cache_krope[0, 0, s * P:(s + 1) * P, :]).then_inc(cache_in, 16)

            def head_weights(i):
                sp.dma_start(wq_raw, w_qb[0, :, i * 2 * QK:(i + 1) * 2 * QK].rearrange(
                    "(k p) f -> p k f", p=P)).then_inc(wq_in, 16)
                for k in range(2):
                    for part in range(2):
                        src = w_kvb[0, k * P:(k + 1) * P, i * 2 * P:(i + 1) * 2 * P]
                        src = src.rearrange("p (j c e) -> p j c e", j=2, c=2)[:, :, part, :]
                        sp.dma_start(wkv[:, k, part, :].rearrange("p (j e) -> p j e", j=2), src).then_inc(wkv_in, 16)
            evicted(sp, NUM[("gate", 1, 2)])
            head_weights(0)
            computed(sp, NUM[("pool", 1, 2)])
            sp.dma_start(w_out_sb, w_out[0].rearrange("(k p) f -> p k f", p=P)).then_inc(w_out_in, 16)
            for t in range(2):
                sp.dma_start(x_again[t], tok_rows(x_sample, x_prompt, t)).then_inc(xa_in[t], 16)
            evicted(sp, NUM[("new",)])
            sp.dma_start(new_ckv[0, 0], new_out[:, 0:KVL]).then_inc(new_st, 16)
            sp.dma_start(new_krope[0, 0], new_out[:, KVL:KVL + ROPE]).then_inc(new_st, 16)
            for i in range(1, 4):
                sp.wait_ge(wq_ok, i)
                sp.wait_ge(proj_mm, i * 12)
                head_weights(i)
            sp.wait_ge(proj_mm, 48)
            sp.dma_start(flip_sb, flip_count).then_inc(flip_in, 16)
            sp.wait_ge(pv_mm, 4 * NT)
            sp.wait_ge(new_st, 32)
            for s in range(2):
                sp.dma_start(w1[s], w_e1[0, 0, :, s * 512:(s + 1) * 512].rearrange(
                    "(k p) f -> p k f", p=P)).then_inc(w1_in[s], 16)
            for t in range(NT):
                s = t % 2
                sp.wait_ge(x2_ok, t + 1)
                if t < NT - 1:
                    sp.dma_start(x2_dram[t * P:(t + 1) * P, :], x2[s]).then_inc(x2_st[s], 16)
                if t + 2 < NT:
                    sp.dma_start(x_again[s], tok_rows(x_sample, x_prompt, t + 2)).then_inc(xa_in[s], 16)
                if t < NT - 1:
                    sp.wait_ge(x2n_ok, t + 1)
                    sp.dma_start(xn_dram[t * P:(t + 1) * P, :], x2n[s]).then_inc(xn_st[s], 16)
            sp.wait_ge(o_mm, 2 * NT)
            for s in range(2):
                sp.dma_start(w3[s], w_e3[0, 0, :, s * 512:(s + 1) * 512].rearrange(
                    "(k p) f -> p k f", p=P)).then_inc(w3_in[s], 16)
            sp.wait_ge(lg_mm, NT)
            sp.dma_start(x2_p, x2[0]).then_inc(x2p_in, 16)
            sp.dma_start(final_row, final_norm_g.rearrange("(a d) -> a d", a=1).to_broadcast([P, D])).then_inc(frow_in, 16)
            for s in range(2):
                sp.wait_ge(x2_st[s], 16 * 4)
                sp.wait_ge(xn_st[s], 16 * 4)
            sp.wait_ge(x2p_in, 16)
            sp.wait_ge(xp_mm, 4)
            for s in range(2):
                sp.wait_ge(rows_in[s], 16)
            for s in range(2):
                sp.dma_start(w2[s], w_e2[0, 0, s * 512:(s + 1) * 512, :].rearrange(
                    "(k p) f -> p k f", p=P)).then_inc(w2_in[s], 16)
            with sp.Fori(0, NE - 1) as e:
                for s in range(2):
                    sp.wait_ge(h_mm, e * 16 + 8 * s + 8)
                    sp.dma_start(w1[s], w_e1[0, bass.ds(e + 1, 1), :, s * 512:(s + 1) * 512].rearrange(
                        "e (k p) f -> p (e k) f", p=P)).then_inc(w1_in[s], 16)
                    sp.dma_start(w3[s], w_e3[0, bass.ds(e + 1, 1), :, s * 512:(s + 1) * 512].rearrange(
                        "e (k p) f -> p (e k) f", p=P)).then_inc(w3_in[s], 16)
                sp.wait_ge(y_mm, e * 8 + 8)
                for s in range(2):
                    sp.dma_start(w2[s], w_e2[0, bass.ds(e + 1, 1), s * 512:(s + 1) * 512, :].rearrange(
                        "e (k p) f -> p (e k) f", p=P)).then_inc(w2_in[s], 16)
            sp.wait_ge(h_mm, 16 * (NE - 1) + 8)
            sp.wait_ge(added, 16 * (NE - 1))
            for t in range(NT - 1):
                sp.dma_start(x_fin[t], x2_dram[t * P:(t + 1) * P, :]).then_inc(fin_in[t], 16)
            for t in range(NT - 1):
                sp.wait_ge(fin_ok, t + 1)
                sp.dma_start(y_sample[0, t * P:(t + 1) * P, :], x_fin[t]).then_inc(fin_st, 16)
            sp.wait_ge(fin_ok, PROMPT + 1)
            sp.dma_start(y_prompt[0], p_fin).then_inc(p_st, 16)
            sp.wait_ge(fin_st, 16 * (NT - 1))
            sp.wait_ge(p_st, 16)
            sp.wait_ge(late_st, 16)

        @block.tensor
        def _(pe):
            def project(n, w_at, m, g):
                g0, gn = GROUPS[g]
                for k in range(KD):
                    mm = pe.matmul(bank[n % 8][:, 0:gn], w_in_sb[:, k, w_at + m * P:w_at + (m + 1) * P],
                                   hT[:, k, g0:g0 + gn], start=(k == 0), stop=(k == KD - 1))
                return mm

            def ada_part(r, ks):
                o = bank[NUM[("ada", r)] % 8]
                pe.wait_ge(cond_ok, 1)
                for k in ks:
                    ch = r * KD + k
                    pe.wait_ge(ada_in[ch % RING], 16 * (ch // RING + 1))
                    for g in range(4):
                        mm = pe.matmul(o[32 * g:32 * g + 32, :], cond[:, k, :],
                                       ada_ring[ch % RING][:, g * 512:(g + 1) * 512],
                                       start=(k == 0), stop=(k == KD - 1))
                    mm.then_inc(ada_mm, 1)

            for n, job in enumerate(JOBS):
                kind = job[0]
                o = bank[n % 8]
                r = {("u", 0, 1): 1, ("u", 1, 1): 2}.get(job[:-1], 0)
                if r:
                    evicted(pe, NUM[("ada", r)] - 8)
                    ada_part(r, range(0, 4))
                if n >= 8:
                    evicted(pe, n - 8)
                if kind == "vecs":
                    pe.wait_ge(const_in, 16)
                    pe.wait_ge(vecs_in, 16 * 7)
                    mm = pe.transpose(o[:, 0:V_ROWS], vecs[0:V_ROWS, :], ident[0:V_ROWS, 0:V_ROWS])
                elif kind == "w_s":
                    pe.wait_ge(ws_in, 16)
                    for h in range(4):
                        mm = pe.transpose(o[:, h * P:(h + 1) * P], ws_raw[:, h, :], ident)
                elif kind == "ada":
                    ada_part(job[1], range(4 if job[1] else 0, KD))
                elif kind == "mod":
                    evicted(pe, NUM[("ada", job[1])])
                    for j in range(4):
                        mm = pe.transpose(o[:, j * P:(j + 1) * P], mod_rows[:, j * P:(j + 1) * P], ident)
                elif kind == "g1":
                    cnd, hf = job[1], job[2]
                    row = 32 * hf + cnd
                    mm = pe.matmul(o, ident[:, row:row + 1].to_broadcast([P, P]), mod_rows,
                                   start=True, stop=True)
                elif kind == "h":
                    g, k = job[1], job[2]
                    if k == 0:
                        pe.wait_ge(xn_ok, GTILES[g][-1] + 1)
                    for a, t in enumerate(GTILES[g]):
                        mm = pe.transpose(o[:, a * P:(a + 1) * P], x_sb[:, t, k * P:(k + 1) * P], ident)
                elif kind == "va":
                    t = job[1]
                    if t == 0:
                        pe.wait_ge(w_in_in[0], 16)
                    if t % 4 == 0:
                        pe.wait_ge(mod_h_d, t // 4 + 1)
                        pe.wait_ge(mod_h_a, t // 4 + 1)
                    for k in range(KD):
                        mm = pe.matmul(o[:, 0:256], hT[:, k, t * P:(t + 1) * P], w_in_sb[:, k, OFF_V:OFF_P],
                                       start=(k == 0), stop=(k == KD - 1))
                elif kind == "u":
                    pe.wait_ge(w_in_in[1], 16)
                    mm = project(n, 0, job[1], job[2])
                elif kind == "pin":
                    pe.wait_ge(w_in_in[2], 16)
                    mm = project(n, OFF_P, job[1], job[2])
                elif kind == "ckv":
                    mm = project(n, OFF_CKV, job[1], job[2])
                elif kind == "cq":
                    mm = project(n, OFF_CQ, job[1], job[2])
                elif kind in ("sskv", "ssq"):
                    g = job[1]
                    gn = GROUPS[g][1]
                    parts = 2 if kind == "sskv" else 3
                    base = (2 * g if kind == "sskv" else 6 + 3 * g)
                    for m in range(parts):
                        pe.wait_ge(sq_ok, base + m + 1)
                        mm = pe.matmul(o[:, 0:gn], ones, sq[:, (base + m) % 4, 0:gn],
                                       start=(m == 0), stop=(m == parts - 1))
                        if m < parts - 1:
                            mm.then_inc(raw_used, 1)
                elif kind == "kr":
                    g0, gn = GROUPS[job[1]]
                    pe.wait_ge(wrot_ok, 1)
                    for k in range(KD):
                        for q in range(4):
                            w_k = w_rot[:, k, :] if q < 2 else w_in_sb[:, k, OFF_KR:COLS]
                            mm = pe.matmul(o[32 * q:32 * q + 32, 0:gn], w_k, hT[:, k, g0:g0 + gn],
                                           start=(k == 0), stop=(k == KD - 1))
                elif kind == "gate":
                    m, g = job[1], job[2]
                    if (m, g) == (0, 0):
                        evicted(pe, NUM[("w_s",)])
                        evicted(pe, NUM[("va", NT - 1)])
                    for a, t in enumerate(GTILES[g]):
                        for j in range(2):
                            h = 2 * m + j
                            mm = pe.matmul(o[64 * j:64 * j + 64, a * P:(a + 1) * P], va[:, t, h * 64:(h + 1) * 64],
                                           wsT[:, h, :], start=True, stop=True)
                elif kind == "pool":
                    m, g = job[1], job[2]
                    pe.wait_ge(wpool_in, 16 * 4)
                    pe.wait_ge(diff_ok, 2)
                    gn, at = GROUPS[g][1], FLAT_AT[g]
                    mm = pe.matmul(o[:, 0:gn], w_pool_sb[:, m, :], win_sum[2 * m][:, at:at + gn],
                                   start=True, stop=True)
                elif kind == "cache_c":
                    pe.wait_ge(cache_in, 16 * 6)
                    for k in range(2):
                        for s in range(2):
                            mm = pe.transpose(o[:, (2 * k + s) * P:(2 * k + s + 1) * P],
                                              cache_c[:, s, k * P:(k + 1) * P], ident)
                elif kind == "cache_r":
                    for s in range(2):
                        mm = pe.transpose(o[:, s * P:(s + 1) * P], cache_r[:, s, :], ident)
                elif kind == "new":
                    evicted(pe, NUM[("sskv", 2)])
                    for k in range(2):
                        pe.transpose(o[:, k * P:(k + 1) * P], ckvT[:, k, KEYS:ALLK], ident)
                    evicted(pe, NUM[("kr", 2)])
                    mm = pe.transpose(o[:, KVL:KVL + NOPE], kT[64:128, 0, KEYS:ALLK], ident[64:128, 64:128])
                if kind != "ada":
                    mm.then_inc(job_mm, 1)

            last = len(JOBS) - 1
            for n in range(last - 7, last + 1):
                evicted(pe, n)
            def queries(i, x):
                j, g = divmod(x, 3)
                g0, gn = GROUPS[g]
                if x == 0:
                    pe.wait_ge(wq_ok, i + 1)
                if x >= 4 and not (isinstance(i, int) and i == 0):
                    pe.wait_ge(exp_ok, i * 18 - 5 + x)
                for k in range(3):
                    mm = pe.matmul(bank[Q_BANK[x]][:, 0:gn], wq[:, k, j, :], cqT[:, k, g0:g0 + gn],
                                   start=(k == 0), stop=(k == 2))
                mm.then_inc(proj_mm, 1)

            def values(i, g):
                pe.wait_ge(q_out, i * 6 + (4, 6, 6)[g])
                if g == 2:
                    pe.wait_ge(k_out, i * 3 + 3)
                for a in range(V_TILES[g]):
                    kt = 4 * g + a
                    for k in range(2):
                        mm = pe.matmul(bank[V_BANK[g]][:, a * P:(a + 1) * P], ckvT[:, k, kt * P:(kt + 1) * P],
                                       wkv[:, k, 1, :], start=(k == 0), stop=(k == 1))
                mm.then_inc(proj_mm, 1)

            def score(i, n, ch):
                t, j = divmod(n, 2)
                if n == 0:
                    pe.wait_ge(k_out, i * 3 + ch + 1)
                if n == 1 and ch < 2:
                    pe.wait_ge(v_out, i * 3 + 2 + ch)
                if n >= 2 and ch == 0:
                    pe.wait_ge(exp_ok, i * 18 + n - 1)
                if t < NT - 1:
                    k0, kn = ((0, 512), (512, 512), (1024, 256))[ch]
                else:
                    k0, kn = KEYS, NPR
                mm = pe.matmul(bank[3 * (n % 2) + ch][:, 0:kn], qT[:, j, t * P:(t + 1) * P], kT[:, j, k0:k0 + kn],
                               start=True, stop=True)
                if ch == 2 or t == NT - 1:
                    mm.then_inc(s_mm, 1)

            def keys_values(i):
                pe.wait_ge(wkv_in, i * 64 + 64)
                for g, (k0, kn) in enumerate(K_GROUPS):
                    pe.wait_ge(q_out, i * 6 + g + 1)
                    for k in range(2):
                        mm = pe.matmul(bank[Q_BANK[g]][:, 0:kn], wkv[:, k, 0, :], ckvT[:, k, k0:k0 + kn],
                                       start=(k == 0), stop=(k == 1))
                    mm.then_inc(proj_mm, 1)
                values(i, 0)
                pe.wait_ge(q_out, i * 6 + 5)
                for ch in range(3):
                    score(i, 0, ch)
                values(i, 1)
                values(i, 2)

            def attend(i, fill):
                def turn(n, ch):
                    if ch == 0:
                        pe.wait_ge(norm_ok, i * 18 + n + 1)
                    if (n, ch) != (0, 0):
                        pe.wait_ge(t_out, i * 50 + turns_before(n, ch))
                    for a in range(CHUNK_TILES[ch] if n < 16 else 1):
                        kt = 4 * ch + a
                        mm = pe.transpose(bank[6][:, a * P:(a + 1) * P], prob[n % 2][:, kt * P:(kt + 1) * P], ident)
                    mm.then_inc(t_mm, 1)

                def weigh(t, half):
                    if t < NT - 1:
                        pe.wait_ge(t_out, i * 50 + turns_before(2 * t + 1, 1 + half) + 1)
                        tiles = range(5 * half, 5 * half + 5)
                    else:
                        pe.wait_ge(t_out, i * 50 + 50)
                        tiles = range(10, 11)
                    if t > 0 and half == 0:
                        pe.wait_ge(pv_out, i * NT + t)
                    for kt in tiles:
                        for j in range(2):
                            src = kt if t < NT - 1 else 0
                            mm = pe.matmul(bank[7][64 * j:64 * j + 64, 0:P], v_sb[:, kt, 64 * j:64 * j + 64],
                                           probT[:, 2 * (t % 2) + j, src * P:(src + 1) * P],
                                           start=(kt in (0, 10)), stop=(kt in (9, 10)))
                    if kt >= 9:
                        mm.then_inc(pv_mm, 1)

                for n in range(1, 16):
                    score(i, n, 0)
                    if n >= 2:
                        turn(n - 2, 0)
                    score(i, n, 1)
                    if n >= 2:
                        turn(n - 2, 1)
                    if n >= 4:
                        weigh((n - 4) // 2, n % 2)
                    score(i, n, 2)
                    if n >= 2:
                        turn(n - 2, 2)
                for n in (16, 17):
                    score(i, n, 0)
                    turn(n - 2, 0)
                    weigh(6, n % 2)
                    turn(n - 2, 1)
                    fill(n - 16)
                    turn(n - 2, 2)
                for n in (16, 17):
                    turn(n, 0)
                    weigh(7, n % 2)
                    fill(n - 14)
                weigh(8, 0)
                fill(4)
                fill(5)

            def out_proj(x, ks=range(KD)):
                t, hf = divmod(x, 2)
                if ks[0] == 0:
                    if x == 0:
                        pe.wait_ge(w_out_in, 16)
                        evicted(pe, NUM[("pool", 1, 2)])
                    if hf == 0:
                        pe.wait_ge(pv_out, 3 * NT + t + 1)
                    if x >= 6:
                        pe.wait_ge(o_out, x - 1)
                    elif x >= 4:
                        pe.wait_ge(o_out, x - 3)
                    elif x >= 2:
                        pe.wait_ge(exp_ok, 69 + x)
                for k in ks:
                    mm = pe.matmul(bank[o_bank(x)], mixT[:, k, t * P:(t + 1) * P],
                                   w_out_sb[:, k, hf * 512:(hf + 1) * 512], start=(k == 0), stop=(k == KD - 1))
                if k == KD - 1:
                    mm.then_inc(o_mm, 1)

            for x in range(6):
                queries(0, x)
            keys_values(0)
            with pe.Fori(0, 3) as i:
                attend(i, lambda x: queries(i + 1, x))
                keys_values(i + 1)
            attend(3, lambda x: out_proj(x) if x < 4 else None)

            def h2_turn(t):
                pe.wait_ge(x2n_ok, t + 1)
                for hf in range(2):
                    if t >= 1:
                        pe.wait_ge(h2_out, 2 * t - 1 + hf)
                    for a in range(4):
                        kk = 4 * hf + a
                        mm = pe.transpose(bank[4 + hf][:, a * P:(a + 1) * P], x2n[t % 2][:, kk * P:(kk + 1) * P], ident)
                    mm.then_inc(h2_mm, 1)

            def logits(t):
                pe.wait_ge(h2_out, 2 * t + 2)
                if t == 0:
                    pe.wait_ge(w_r_in, 16)
                    pe.wait_ge(t_out, 4 * 50)
                else:
                    pe.wait_ge(lg_out, t)
                for k in range(KD):
                    mm = pe.matmul(bank[6][0:NE, 0:P], w_r[:, k, :],
                                   h2T[:, k, t * P:(t + 1) * P], start=(k == 0), stop=(k == KD - 1))
                mm.then_inc(lg_mm, 1)

            def by_token(g):
                pe.wait_ge(lg_out, R_TILES[g][-1] + 1)
                for t in R_TILES[g]:
                    mm = pe.transpose(bank[7][:, t * NE:(t + 1) * NE], aff[0:NE, t * P:(t + 1) * P], ident[0:NE, 0:NE])
                mm.then_inc(tok_mm, 1)

            def by_expert(g):
                pe.wait_ge(prob_ok, g + 1)
                if g:
                    pe.wait_ge(aff_out, 1)
                for a, t in enumerate(R_TILES[g]):
                    mm = pe.transpose(bank[(0, 0, 3)[g]][0:NE, a * P:(a + 1) * P], prob_e[:, t, :], ident)
                mm.then_inc(back_mm, 1)

            out_proj(4)
            out_proj(5)
            h2_turn(0)
            out_proj(6)
            h2_turn(1)
            logits(0)
            out_proj(7)
            h2_turn(2)
            logits(1)
            for t in range(4, 8):
                out_proj(2 * t)
                logits(t - 2)
                if t == 5:
                    out_proj(11, range(0, 1))
                    by_token(0)
                    out_proj(11, range(1, 5))
                    by_expert(0)
                    out_proj(11, range(5, KD))
                else:
                    out_proj(2 * t + 1)
                h2_turn(t - 1)
            out_proj(16)
            h2_turn(7)
            logits(6)
            out_proj(17, range(0, 2))
            logits(7)
            out_proj(17, range(2, 3))
            by_token(1)
            out_proj(17, range(3, 6))
            by_expert(1)
            out_proj(17, range(6, KD))
            h2_turn(8)
            logits(8)
            by_token(2)
            by_expert(2)

            pe.wait_ge(diag_ok, 1)
            for a, x in enumerate((diag_idx, diag_gate)):
                mm = pe.matmul(bank[5][:, a * PSLOTS:(a + 1) * PSLOTS], ones[0:NE, :], x[0:NE, :], start=True, stop=True)
            mm.then_inc(row_mm, 1)
            pe.wait_ge(onehot_ok, 1)
            pe.wait_ge(o_out, 2 * NT)
            pe.wait_ge(lg_out, NT)
            for k in range(KD):
                mm = pe.matmul(bank[XP_BANK[k // 2]][:, k % 2 * PSLOTS:(k % 2 + 1) * PSLOTS],
                               x2n[0][:, k * P:(k + 1) * P], pick_p, start=True, stop=True)
                if k % 2:
                    mm.then_inc(xp_mm, 1)
            pe.wait_ge(list_ok, 1)
            pe.wait_ge(aff_out, 3)
            for a, x in enumerate((list_val, list_idx_f)):
                mm = pe.transpose(bank[3][:, P + a * NE:P + (a + 1) * NE], x[0:NE, 0:CAPS], ident[0:NE, 0:NE])
            mm.then_inc(flip_mm, 1)
            pe.wait_ge(flip_in, 16)
            pe.wait_ge(turned_ok, 1)
            for a in range(2):
                mm = pe.matmul(bank[3][0:NE, (2 + a) * P:(3 + a) * P], list_turned[:, a * NE:(a + 1) * NE], flip_sb[:, 0:P],
                               start=True, stop=True)
            mm.then_inc(flip_mm, 1)
            pe.wait_ge(merged, 1)
            pe.transpose(bank[4][:, 0:NE], top_val[0:NE, 0:CAPS], ident[0:NE, 0:NE])
            pe.transpose(bank[4][:, NE:2 * NE], top_idx_f[0:NE, 0:CAPS], ident[0:NE, 0:NE]).then_inc(picks_mm, 1)

            def gathered(half, b, k, q, first=False):
                if k == 0:
                    pe.wait_ge(rows_in[b], half * 16 + 16)
                if not (first and k < 2):
                    pe.wait_ge(tr_out, q - 1)
                o = bank[6 + k % 2]
                pe.transpose(o[:, 0:CAPS], x_rows[b][:, k * P:(k + 1) * P], ident).then_inc(tr_mm, 1)

            def back(e, k, q):
                if k == 0:
                    pe.wait_ge(y_out, e * 8 + 8)
                pe.wait_ge(tr_out, q - 1)
                o = bank[6 + k % 2]
                pe.transpose(o[:, 0:P], yT[:, k, :], ident).then_inc(tr_mm, 1)

            def expert(half, b, first=False, final=False):
                e = half * 2 + b
                pe.wait_ge(xp_put, e + 1)
                for f in range(8):
                    s = f // 4
                    if f % 4 == 0:
                        pe.wait_ge(w1_in[s], e * 16 + 16)
                        pe.wait_ge(w3_in[s], e * 16 + 16)
                    for w, o, freed in ((w1, bank[f % 2], silu_ok), (w3, bank[2 + f % 2], hid_ok)):
                        if not (first and f < 2):
                            pe.wait_ge(freed, e * 8 + f - 1)
                        for k in range(KD):
                            if f == 0 and w is w1 and k in (0, KD - 1):
                                pe.wait_ge(tr_out, e * 16 + (8 if first else 0) - (k == 0))
                            mm = pe.matmul(o[:, 0:CAP], w[s][:, k, (f % 4) * P:(f % 4 + 1) * P], xsT[b][:, k, :],
                                           start=(k == 0), stop=(k == KD - 1))
                        mm.then_inc(h_mm, 1)
                    for k in (() if first else (2 * f, 2 * f + 1) if final and f < 4 else () if final else (f,)):
                        back(e - 1, k, e * 16 + k)
                for dm in range(8):
                    if not final:
                        gathered(half + b, 1 - b, dm, e * 16 + 8 + dm)
                    if first and dm == 1:
                        pe.wait_ge(pgt_ok, 1)
                    if not (first and dm < 2):
                        pe.wait_ge(y_out, e * 8 + dm - 1)
                    for f in range(8):
                        if dm == 0 and f % 4 == 0:
                            pe.wait_ge(w2_in[f // 4], e * 16 + 16)
                        if dm == 0 and f in (0, 7):
                            pe.wait_ge(hid_ok, e * 8 + 7 + f // 7)
                        mm = pe.matmul(bank[4 + dm % 2][:, 0:CAP], w2[f // 4][:, f % 4, dm * P:(dm + 1) * P],
                                       hidT[:, f, :], start=(f == 0), stop=(f == 7))
                    mm.then_inc(y_mm, 1)

            pe.wait_ge(xp_ok, 1)
            pe.wait_ge(picks_ok, 1)
            for k in range(KD):
                gathered(0, 0, k, k, first=True)
            pe.wait_ge(gated_ok, 1)
            for half in range(2):
                mm = pe.transpose(bank[5][:, half * P:(half + 1) * P], pick_gate[:, half * P:(half + 1) * P], ident)
            mm.then_inc(turn_mm, 1)
            expert(0, 0, first=True)
            with pe.Fori(0, NE // 2 - 1) as i2:
                expert(i2, 1)
                expert(i2 + 1, 0)
            expert(NE // 2 - 1, 1, final=True)
            for n in range(KD):
                back(NE - 1, n, NE * 16 - 8 + n)
                half = n // 4
                for k in (2 * n - 8 * half, 2 * n - 8 * half + 1):
                    mm = pe.transpose(bank[2 * half + k // 4][:, k % 4 * P:(k % 4 + 1) * P],
                                      ypT[:, k, half * P:(half + 1) * P], ident)
                if k == KD - 1:
                    mm.then_inc(yp_mm, 1)
            for half in range(2):
                pe.wait_ge(yp_out, half + 1)
                for hf in range(2):
                    mm = pe.matmul(bank[4 + hf], pick_gate_T[:, half, :], y_p[half][:, hf * 512:(hf + 1) * 512],
                                   start=(half == 0), stop=(half == 1))
            mm.then_inc(prompt_mm, 1)

        @block.scalar
        def _(act):
            act.wait_ge(cleared, 1)
            act.wait_ge(out_d, 1)
            for cnd in range(2):
                a = act.activation(cond[:, :, cnd], vT[:, V_C + 8 * cnd:V_C + 8 * cnd + 8], ACT.Silu)
            a.then_inc(cond_ok, 1)
            for t in range(NT):
                act.wait_ge(x_in[t], 16)
                a = act.activation(hreg[:, t * D:(t + 1) * D], x_sb[:, t, :], ACT.Square, accum_out=ss_x[:, t:t + 1])
                if t in (3, 7, 8):
                    a.then_inc(ssx_ok, 1)
            act.wait_ge(var_ok, 1)
            act.activation(rs_x, rs_x, ACT.Sqrt).then_inc(sqrt_ok, 1)
            squares = 0
            for n, job in enumerate(JOBS):
                kind = job[0]
                o = bank[n % 8]
                if kind in ("ckv", "cq"):
                    g0, gn = GROUPS[job[2]]
                    src = ckvT if kind == "ckv" else cqT
                    at = g0 if job[2] < 2 or kind == "cq" else KEYS
                    evicted(act, n)
                    if squares >= 4:
                        m = squares - 4
                        if m in LAST_SQ:
                            computed(act, NUM[LAST_SQ[m]])
                        else:
                            act.wait_ge(raw_used, 1 + sum(x not in LAST_SQ for x in range(m)))
                    act.activation(sq[:, squares % 4, 0:gn], src[:, job[1], at:at + gn], ACT.Square).then_inc(sq_ok, 1)
                    squares += 1
                if kind in ("sskv", "ssq"):
                    gn = GROUPS[job[1]][1]
                    m = job[1] + (3 if kind == "ssq" else 0)
                    act.wait_ge(nvar_ok, m + 1)
                    act.activation(rt[:, m % 2, 0:gn], rt[:, m % 2, 0:gn], ACT.Sqrt).then_inc(nsqrt_ok, 1)
                if job[-1] != "A":
                    continue
                if kind != "va":
                    computed(act, n)
                if kind == "h":
                    g, k = job[1], job[2]
                    g0, gn = GROUPS[g]
                    a = act.activation(hT[:, k, g0:g0 + gn], o[:, 0:gn], ACT.Copy)
                elif kind == "va":
                    if job[1] == 0:
                        act.wait_ge(gain_ok, 1)
                        evicted(act, NUM[("h", 2, KD - 1)])
                        for g, (x, w) in enumerate(GROUPS):
                            for k in range(1, KD, 2):
                                a = act.activation(hT[:, k, x:x + w], hT[:, k, x:x + w], ACT.Identity,
                                                   bias=modT[:, g // 2, k:k + 1], scale=gain1[:, g // 2, k:k + 1])
                            a.then_inc(mod_h_a, 1)
                    computed(act, n)
                    a = act.activation(va[:, job[1], :], o[:, 0:256], ACT.Gelu_apprx_tanh)
                elif kind == "u":
                    g0, gn = GROUPS[job[2]]
                    a = act.activation(mixT[:, job[1], g0:g0 + gn], o[:, 0:gn], ACT.Gelu_apprx_tanh)
                elif kind == "pool":
                    g0, gn = GROUPS[job[2]]
                    a = act.activation(mixT[:, 2 + job[1], g0:g0 + gn], o[:, 0:gn], ACT.Copy,
                                       scale=vT[:, V_PS + job[1]:V_PS + job[1] + 1])
                elif kind == "cache_c":
                    a = act.activation(ckvT[:, :, NS:KEYS], o.rearrange("p (k s) -> p k s", k=2), ACT.Copy)
                elif kind == "cache_r":
                    act.activation(kT[64:128, 0, NS:KEYS], o[64:128, 0:PAST], ACT.Copy)
                    a = act.activation(kT[64:128, 1, NS:KEYS], o[64:128, 0:PAST], ACT.Copy)
                elif kind == "new":
                    a = act.activation(new_out, o[:, 0:KVL + NOPE], ACT.Copy)
                a.then_inc(out_a, 1)

            def keys_out(i):
                for g, (k0, kn) in enumerate(K_GROUPS):
                    act.wait_ge(proj_mm, i * 12 + 7 + g)
                    o = bank[Q_BANK[g]]
                    act.activation(kT[0:64, 0, k0:k0 + kn], o[0:64, 0:kn], ACT.Copy)
                    act.activation(kT[0:64, 1, k0:k0 + kn], o[64:128, 0:kn], ACT.Copy).then_inc(k_out, 1)

            def attend(i):
                def turned(n, ch):
                    t, j = divmod(n, 2)
                    act.wait_ge(t_mm, i * 50 + turns_before(n, ch) + 1)
                    w = CHUNK_TILES[ch] * P if n < 16 else P
                    act.activation(probT[:, 2 * (t % 2) + j, ch * 512:ch * 512 + w], bank[6][:, 0:w],
                                   ACT.Copy).then_inc(t_out, 1)

                for n in range(18):
                    if n >= 2:
                        turned(n - 2, 2)
                    if 1 <= n <= 16:
                        turned(n - 1, 0)
                    act.wait_ge(neg_ok, i * 18 + n + 1)
                    if n >= 2:
                        act.wait_ge(t_mm, i * 50 + 3 * (n - 1))
                    w = KEYS if n < 16 else NPR
                    s = 3 * (n % 2)
                    src = ps[:, s:s + 3, :].rearrange("p b f -> p (b f)")[:, 0:w]
                    act.activation(prob[n % 2][:, 0:w], src, ACT.Exp, bias=a_neg[:, n % 4:n % 4 + 1], scale=SCALE,
                                   accum_out=a_sum[:, n % 4:n % 4 + 1]).then_inc(exp_ok, 1)
                    if 1 <= n <= 16:
                        turned(n - 1, 1)
                turned(16, 0)
                turned(17, 0)

            keys_out(0)
            with act.Fori(0, 3) as i:
                attend(i)
                keys_out(i + 1)
            attend(3)

            def h2_evict(t):
                cnd = t // 8
                for hf in range(2):
                    act.wait_ge(h2_mm, 2 * t + 1 + hf)
                    for a in range(4):
                        kk = 4 * hf + a
                        ins = act.activation(h2T[:, kk, t * P:(t + 1) * P], bank[4 + hf][:, a * P:(a + 1) * P],
                                             ACT.Identity, bias=modT[:, cnd, 24 + kk:25 + kk],
                                             scale=gain2[:, cnd, kk:kk + 1])
                    ins.then_inc(h2_out, 1)

            def router_exp(g):
                a, z = R_TILES[g][0], R_TILES[g][-1] + 1
                act.wait_ge(shift_ok, g + 1)
                act.activation(prob_e[:, a:z, :], logit[:, a:z, :], ACT.Exp).then_inc(r_exp, 1)

            act.wait_ge(gain_ok, 2)
            for t in range(NT):
                s = t % 2
                if t == 5:
                    router_exp(0)
                for x in range(3) if t == 3 else range(t - 1, t) if t > 3 else ():
                    h2_evict(x)
                if t == 8:
                    router_exp(1)
                act.wait_ge(x2_ok, t + 1)
                if t >= 2:
                    act.wait_ge(xn_st[s], 16 * (t // 2))
                    act.wait_ge(h2_mm, 2 * (t - 1))
                act.activation(x2n[s], x2[s], ACT.Square, accum_out=ss2[:, s:s + 1]).then_inc(ss2_ok, 1)
                act.wait_ge(var2_ok, t + 1)
                act.activation(rs2[:, s:s + 1], ss2[:, s:s + 1], ACT.Sqrt).then_inc(sqrt2_ok, 1)
                act.wait_ge(rec2_ok, t + 1)
                act.activation(x2n[s], x2[s], ACT.Copy, scale=rs2[:, s:s + 1]).then_inc(x2n_ok, 1)
            h2_evict(8)
            router_exp(2)
            for k in range(KD):
                act.wait_ge(xp_mm, k // 2 + 1)
                ins = act.activation(xpT[:, k, :], bank[XP_BANK[k // 2]][:, k % 2 * PSLOTS:(k % 2 + 1) * PSLOTS],
                                     ACT.Identity, bias=modT[:, 1, 24 + k:25 + k], scale=gain2[:, 1, k:k + 1])
            ins.then_inc(xp_ok, 1)
            act.wait_ge(turn_mm, 1)
            act.activation(pick_gate_T, bank[5][:, 0:2 * P].rearrange("p (h t) -> p h t", h=2), ACT.Copy).then_inc(pgt_ok, 1)

            def fin_square(n):
                rows, ss, _ = fin_sets[n]
                if n < LATE:
                    act.wait_ge(fin_in[n], 16)
                elif n == LATE:
                    act.wait_ge(tr_out, NE * 16)
                else:
                    act.wait_ge(prompt_ok, 1)
                if n >= 2:
                    act.wait_ge(fss_ok, n - 1)
                act.activation(fin_squares[n % 2], rows, ACT.Square, accum_out=ss).then_inc(fss_ok, 1)

            def fin_sqrt(n):
                rs = fin_sets[n][2]
                act.wait_ge(fvar_ok, n + 1)
                act.activation(rs, rs, ACT.Sqrt).then_inc(fsqrt_ok, 1)

            def expert(e, first=False, final=False):
                for f in range(8):
                    act.wait_ge(h_mm, e * 16 + 2 * f + 1)
                    if not (first and f < 2):
                        act.wait_ge(hid_ok, e * 8 + f - 1)
                    act.activation(silu_h[:, f % 2, :], bank[f % 2][:, 0:CAP], ACT.Silu).then_inc(silu_ok, 1)
                for dm in range(8):
                    act.wait_ge(y_mm, e * 8 + dm + 1)
                    act.activation(yT[:, dm, :], bank[4 + dm % 2][:, 0:CAPS], ACT.Copy,
                                   scale=modT[:, 0, 40 + dm:41 + dm])
                    act.activation(hreg[:, bass.ds(e * CAPP + YPT + dm * PSLOTS, CAPP)],
                                   bank[4 + dm % 2][:, CAPS:CAP], ACT.Copy,
                                   scale=modT[:, 1, 40 + dm:41 + dm]).then_inc(y_out, 1)
                    if final:
                        if dm > 0:
                            fin_sqrt(dm - 1)
                        fin_square(dm)

            expert(0, first=True)
            with act.Fori(1, NE - 1) as e:
                expert(e)
            expert(NE - 1, final=True)

            fin_sqrt(7)
            for half in range(2):
                act.wait_ge(yp_mm, half + 1)
                act.activation(y_p[half], ps[:, 2 * half:2 * half + 2, :].rearrange("p b f -> p (b f)"),
                               ACT.Copy).then_inc(yp_out, 1)
                if half == 0:
                    fin_square(LATE)
            fin_sqrt(LATE)
            fin_square(PROMPT)
            fin_sqrt(PROMPT)

        @block.vector
        def _(dve):
            steps = [0]

            def then(ins):
                steps[0] += 1
                ins.then_inc(dve_step, 1)
                dve.wait_ge(dve_step, steps[0])

            dve.memset(cond[:], 0.0)
            dve.memset(w_pool_sb[:], 0.0)
            dve.memset(b_rows, 0.0).then_inc(cleared, 1)

            def fold_wq(i):
                dve.wait_ge(wq_in, i * 16 + 16)
                for k in range(3):
                    g = vT[:, V_QN + k:V_QN + k + 1]
                    raw = wq_raw[:, k, :].rearrange("p (j f) -> p j f", j=2)
                    dve.tensor_scalar(wq[:, k, :, 0:QK], raw, g, None, ALU.mult)
                    src = raw[:, :, NOPE:QK].rearrange("p j (b s e) -> p j b s e", b=2, s=2)
                    dst = wq[:, k, :, QK:P].rearrange("p j (b s e) -> p j b s e", b=2, s=2)
                    for s in range(2):
                        ins = dve.tensor_scalar(dst[:, :, :, s, :], src[:, :, :, 1 - s, :], g, None, ALU.mult)
                ins.then_inc(wq_ok, 1)

            normed = 0
            for n, job in enumerate(JOBS):
                kind = job[0]
                o = bank[n % 8]
                if job[-1] != "D":
                    continue
                computed(dve, n)
                if kind == "vecs":
                    dve.tensor_copy(vT[:], o[:, 0:V_ROWS]).then_inc(out_d, 1)
                elif kind == "w_s":
                    dve.tensor_copy(wsT[:].rearrange("p h q -> p (h q)"), o).then_inc(out_d, 1)
                    dve.wait_ge(ssx_ok, 3)
                    dve.tensor_scalar(rs_x, ss_x, 1.0 / D, EPS, ALU.mult, ALU.add).then_inc(var_ok, 1)
                    dve.wait_ge(sqrt_ok, 1)
                    dve.reciprocal(rx, rs_x).then_inc(rx_ok, 1)
                    dve.wait_ge(rx_ok, 1)
                    for t in range(NT):
                        dve.tensor_scalar(x_sb[:, t, :], x_sb[:, t, :], rx[:, t:t + 1], None,
                                          ALU.mult).then_inc(xn_ok, 1)
                elif kind == "ada":
                    r = job[1]
                    if r == 0:
                        dve.wait_ge(brows_in, 16 * 4)
                    dve.tensor_tensor(mod_rows, o, b_rows[:, r, :], ALU.add).then_inc(out_d, 1)
                elif kind == "mod":
                    r = job[1]
                    v = o.rearrange("p (j g c) -> p g j c", j=4, g=4)
                    for cnd in range(2):
                        ins = dve.tensor_copy(modT[:, cnd, 16 * r:16 * r + 16].rearrange("p (g j) -> p g j", g=4),
                                              v[:, :, :, cnd])
                    ins.then_inc(out_d, 1)
                    if r in (0, 2):
                        evicted(dve, n)
                        gain, at, vn = (gain1, 8, V_N1) if r == 0 else (gain2, 32, V_N2)
                        for cnd in range(2):
                            ins = dve.scalar_tensor_tensor(out=gain[:, cnd, :], in0=modT[:, cnd, at:at + 8], scalar=1.0,
                                                           in1=vT[:, vn:vn + 8], op0=ALU.add, op1=ALU.mult)
                        ins.then_inc(gain_ok, 1)
                    if r == 0:
                        dve.wait_ge(gain_ok, 1)
                        evicted(dve, NUM[("h", 2, KD - 2)])
                        for g, (x, w) in enumerate(GROUPS):
                            for k in range(0, KD, 2):
                                ins = dve.tensor_scalar(hT[:, k, x:x + w], hT[:, k, x:x + w],
                                                        gain1[:, g // 2, k:k + 1], modT[:, g // 2, k:k + 1],
                                                        ALU.mult, ALU.add)
                            ins.then_inc(mod_h_d, 1)
                elif kind == "g1":
                    dve.tensor_copy(g1_rows[:, job[1], job[2] * 512:job[2] * 512 + 512], o).then_inc(out_d, 1)
                elif kind == "h":
                    g, k = job[1], job[2]
                    g0, gn = GROUPS[g]
                    dve.tensor_copy(hT[:, k, g0:g0 + gn], o[:, 0:gn]).then_inc(out_d, 1)
                elif kind == "pin":
                    m, g = job[1], job[2]
                    gn = GROUPS[g][1]
                    if (m, g) == (0, 0):
                        dve.wait_ge(pool_cleared, 1)
                        dve.wait_ge(w_in_in[2], 16)
                        src = w_in_sb[:, :, OFF_KR:COLS].rearrange("p k (b s e) -> p k b s e", b=2, s=2)
                        dst = w_rot[:].rearrange("p k (b s e) -> p k b s e", b=2, s=2)
                        for s in range(2):
                            ins = dve.tensor_copy(dst[:, :, :, s, :], src[:, :, :, 1 - s, :])
                        ins.then_inc(wrot_ok, 1)
                    dve.tensor_copy(pin[:, m, FLAT_AT[g]:FLAT_AT[g] + gn], o[:, 0:gn]).then_inc(out_d, 1)
                elif kind == "ckv":
                    g0, gn = GROUPS[job[2]]
                    at = g0 if job[2] < 2 else KEYS
                    dve.tensor_copy(ckvT[:, job[1], at:at + gn], o[:, 0:gn]).then_inc(out_d, 1)
                elif kind == "cq":
                    g0, gn = GROUPS[job[2]]
                    dve.tensor_copy(cqT[:, job[1], g0:g0 + gn], o[:, 0:gn]).then_inc(out_d, 1)
                elif kind in ("sskv", "ssq"):
                    g = job[1]
                    g0, gn = GROUPS[g]
                    width = KVL if kind == "sskv" else QL
                    evicted(dve, max(x for x in range(n) if JOBS[x][-1] == "D"))
                    r = rt[:, normed % 2, 0:gn]
                    dve.tensor_scalar(r, o[:, 0:gn], 1.0 / width, EPS, ALU.mult, ALU.add).then_inc(nvar_ok, 1)
                    dve.wait_ge(nvar_ok, normed + 1)
                    dve.wait_ge(nsqrt_ok, normed + 1)
                    then(dve.reciprocal(r, r))
                    normed += 1
                    if kind == "sskv":
                        at = g0 if g < 2 else KEYS
                        for m in range(2):
                            ins = dve.scalar_tensor_tensor(out=ckvT[:, m, at:at + gn], in0=ckvT[:, m, at:at + gn],
                                                           scalar=vT[:, V_KN + m:V_KN + m + 1], in1=r,
                                                           op0=ALU.mult, op1=ALU.mult)
                        ins.then_inc(out_d, 1)
                    else:
                        dve.wait_ge(rope_in, 32)
                        dve.tensor_tensor(q_mul[:, g0:g0 + gn], q_mul[:, g0:g0 + gn], r, ALU.mult).then_inc(out_d, 1)
                elif kind == "kr":
                    g0, gn = GROUPS[job[1]]
                    at = g0 if job[1] < 2 else KEYS
                    if job[1] == 0:
                        computed(dve, NUM[("kr", 2)])
                    evicted(dve, n - 1)
                    tmp = rt[64:128, 0, 0:gn]
                    main = rt[64:128, 1, 0:gn]
                    dve.tensor_tensor(tmp, o[0:64, 0:gn], kr_mul[0:64, g0:g0 + gn], ALU.mult)
                    then(dve.tensor_tensor(main, o[64:128, 0:gn], kr_mul[64:128, g0:g0 + gn], ALU.mult))
                    dve.tensor_tensor(kT[64:128, 0, at:at + gn], tmp, main, ALU.add)
                    dve.tensor_tensor(kT[64:128, 1, at:at + gn], tmp, main, ALU.add).then_inc(out_d, 1)
                elif kind == "gate":
                    m, g = job[1], job[2]
                    g0, gn = GROUPS[g]
                    if (m, g) == (0, 0):
                        dve.wait_ge(bs_in, 16 * 4)
                        evicted(dve, NUM[("u", 1, 2)])
                    evicted(dve, max(x for x in range(n) if JOBS[x][-1] == "D"))
                    a = gn // P
                    tmp = share[:, 0:gn]
                    then(dve.tensor_tensor(tmp.rearrange("p (a q) -> p a q", a=a),
                                           o[:, 0:gn].rearrange("p (a q) -> p a q", a=a),
                                           bs_sb[:, m:m + 1, :].to_broadcast([P, a, P]), ALU.add))
                    dve.tensor_tensor(mixT[:, m, g0:g0 + gn], mixT[:, m, g0:g0 + gn], tmp, ALU.mult).then_inc(out_d, 1)

            fold_wq(0)
            evicted(dve, max(n for n in range(len(JOBS)) if JOBS[n][-1] == "D"))
            def queries_out(i, x):
                j, g = divmod(x, 3)
                g0, gn = GROUPS[g]
                dve.wait_ge(proj_mm, i * 12 + x + 1)
                dve.tensor_tensor(qT[:, j, g0:g0 + gn], bank[Q_BANK[x]][:, 0:gn], q_mul[:, g0:g0 + gn],
                                  ALU.mult).then_inc(q_out, 1)

            def values_out(i, g):
                dve.wait_ge(proj_mm, i * 12 + 10 + g)
                w = V_TILES[g]
                dve.tensor_copy(v_sb[:, 4 * g:4 * g + w, :].rearrange("p a f -> p (a f)"),
                                bank[V_BANK[g]][:, 0:w * P]).then_inc(v_out, 1)

            def highest(i, n):
                w = KEYS if n < 16 else NPR
                s = 3 * (n % 2)
                r = n % 4
                src = ps[:, s:s + 3, :].rearrange("p b f -> p (b f)")[:, 0:w]
                dve.wait_ge(s_mm, i * 18 + n + 1)
                dve.tensor_reduce(a_max[:, r:r + 1], src, AX_X, ALU.max).then_inc(max_ok, 1)
                dve.wait_ge(max_ok, i * 18 + n + 1)
                dve.tensor_scalar(a_neg[:, r:r + 1], a_max[:, r:r + 1], -SCALE, None, ALU.mult).then_inc(neg_ok, 1)

            def keys_values(i):
                values_out(i, 0)
                highest(i, 0)
                values_out(i, 1)
                values_out(i, 2)

            def attend(i, more):
                def weighed(t):
                    dve.wait_ge(pv_mm, i * NT + t + 1)
                    dve.tensor_copy(mreg[:, bass.ds(i * T + 4 * T + t * P, P)], bank[7][:, 0:P]).then_inc(pv_out, 1)

                for n in range(18):
                    w = KEYS if n < 16 else NPR
                    r = n % 4
                    if n > 0:
                        highest(i, n)
                    if n % 2 and n >= 5:
                        weighed((n - 5) // 2)
                    dve.wait_ge(exp_ok, i * 18 + n + 1)
                    dve.reciprocal(a_rec[:, r:r + 1], a_sum[:, r:r + 1]).then_inc(rec_ok, 1)
                    dve.wait_ge(rec_ok, i * 18 + n + 1)
                    dve.tensor_scalar(prob[n % 2][:, 0:w], prob[n % 2][:, 0:w], a_rec[:, r:r + 1], None,
                                      ALU.mult).then_inc(norm_ok, 1)
                    if more and n == 8:
                        fold_wq(i + 1)
                for x in range(6):
                    if more:
                        queries_out(i + 1, x)
                    if x in (1, 3):
                        weighed(7 + x // 2)

            for x in range(6):
                queries_out(0, x)
            keys_values(0)
            with dve.Fori(0, 3) as i:
                attend(i, True)
                keys_values(i + 1)
            attend(3, False)

            def o_evict(x):
                t, hf = divmod(x, 2)
                s = t % 2
                if hf == 0 and t >= 2:
                    dve.wait_ge(x2_st[s], 16 * (t // 2))
                    dve.wait_ge(x2n_ok, t - 1)
                dve.wait_ge(o_mm, x + 1)
                dve.tensor_tensor(x2[s][:, hf * 512:(hf + 1) * 512], bank[o_bank(x)],
                                  g1_rows[:, t // 8, hf * 512:(hf + 1) * 512], ALU.mult).then_inc(o_out, 1)

            def mean2(t):
                s = t % 2
                dve.wait_ge(ss2_ok, t + 1)
                dve.tensor_scalar(ss2[:, s:s + 1], ss2[:, s:s + 1], 1.0 / D, EPS, ALU.mult, ALU.add).then_inc(var2_ok, 1)

            def norm2(t):
                s = t % 2
                dve.wait_ge(sqrt2_ok, t + 1)
                dve.reciprocal(rs2[:, s:s + 1], rs2[:, s:s + 1]).then_inc(rec2_ok, 1)

            def logits_out(t):
                dve.wait_ge(lg_mm, t + 1)
                dve.tensor_copy(aff[0:NE, t * P:(t + 1) * P], bank[6][0:NE, 0:P]).then_inc(lg_out, 1)

            done = [0]

            def routed(ins):
                done[0] += 1
                ins.then_inc(r_step, 1)
                dve.wait_ge(r_step, done[0])

            def shifted(g):
                a, z = R_TILES[g][0], R_TILES[g][-1] + 1
                dve.wait_ge(tok_mm, g + 1)
                routed(dve.tensor_copy(logit[:, a:z, :].rearrange("p t e -> p (t e)"), bank[7][:, a * NE:z * NE]))
                routed(dve.tensor_reduce(r_stat[:, 0, a:z], logit[:, a:z, :], AX_X, ALU.max))
                dve.tensor_tensor(logit[:, a:z, :], logit[:, a:z, :],
                                  r_stat[:, 0, a:z].unsqueeze(2).to_broadcast([P, z - a, NE]),
                                  ALU.subtract).then_inc(shift_ok, 1)

            def normalised(g):
                a, z = R_TILES[g][0], R_TILES[g][-1] + 1
                dve.wait_ge(r_exp, g + 1)
                routed(dve.tensor_reduce(r_stat[:, 1, a:z], prob_e[:, a:z, :], AX_X, ALU.add))
                routed(dve.reciprocal(r_stat[:, 2, a:z], r_stat[:, 1, a:z]))
                dve.tensor_tensor(prob_e[:, a:z, :], prob_e[:, a:z, :],
                                  r_stat[:, 2, a:z].unsqueeze(2).to_broadcast([P, z - a, NE]),
                                  ALU.mult).then_inc(prob_ok, 1)

            def probs_out(g):
                a = R_TILES[g][0] * P
                n = len(R_TILES[g]) * P
                dve.wait_ge(back_mm, g + 1)
                dve.tensor_copy(aff[0:NE, a:a + n], bank[(0, 0, 3)[g]][0:NE, 0:n]).then_inc(aff_out, 1)
                dve.wait_ge(aff_out, g + 1)

            def pick(g, rounds):
                a, z = R_TILES[g][0] * P, (R_TILES[g][-1] + 1) * P
                vals = top_val[0:NE, CAPS:CAP] if g == 2 else list_val[0:NE, g * CAPS:(g + 1) * CAPS]
                cap = CAPP if g == 2 else CAPS
                for r in rounds:
                    v = vals[:, 8 * r:8 * r + 8]
                    at = g * CAPS + 8 * r
                    routed(dve.max(v, aff[0:NE, a:z]))
                    ins = dve.max_index(list_idx[:, at:at + 8], v, aff[0:NE, a:z])
                    if r < cap // 8 - 1:
                        ins = dve.match_replace(aff[0:NE, a:z], v, aff[0:NE, a:z], -1.0)
                    routed(ins)

            def prompt_diagonals():
                routed(dve.tensor_copy(top_idx_f[0:NE, CAPS:CAP], list_idx[:, 2 * CAPS:CAPS + CAP]))
                for out, src in ((diag_idx, top_idx_f), (diag_gate, top_val)):
                    ins = dve.tensor_tensor(out[0:NE, :].rearrange("p (e s) -> p e s", e=NE),
                                            src[0:NE, CAPS:CAP].unsqueeze(1).to_broadcast([NE, NE, CAPP]),
                                            ident[0:NE, 0:NE].unsqueeze(2).to_broadcast([NE, NE, CAPP]), ALU.mult)
                ins.then_inc(diag_ok, 1)

            def prompt_picks():
                dve.wait_ge(row_mm, 1)
                dve.tensor_scalar(pick_p, bank[5][:, 0:PSLOTS], flip_sb[:, P:P + 1], None,
                                  ALU.is_equal).then_inc(onehot_ok, 1)

            dve.wait_ge(gain_ok, 2)
            dve.wait_ge(flip_in, 16)
            for t in range(5):
                o_evict(2 * t)
                if t == 3:
                    logits_out(0)
                elif t == 4:
                    logits_out(2)
                o_evict(2 * t + 1)
                if t == 3:
                    logits_out(1)
                mean2(t)
                norm2(t)
            o_evict(10)
            logits_out(3)
            shifted(0)
            normalised(0)
            probs_out(0)
            pick(0, range(0, 1))
            o_evict(11)
            pick(0, range(1, 2))
            mean2(5)
            norm2(5)
            pick(0, range(2, 4))
            o_evict(12)
            logits_out(4)
            pick(0, range(4, 6))
            o_evict(13)
            pick(0, range(6, 7))
            mean2(6)
            norm2(6)
            pick(0, range(7, 10))
            o_evict(14)
            logits_out(5)
            pick(0, range(10, 12))
            o_evict(15)
            pick(0, range(12, 13))
            mean2(7)
            norm2(7)
            pick(0, range(13, 15))
            o_evict(16)
            logits_out(6)
            pick(0, range(15, 16))
            dve.tensor_copy(list_idx_f[0:NE, 0:CAPS], list_idx[:, 0:CAPS]).then_inc(list_ok, 1)
            logits_out(7)
            shifted(1)
            normalised(1)
            probs_out(1)
            o_evict(17)
            pick(1, range(0, 1))
            mean2(8)
            pick(1, range(1, 2))
            norm2(8)
            pick(1, range(2, 6))
            logits_out(8)
            shifted(2)
            pick(1, range(6, 7))
            normalised(2)
            pick(1, range(7, 8))
            probs_out(2)
            pick(2, range(0, 2))
            prompt_diagonals()
            pick(1, range(8, 9))
            prompt_picks()
            pick(1, range(9, 13))
            dve.wait_ge(flip_mm, 1)
            dve.tensor_copy(list_turned, bank[3][:, P:P + 2 * NE]).then_inc(turned_ok, 1)
            pick(1, range(13, 16))
            last_i = list_idx_f[0:NE, CAPS:2 * CAPS]
            routed(dve.tensor_copy(last_i, list_idx[:, CAPS:2 * CAPS]))
            routed(dve.tensor_scalar(last_i, last_i, float(R_TILES[1][0] * P), None, ALU.add))
            dve.wait_ge(flip_mm, 2)
            first_v, first_i = bank[3][0:NE, 2 * P:3 * P], bank[3][0:NE, 3 * P:4 * P]
            last_v = list_val[0:NE, CAPS:2 * CAPS]
            mask, diff = merge_mask[0:NE, :], merge_diff[0:NE, :]
            dve.tensor_tensor(mask, first_v, last_v, ALU.is_ge)
            dve.tensor_tensor(top_val[0:NE, 0:CAPS], first_v, last_v, ALU.max)
            routed(dve.tensor_tensor(diff, first_i, last_i, ALU.subtract))
            routed(dve.tensor_tensor(diff, diff, mask, ALU.mult))
            dve.tensor_tensor(top_idx_f[0:NE, 0:CAPS], diff, last_i, ALU.add).then_inc(merged, 1)
            dve.wait_ge(picks_mm, 1)
            dve.tensor_copy(picked, bank[4][:, 0:NE])
            dve.tensor_copy(pick_s[:], bank[4][:, NE:2 * NE]).then_inc(picks_ok, 1)
            dve.wait_ge(onehot_ok, 1)
            dve.tensor_tensor(pick_gate, pick_p, bank[5][:, PSLOTS:2 * PSLOTS], ALU.mult).then_inc(gated_ok, 1)

            def gathered(b, k, q):
                dve.wait_ge(tr_mm, q + 1)
                dve.tensor_scalar(xsT[b][:, k, 0:CAPS], bank[6 + k % 2][:, 0:CAPS], gain2[:, 0, k:k + 1],
                                  modT[:, 0, 24 + k:25 + k], ALU.mult, ALU.add).then_inc(tr_out, 1)

            def back(e, b, k, q, first=False, last=False):
                if k == 0 and not first:
                    dve.wait_ge(added, (e - 1) * 16)
                dve.wait_ge(tr_mm, q + 1)
                o = bank[6 + k % 2]
                if last:
                    if k == 0:
                        dve.wait_ge(late_in, 16)
                    dve.scalar_tensor_tensor(out=y_rows[b][:, k * P:(k + 1) * P], in0=o[:, 0:P],
                                             scalar=picked[:, e:e + 1], in1=y_rows[1 - b][:, k * P:(k + 1) * P],
                                             op0=ALU.mult, op1=ALU.add).then_inc(tr_out, 1)
                    return
                dve.tensor_scalar(y_rows[b][:, k * P:(k + 1) * P], o[:, 0:P],
                                  creg[:, bass.ds(PICKED + e, 1)], None, ALU.mult).then_inc(tr_out, 1)

            def expert(e, b, first=False, unscattered=False, final=False):
                for f in range(8):
                    dve.wait_ge(silu_ok, e * 8 + f + 1)
                    dve.wait_ge(h_mm, e * 16 + 2 * f + 2)
                    dve.tensor_tensor(hidT[:, f, :], bank[2 + f % 2][:, 0:CAP], silu_h[:, f % 2, :],
                                      ALU.mult).then_inc(hid_ok, 1)
                    for k in (() if first else (2 * f, 2 * f + 1) if final and f < 4 else () if final else (f,)):
                        back(e - 1, 1 - b, k, e * 16 + k, first=unscattered)
                for dm in range(8):
                    if not final:
                        gathered(1 - b, dm, e * 16 + 8 + dm)

            for k in range(KD):
                gathered(0, k, k)
            expert(0, 0, first=True)
            expert(1, 1, unscattered=True)
            expert(2, 0, unscattered=True)
            with dve.Fori(1, NE // 2 - 1) as i2:
                expert(i2 * 2 + 1, 1)
                expert(i2 * 2 + 2, 0)
            expert(NE - 1, 1, final=True)

            def fin_var(n):
                _, ss, rs = fin_sets[n]
                dve.wait_ge(fss_ok, n + 1)
                dve.tensor_scalar(rs, ss, 1.0 / D, EPS, ALU.mult, ALU.add).then_inc(fvar_ok, 1)

            def fin_scale(n):
                rows, ss, rs = fin_sets[n]
                dve.wait_ge(fsqrt_ok, n + 1)
                dve.reciprocal(ss, rs).then_inc(frec_ok, 1)
                dve.wait_ge(frec_ok, n + 1)
                dve.scalar_tensor_tensor(out=rows, in0=rows, scalar=ss, in1=final_row,
                                         op0=ALU.mult, op1=ALU.mult).then_inc(fin_ok, 1)

            def fin_norm(n):
                fin_var(n)
                fin_scale(n)

            dve.wait_ge(frow_in, 16)
            for t in range(NT - 1):
                fin_var(t)
                if t > 0:
                    fin_scale(t - 1)
            for k in range(KD):
                back(NE - 1, 1, k, NE * 16 - 8 + k, last=True)
            fin_scale(7)
            fin_norm(LATE)
            dve.wait_ge(prompt_mm, 1)
            dve.wait_ge(x2p_in, 16)
            dve.tensor_tensor(p_fin, x2_p, ps[:, 4:6, :].rearrange("p b f -> p (b f)"),
                              ALU.add).then_inc(prompt_ok, 1)
            fin_norm(PROMPT)

        @block.gpsimd
        def _(pool):
            steps = [0]

            def then(ins):
                steps[0] += 1
                ins.then_inc(pool_step, 1)
                pool.wait_ge(pool_step, steps[0])

            pool.wait_ge(ada_mm, 24)
            pool.memset(pin, 0.0).then_inc(pool_cleared, 1)
            pool.wait_ge(inv_in, 16)
            for m in range(2):
                evicted(pool, NUM[("pin", m, 2)])
                p, a, b = pin[:, m, :], win_sum[2 * m], win_sum[2 * m + 1]
                then(pool.memset(b[:, 0:FLAT], 0.0))
                then(pool.memset(a[:, 0:FLAT], 0.0))
                then(pool.tensor_tensor(a[:, 1:FLAT], p[:, 1:FLAT], p[:, 0:FLAT - 1], ALU.add))
                lo = 64 if m == 0 else 0
                then(pool.tensor_tensor(b[lo:, 2:FLAT - 1], a[lo:, 1:FLAT - 2], a[lo:, 3:FLAT], ALU.add))
                if m == 1:
                    then(pool.tensor_tensor(a[:, 4:FLAT - 4], b[:, 2:FLAT - 6], b[:, 6:FLAT - 2], ALU.add))
                    then(pool.tensor_tensor(b[64:, 8:FLAT - 8], a[64:, 4:FLAT - 12], a[64:, 12:FLAT - 4], ALU.add))
                then(pool.tensor_tensor(a[0:64, :], a[0:64, :], inv_sb[0:64, m, :], ALU.mult))
                then(pool.tensor_tensor(a[64:, :], b[64:, :], inv_sb[64:, m, :], ALU.mult))
                pool.tensor_tensor(a, a, p, ALU.subtract).then_inc(diff_ok, 1)
            computed(pool, NUM[("kr", 2)])
            pool.memset(cache_r, 0.0).then_inc(crope_zero, 1)

            for t in range(NT):
                pool.wait_ge(o_out, 2 * t + 2)
                pool.wait_ge(xa_in[t % 2], 16 * (t // 2 + 1))
                pool.tensor_tensor(x2[t % 2], x2[t % 2], x_again[t % 2], ALU.add).then_inc(x2_ok, 1)

            def gather(e, b, later=True):
                if later:
                    pool.wait_ge(h_mm, (e - 2) * 16 + 1)
                pool.tensor_copy(idx_g[b][:], pick_s[:, e:e + 1]).then_inc(idx_ok, 1)
                pool.wait_ge(idx_ok, e + 1)
                pool.indirect_dma_start(out=x_rows[b], out_offset=None, in_=xn_dram,
                                        in_offset=bass.IndirectOffsetOnAxis(ap=idx_g[b][:], axis=0)
                                        ).then_inc(rows_in[b], 16)

            def put_prompt(e):
                pool.tensor_copy(xsT[e % 2][:, :, CAPS:CAP], xpT[:, :, e * CAPP:(e + 1) * CAPP]).then_inc(xp_put, 1)

            def scatter(e, b, ready):
                pool.tensor_copy(idx_s[:], pick_s[:, e:e + 1]).then_inc(sidx_ok, 1)
                pool.wait_ge(sidx_ok, e + 1)
                pool.wait_ge(tr_out, ready)
                pool.indirect_dma_start(out=x2_dram, out_offset=bass.IndirectOffsetOnAxis(ap=idx_s[:], axis=0),
                                        in_=y_rows[b], in_offset=None, compute_op=ALU.add).then_inc(added, 16)
                if e + 2 < NE:
                    put_prompt(e + 2)
                pool.wait_ge(added, (e + 1) * 16)

            pool.wait_ge(picks_ok, 1)
            for s in range(2):
                pool.wait_ge(xn_st[s], 16 * 4)
                pool.wait_ge(x2_st[s], 16 * 4)
            gather(0, 0, later=False)
            gather(1, 1, later=False)
            pool.wait_ge(xp_ok, 1)
            put_prompt(0)
            put_prompt(1)
            for e in range(NE - 1):
                if e + 2 < NE:
                    gather(e + 2, e % 2)
                scatter(e, e % 2, e * 16 + 24)
            pool.tensor_copy(idx_s[:], pick_s[:, NE - 1:NE]).then_inc(sidx_ok, 1)
            pool.wait_ge(sidx_ok, NE)
            pool.indirect_dma_start(out=y_rows[0], out_offset=None, in_=x2_dram,
                                    in_offset=bass.IndirectOffsetOnAxis(ap=idx_s[:], axis=0)).then_inc(late_in, 16)
            pool.wait_ge(fin_st, 16 * (NT - 1))
            pool.wait_ge(fin_ok, LATE + 1)
            pool.indirect_dma_start(out=y_sample[0], out_offset=bass.IndirectOffsetOnAxis(ap=idx_s[:], axis=0),
                                    in_=y_rows[1], in_offset=None).then_inc(late_st, 16)


Q_BANK = (1, 2, 4, 5, 0, 3)
K_GROUPS = ((0, 512), (512, 512), (1024, 384))
V_BANK, V_TILES = (5, 3, 4), (4, 4, 3)
CHUNK_TILES = (4, 4, 2)


def o_bank(x):
    return (1, 2, 0, 3)[x] if x < 4 else 1 + x % 2


def turns_before(n, ch):
    return 3 * n + ch if n < 16 else 32 + n


XP_BANK = (1, 2, 6, 7)
LAST_SQ = {2 * g + 1: ("sskv", g) for g in range(3)} | {6 + 3 * g + 2: ("ssq", g) for g in range(3)}


_INS = ['x_prompt', 'x_sample', 'cache_ckv', 'cache_krope', 'c', 'c_ctx', 'w_ada', 'b_ada', 'norm1_g', 'norm2_g',
        'w_in', 'w_s', 'b_s', 'w_pool', 'pool_scale', 'q_norm_g', 'w_qb', 'kv_norm_g', 'w_kvb', 'w_out', 'w_router',
        'w_e1', 'w_e3', 'w_e2', 'final_norm_g']
_OUTS = [(1, NPR, D), (1, NS, D), (1, 1, NPR, KVL), (1, 1, NPR, ROPE)]


def kernel(**inputs):
    import concourse.bacc as _bacc
    from concourse.bass_utils import run_bass_kernel_spmd as _run

    nc = _bacc.Bacc("TRN2", target_bir_lowering=False, num_devices=1)
    arrays, args = {}, []
    for name, a in [(n, inputs[n]) for n in _INS] + list(tables().items()):
        a = np.ascontiguousarray(a)
        arrays[f"in_{name}_dram"] = a
        args.append(nc.dram_tensor(f"in_{name}_dram", a.shape, mybir.dt.from_np(a.dtype), kind="ExternalInput").ap())
    for i, shape in enumerate(_OUTS):
        args.append(nc.dram_tensor(f"out_{i}_dram", shape, F32, kind="ExternalOutput").ap())
    build(nc, *args)
    r = _run(nc, [arrays], core_ids=[0])
    return tuple(r.results[0][f"out_{i}_dram"] for i in range(len(_OUTS)))
```
